# Optimizing a Trainium2 kernel written in Bass

```python
import math
import jax, jax.numpy as jnp
from jax import lax
import numpy as np

D_MODEL = 1024
BATCH = 1
SEQ = 256
DEPTH = 2

N_MIXERS = 2
RET_QK_DIM = 256
RET_HEADS = D_MODEL // RET_QK_DIM
RET_V_DIM = 2 * RET_QK_DIM
RET_QK = RET_HEADS * RET_QK_DIM
RET_V = RET_HEADS * RET_V_DIM
RET_CHUNK = 128
ROPE_BASE = 10000.0
DILATED_PAIRS = ((128, 1), (512, 4), (2048, 16))
ATT_GROUPS = 3
ATT_HEAD_DIM = 64
ATT_HEADS = D_MODEL // ATT_HEAD_DIM
ATT_GROUP_W = ATT_HEADS * ATT_HEAD_DIM
BAND_BLOCK = 128
NUM_BUCKETS = 32
MAX_DISTANCE = 2048
D_FF = ((8 * D_MODEL + 3 * 256 - 1) // (3 * 256)) * 256
DEEPNORM_ALPHA = (2 * DEPTH) ** 0.25
DEEPNORM_BETA = (8 * DEPTH) ** -0.25
LN_EPS = 1e-5
GN_EPS = 1e-5


def _layer_norm(x, g, b):
    xf = x.astype(jnp.float32)
    mu = jnp.mean(xf, axis=-1, keepdims=True)
    var = jnp.mean(jnp.square(xf - mu), axis=-1, keepdims=True)
    y = (xf - mu) * lax.rsqrt(var + LN_EPS) * g.astype(jnp.float32) + b.astype(jnp.float32)
    return y.astype(x.dtype)

def _rope(x):
    B, T, H, d = x.shape
    inv = 1.0 / (ROPE_BASE ** jnp.linspace(0.0, 1.0, d // 2, dtype=jnp.float32))
    ang = jnp.arange(T, dtype=jnp.float32)[:, None] * inv[None, :]
    c = jnp.cos(ang)[None, :, None, :]
    s = jnp.sin(ang)[None, :, None, :]
    xp = x.reshape(B, T, H, d // 2, 2)
    a, b = xp[..., 0], xp[..., 1]
    return jnp.stack([a * c - b * s, a * s + b * c], axis=-1).reshape(B, T, H, d)

def retention(x, w_in, w_out):
    B, T, _ = x.shape
    H, dk, dv, C = RET_HEADS, RET_QK_DIM, RET_V_DIM, RET_CHUNK
    N = T // C
    proj = x @ w_in
    q, k, v, gate = jnp.split(proj, [RET_QK, 2 * RET_QK, 2 * RET_QK + RET_V], axis=-1)
    q = _rope(q.reshape(B, T, H, dk).astype(jnp.float32))
    k = _rope(k.reshape(B, T, H, dk).astype(jnp.float32)) * (dk ** -0.5)
    v = v.reshape(B, T, H, dv).astype(jnp.float32)

    def to_chunks(t):
        return t.reshape(B, N, C, H, t.shape[-1]).transpose(1, 0, 3, 2, 4)

    qc, kc, vc = to_chunks(q), to_chunks(k), to_chunks(v)
    log_gamma = jnp.log(1.0 - 2.0 ** (-5.0 - jnp.arange(H, dtype=jnp.float32)))
    idx = jnp.arange(C, dtype=jnp.float32)
    diff = idx[:, None] - idx[None, :]
    intra = jnp.where(diff[None] >= 0,
                      jnp.exp(jnp.maximum(diff, 0.0)[None] * log_gamma[:, None, None]), 0.0)
    xi = jnp.exp((idx[None, :] + 1.0) * log_gamma[:, None])[..., None]
    zeta = jnp.exp((C - 1.0 - idx[None, :]) * log_gamma[:, None])[..., None]
    gamma_c = jnp.exp(C * log_gamma)[:, None, None]

    def body(state, inp):
        qi, ki, vi = inp
        s = jnp.einsum('bhid,bhjd->bhij', qi, ki) * intra
        inner = jnp.einsum('bhij,bhje->bhie', s, vi)
        cross = jnp.einsum('bhid,bhde->bhie', qi * xi, state)
        state = gamma_c * state + jnp.einsum('bhjd,bhje->bhde', ki * zeta, vi)
        return state, inner + cross

    state0 = jnp.zeros((B, H, dk, dv), jnp.float32)
    _, y = lax.scan(body, state0, (qc, kc, vc))
    y = y.transpose(1, 0, 3, 2, 4).reshape(B, T, H, dv)
    mu = jnp.mean(y, axis=-1, keepdims=True)
    var = jnp.mean(jnp.square(y - mu), axis=-1, keepdims=True)
    y = ((y - mu) * lax.rsqrt(var + GN_EPS)).reshape(B, T, RET_V).astype(x.dtype)
    return (jax.nn.silu(gate) * y) @ w_out

def _t5_bucket(dist):
    max_exact = NUM_BUCKETS // 2
    d_f = jnp.maximum(dist, 1).astype(jnp.float32)
    large = max_exact + (jnp.log(d_f / max_exact) / math.log(MAX_DISTANCE / max_exact)
                         * (NUM_BUCKETS - max_exact)).astype(jnp.int32)
    large = jnp.minimum(large, NUM_BUCKETS - 1)
    return jnp.where(dist < max_exact, dist, large)

def _dilated_group(q, k, v, bias_table, window, dil):
    B, H, T, hd = q.shape
    blk = BAND_BLOCK
    steps = window // dil
    L = T // dil
    nb = -(-L // blk)
    Lp = nb * blk

    def to_blocks(t):
        t = t.reshape(B, H, L, dil, hd).transpose(0, 1, 3, 2, 4)
        t = jnp.pad(t, ((0, 0), (0, 0), (0, 0), (0, Lp - L), (0, 0)))
        return t.reshape(B, H, dil, nb, blk, hd)

    def band(t):
        prev = jnp.pad(t, ((0, 0), (0, 0), (0, 0), (1, 0), (0, 0), (0, 0)))[:, :, :, :-1]
        return jnp.concatenate([prev, t], axis=4)

    qb = to_blocks(q)
    kw = band(to_blocks(k))
    vw = band(to_blocks(v))
    qi = jnp.arange(blk)[:, None]
    kj = jnp.arange(2 * blk)[None, :]
    delta = qi + blk - kj
    band_ok = (delta >= 0) & (delta <= steps)
    key_ok = (jnp.arange(nb)[:, None, None] * blk - blk + kj[None]) >= 0
    mask = band_ok[None] & key_ok
    bucket = _t5_bucket(jnp.maximum(delta, 0) * dil)
    bias = bias_table[:, bucket].astype(jnp.float32)

    s = jnp.einsum('bhrnqd,bhrnkd->bhrnqk', qb, kw).astype(jnp.float32) * (hd ** -0.5)
    s = s + bias[None, :, None, None]
    s = jnp.where(mask[None, None, None], s, -jnp.inf)
    m = jnp.max(s, axis=-1, keepdims=True)
    e = jnp.exp(s - m)
    den = jnp.sum(e, axis=-1, keepdims=True)
    p = e / den
    lse = (m + jnp.log(den))[..., 0]
    o = jnp.einsum('bhrnqk,bhrnkd->bhrnqd', p.astype(v.dtype), vw)
    o = o.reshape(B, H, dil, Lp, hd)[:, :, :, :L].transpose(0, 1, 3, 2, 4).reshape(B, H, T, hd)
    lse = lse.reshape(B, H, dil, Lp)[..., :L].transpose(0, 1, 3, 2).reshape(B, H, T)
    return o, lse

def dilated_attention(x, w_in, w_out, rel_bias):
    B, T, _ = x.shape
    proj = (x @ w_in).reshape(B, T, 3, ATT_GROUPS, ATT_HEADS, ATT_HEAD_DIM)
    proj = proj.transpose(2, 3, 0, 4, 1, 5)
    outs, lses = [], []
    for g, (window, dil) in enumerate(DILATED_PAIRS):
        o, lse = _dilated_group(proj[0, g], proj[1, g], proj[2, g],
                                rel_bias[g * ATT_HEADS:(g + 1) * ATT_HEADS], window, dil)
        outs.append(o)
        lses.append(lse)
    w = jax.nn.softmax(jnp.stack(lses, axis=0), axis=0)
    o = jnp.sum(w[..., None] * jnp.stack(outs, axis=0).astype(jnp.float32), axis=0)
    o = o.transpose(0, 2, 1, 3).reshape(B, T, ATT_GROUP_W).astype(x.dtype)
    return o @ w_out

def swiglu_ffn(x, w_up, w_down):
    gate, up = jnp.split(x @ w_up, 2, axis=-1)
    return (jax.nn.silu(gate) * up) @ w_down

def first_inputs(seed: int = 0) -> dict:
    key = jax.random.key(seed)
    ks = jax.random.split(key, 10)
    n_ret = (DEPTH + 1) // 2
    n_att = DEPTH // 2
    f32 = jnp.float32
    x = jax.random.normal(ks[0], (BATCH, SEQ, D_MODEL), f32)
    ret_w_in = jax.random.normal(ks[1], (n_ret, D_MODEL, 2 * RET_QK + 2 * RET_V), f32) * D_MODEL ** -0.5
    ret_w_out = jax.random.normal(ks[2], (n_ret, RET_V, D_MODEL), f32) * (RET_V ** -0.5 * DEEPNORM_BETA)
    attn_w_in = jax.random.normal(ks[3], (n_att, D_MODEL, 3 * ATT_GROUPS * ATT_GROUP_W), f32) * D_MODEL ** -0.5
    attn_w_out = jax.random.normal(ks[4], (n_att, ATT_GROUP_W, D_MODEL), f32) * (ATT_GROUP_W ** -0.5 * DEEPNORM_BETA)
    rel_bias = jax.random.normal(ks[5], (ATT_GROUPS * ATT_HEADS, NUM_BUCKETS), f32) * 0.2
    ffn_w_up = jax.random.normal(ks[6], (DEPTH, D_MODEL, 2 * D_FF), f32) * D_MODEL ** -0.5
    ffn_w_down = jax.random.normal(ks[7], (DEPTH, D_FF, D_MODEL), f32) * (D_FF ** -0.5 * DEEPNORM_BETA)
    ln_gain = 1.0 + 0.02 * jax.random.normal(ks[8], (DEPTH, 2, D_MODEL), f32)
    ln_bias = 0.02 * jax.random.normal(ks[9], (DEPTH, 2, D_MODEL), f32)
    return {"x": x, "ret_w_in": ret_w_in, "ret_w_out": ret_w_out,
            "attn_w_in": attn_w_in, "attn_w_out": attn_w_out, "rel_bias": rel_bias,
            "ffn_w_up": ffn_w_up, "ffn_w_down": ffn_w_down,
            "ln_gain": ln_gain, "ln_bias": ln_bias}

def first_block(x, ret_w_in, ret_w_out, attn_w_in, attn_w_out, rel_bias,
              ffn_w_up, ffn_w_down, ln_gain, ln_bias):
    for i in range(DEPTH):
        j = i // N_MIXERS
        if i % N_MIXERS == 0:
            mix = retention(x, ret_w_in[j], ret_w_out[j])
        else:
            mix = dilated_attention(x, attn_w_in[j], attn_w_out[j], rel_bias)
        x = _layer_norm(DEEPNORM_ALPHA * x + mix, ln_gain[i, 0], ln_bias[i, 0])
        x = _layer_norm(DEEPNORM_ALPHA * x + swiglu_ffn(x, ffn_w_up[i], ffn_w_down[i]),
                        ln_gain[i, 1], ln_bias[i, 1])
    return x


GRID_W = 64
CTX_LEN = 256
N_EVEN = (DEPTH + 1) // 2
N_ODD = DEPTH // 2

C_HYENA = D_MODEL // 2
C_NA = D_MODEL - C_HYENA
NA_HEAD_DIM = 32
NA_HEADS = C_NA // NA_HEAD_DIM
NA_WIN_R = 8
NA_WIN_C = 16
NA_QB = 16
NA_BAND = NA_QB + NA_WIN_C
HYENA_ORDER = 2
HYENA_SHORT = 3
HYENA_EMB = 33
HYENA_BANDS = (HYENA_EMB - 1) // 2
HYENA_FILTER_HID = 64
HYENA_FAST_DECAY = 0.3
HYENA_SLOW_DECAY = 1.5
HYENA_TARGET = 1e-2
F_GROUPS = 4
D_FF_2 = 2816
N_EXPERTS = 8
TOP_K = 2
D_FF_EXPERT = 3584
N_MOD = 6
EPS = 1e-6
NEG_INF = -1e30


def rmsnorm(x, g):
    x32 = x.astype(jnp.float32)
    y = x32 * lax.rsqrt(jnp.mean(x32 * x32, axis=-1, keepdims=True) + EPS)
    return (y * g.astype(jnp.float32)).astype(x.dtype)

def modulate(h, shift, scale):
    return h * (1 + scale) + shift

def ada_params(cvec, w, b):
    return jnp.split(jax.nn.silu(cvec) @ w + b, N_MOD, axis=-1)

def swiglu(h, w1, w3, w2):
    return (jax.nn.silu(h @ w1) * (h @ w3)) @ w2

def moe_swiglu(h, w_router, b_router, w1, w3, w2):
    logits = (h @ w_router).astype(jnp.float32) + b_router.astype(jnp.float32)
    top_val, top_idx = lax.top_k(logits, TOP_K)
    top_w = jax.nn.softmax(top_val, axis=-1)
    gate = jnp.einsum('blk,blke->ble', top_w,
                      jax.nn.one_hot(top_idx, N_EXPERTS, dtype=jnp.float32)).astype(h.dtype)
    out = jnp.zeros_like(h)
    for e in range(N_EXPERTS):
        out = out + gate[..., e:e + 1] * swiglu(h, w1[e], w3[e], w2[e])
    return out

def hyena_filters(L, w1, b1, w2, b2, w3, freq):
    f32 = jnp.float32
    w1, b1, w2, b2, w3, freq = (a.astype(f32) for a in (w1, b1, w2, b2, w3, freq))
    t = jnp.linspace(0.0, 1.0, L, dtype=f32)[:, None]
    bands = jnp.linspace(1e-4, HYENA_BANDS - 1, HYENA_BANDS, dtype=f32)
    ang = (2.0 * math.pi / L) * jnp.arange(L, dtype=f32)[:, None] * bands[None, :]
    feats = jnp.concatenate([t, jnp.cos(ang), -jnp.sin(ang)], axis=-1)
    h = jnp.sin(freq[0] * (feats @ w1 + b1))
    h = jnp.sin(freq[1] * (h @ w2 + b2))
    h = (h @ w3).reshape(L, HYENA_ORDER, 2, C_HYENA)
    deltas = jnp.abs(jnp.linspace(math.log(HYENA_TARGET) / HYENA_SLOW_DECAY,
                                  math.log(HYENA_TARGET) / HYENA_FAST_DECAY, C_HYENA, dtype=f32))
    h = h * jnp.exp(-t * deltas[None, :])[:, None, None, :]
    k = jnp.concatenate([h[:, :, 0], jnp.zeros((1, HYENA_ORDER, C_HYENA), f32), h[:0:-1, :, 1]], axis=0)
    return k / (jnp.sum(jnp.abs(k), axis=0, keepdims=True) + EPS)

def long_conv(u, k, skip):
    L = u.shape[1]
    u32 = u.astype(jnp.float32)
    U = jnp.fft.rfft(u32, n=2 * L, axis=1)
    K = jnp.fft.rfft(k, axis=0)
    y = jnp.fft.irfft(U * K[None], n=2 * L, axis=1)[:, :L]
    return (y + u32 * skip.astype(jnp.float32)).astype(u.dtype)

def hyena_mixer(z, short_w, short_b, f_w1, f_b1, f_w2, f_b2, f_w3, f_freq, skip):
    L = z.shape[1]
    zp = jnp.pad(z, ((0, 0), (1, 1), (0, 0)))
    z = zp[:, :-2] * short_w[0] + zp[:, 1:-1] * short_w[1] + zp[:, 2:] * short_w[2] + short_b
    v, x1, x2 = jnp.split(z, 3, axis=-1)
    filt = hyena_filters(L, f_w1, f_b1, f_w2, f_b2, f_w3, f_freq)
    y = x1 * long_conv(v, filt[:, 0], skip[0])
    y = x2 * long_conv(y, filt[:, 1], skip[1])
    return y

def to_heads(t):
    B, L, _ = t.shape
    return t.reshape(B, L, NA_HEADS, NA_HEAD_DIM).transpose(0, 2, 1, 3)

def to_grid(t, rows):
    B = t.shape[0]
    return t.reshape(B, rows, GRID_W, NA_HEADS, NA_HEAD_DIM).transpose(0, 3, 1, 2, 4)

def context_attention(q, k, v):
    s = jnp.einsum('bhqd,bhkd->bhqk', q, k).astype(jnp.float32) * (NA_HEAD_DIM ** -0.5)
    p = jax.nn.softmax(s, axis=-1).astype(v.dtype)
    o = jnp.einsum('bhqk,bhkd->bhqd', p, v)
    B, H, L, dh = o.shape
    return o.transpose(0, 2, 1, 3).reshape(B, L, H * dh)

def neighborhood_attention(q, k, v, k_ctx, v_ctx, rpb):
    B, H, rows, W, dh = q.shape
    win_r = min(NA_WIN_R, rows)
    ncb = W // NA_QB
    scale = dh ** -0.5
    qcol = jnp.arange(W).reshape(ncb, NA_QB)
    c_start = jnp.clip(qcol - NA_WIN_C // 2, 0, W - NA_WIN_C)
    band_start = jnp.clip(jnp.arange(ncb) * NA_QB - NA_WIN_C // 2, 0, W - NA_BAND)
    band_cols = band_start[:, None] + jnp.arange(NA_BAND)
    kcol = band_cols[:, None, :]
    col_ok = (kcol >= c_start[..., None]) & (kcol < c_start[..., None] + NA_WIN_C)
    col_idx = jnp.clip(kcol - qcol[..., None] + NA_WIN_C - 1, 0, 2 * NA_WIN_C - 2)
    rpb32 = rpb.astype(jnp.float32)
    n_loc = win_r * NA_BAND

    def one_row(r):
        r0 = jnp.clip(r - win_r // 2, 0, rows - win_r)
        q_r = lax.dynamic_index_in_dim(q, r, axis=2, keepdims=False).reshape(B, H, ncb, NA_QB, dh)
        k_r = jnp.take(lax.dynamic_slice_in_dim(k, r0, win_r, axis=2), band_cols, axis=3)
        v_r = jnp.take(lax.dynamic_slice_in_dim(v, r0, win_r, axis=2), band_cols, axis=3)
        row_idx = r0 + jnp.arange(win_r) - r + NA_WIN_R - 1
        bias = rpb32[:, row_idx[None, None, :, None], col_idx[:, :, None, :]]
        s_loc = jnp.einsum('bhjqd,bhrjkd->bhjqrk', q_r, k_r).astype(jnp.float32) * scale + bias
        s_loc = jnp.where(col_ok[:, :, None, :], s_loc, NEG_INF)
        s_ctx = jnp.einsum('bhjqd,bhcd->bhjqc', q_r, k_ctx).astype(jnp.float32) * scale
        logits = jnp.concatenate([s_loc.reshape(B, H, ncb, NA_QB, n_loc), s_ctx], axis=-1)
        p = jax.nn.softmax(logits, axis=-1).astype(v.dtype)
        p_loc = p[..., :n_loc].reshape(B, H, ncb, NA_QB, win_r, NA_BAND)
        o = (jnp.einsum('bhjqrk,bhrjkd->bhjqd', p_loc, v_r)
             + jnp.einsum('bhjqc,bhcd->bhjqd', p[..., n_loc:], v_ctx))
        return o.reshape(B, H, W, dh)

    out = lax.map(one_row, jnp.arange(rows))
    return out.transpose(1, 0, 3, 2, 4).reshape(B, rows * W, H * dh)

def fourier_mix(h):
    B, L, D = h.shape
    hg = h.astype(jnp.float32).reshape(B, L, F_GROUPS, D // F_GROUPS)
    y = jnp.fft.fftn(hg, axes=(1, 3), norm='ortho').real
    return y.reshape(B, L, D).astype(h.dtype)

def second_inputs(seed: int = 0) -> dict:
    key = jax.random.key(seed)
    ks = iter(jax.random.split(key, 32))
    f32 = jnp.float32
    D = D_MODEL

    def dense(shape, fan_in):
        return jax.random.normal(next(ks), shape, f32) * (fan_in ** -0.5)

    def small(shape, s):
        return jax.random.normal(next(ks), shape, f32) * s

    return {
        'x': small((BATCH, SEQ, D), 1.0),
        'c': small((BATCH, D), 1.0),
        'ctx': small((BATCH, CTX_LEN, D), 1.0),
        'c_ctx': small((D,), 1.0),
        'w_ada': dense((DEPTH, D, N_MOD * D), D),
        'b_ada': small((DEPTH, N_MOD * D), 0.02),
        'norm_g': 1.0 + small((DEPTH, 2, D), 0.02),
        'w_in': dense((N_EVEN, D, 3 * C_HYENA + 3 * C_NA), D),
        'hy_short_w': dense((N_EVEN, HYENA_SHORT, 3 * C_HYENA), HYENA_SHORT),
        'hy_short_b': small((N_EVEN, 3 * C_HYENA), 0.02),
        'hy_f_w1': dense((N_EVEN, HYENA_EMB, HYENA_FILTER_HID), HYENA_EMB),
        'hy_f_b1': small((N_EVEN, HYENA_FILTER_HID), 0.02),
        'hy_f_w2': dense((N_EVEN, HYENA_FILTER_HID, HYENA_FILTER_HID), HYENA_FILTER_HID),
        'hy_f_b2': small((N_EVEN, HYENA_FILTER_HID), 0.02),
        'hy_f_w3': dense((N_EVEN, HYENA_FILTER_HID, HYENA_ORDER * 2 * C_HYENA), HYENA_FILTER_HID),
        'hy_f_freq': 1.0 + small((N_EVEN, 2, HYENA_FILTER_HID), 0.02),
        'hy_skip': small((N_EVEN, HYENA_ORDER, C_HYENA), 0.5),
        'na_rpb': small((N_EVEN, NA_HEADS, 2 * NA_WIN_R - 1, 2 * NA_WIN_C - 1), 0.1),
        'w_mix_out': dense((N_EVEN, D, D), D),
        'ffn_w1': dense((N_EVEN, D, D_FF_2), D),
        'ffn_w3': dense((N_EVEN, D, D_FF_2), D),
        'ffn_w2': dense((N_EVEN, D_FF_2, D), D_FF_2),
        'w_fourier': dense((N_ODD, D, D), D),
        'w_router': dense((N_ODD, D, N_EXPERTS), D),
        'b_router': small((N_ODD, N_EXPERTS), 0.01),
        'moe_w1': dense((N_ODD, N_EXPERTS, D, D_FF_EXPERT), D),
        'moe_w3': dense((N_ODD, N_EXPERTS, D, D_FF_EXPERT), D),
        'moe_w2': dense((N_ODD, N_EXPERTS, D_FF_EXPERT, D), D_FF_EXPERT),
        'final_g': 1.0 + small((D,), 0.02),
    }

def second_block(x, c, ctx, c_ctx, w_ada, b_ada, norm_g, w_in, hy_short_w, hy_short_b,
              hy_f_w1, hy_f_b1, hy_f_w2, hy_f_b2, hy_f_w3, hy_f_freq, hy_skip, na_rpb,
              w_mix_out, ffn_w1, ffn_w3, ffn_w2, w_fourier, w_router, b_router,
              moe_w1, moe_w3, moe_w2, final_g):
    rows = x.shape[1] // GRID_W
    kv_off = 3 * C_HYENA + C_NA
    xc = ctx
    for layer in range(DEPTH):
        even = layer % 2 == 0
        update_ctx = any(l % 2 == 0 for l in range(layer + 1, DEPTH))
        g_mix, g_ffn = norm_g[layer, 0], norm_g[layer, 1]
        sh1, sc1, gt1, sh2, sc2, gt2 = ada_params(c[:, None, :], w_ada[layer], b_ada[layer])
        if even or update_ctx:
            csh1, csc1, cgt1, csh2, csc2, cgt2 = ada_params(c_ctx[None, None, :], w_ada[layer], b_ada[layer])
        if even:
            i = layer // 2
            hy = (hy_short_w[i], hy_short_b[i], hy_f_w1[i], hy_f_b1[i], hy_f_w2[i], hy_f_b2[i],
                  hy_f_w3[i], hy_f_freq[i], hy_skip[i])
            h = modulate(rmsnorm(x, g_mix), sh1, sc1)
            z = h @ w_in[i]
            q, k, v = jnp.split(z[..., 3 * C_HYENA:], 3, axis=-1)
            hc = modulate(rmsnorm(xc, g_mix), csh1, csc1)
            if update_ctx:
                zc = hc @ w_in[i]
                kvc = zc[..., kv_off:]
            else:
                kvc = hc @ w_in[i][:, kv_off:]
            kc, vc = jnp.split(kvc, 2, axis=-1)
            kc, vc = to_heads(kc), to_heads(vc)
            y_na = neighborhood_attention(to_grid(q, rows), to_grid(k, rows), to_grid(v, rows), kc, vc, na_rpb[i])
            y_hy = hyena_mixer(z[..., :3 * C_HYENA], *hy)
            x = x + gt1 * (jnp.concatenate([y_hy, y_na], axis=-1) @ w_mix_out[i])
            if update_ctx:
                yc_na = context_attention(to_heads(zc[..., 3 * C_HYENA:kv_off]), kc, vc)
                yc_hy = hyena_mixer(zc[..., :3 * C_HYENA], *hy)
                xc = xc + cgt1 * (jnp.concatenate([yc_hy, yc_na], axis=-1) @ w_mix_out[i])
            x = x + gt2 * swiglu(modulate(rmsnorm(x, g_ffn), sh2, sc2), ffn_w1[i], ffn_w3[i], ffn_w2[i])
            if update_ctx:
                xc = xc + cgt2 * swiglu(modulate(rmsnorm(xc, g_ffn), csh2, csc2), ffn_w1[i], ffn_w3[i], ffn_w2[i])
        else:
            j = layer // 2
            x = x + gt1 * (fourier_mix(modulate(rmsnorm(x, g_mix), sh1, sc1)) @ w_fourier[j])
            x = x + gt2 * moe_swiglu(modulate(rmsnorm(x, g_ffn), sh2, sc2), w_router[j], b_router[j],
                                     moe_w1[j], moe_w3[j], moe_w2[j])
            if update_ctx:
                xc = xc + cgt1 * (fourier_mix(modulate(rmsnorm(xc, g_mix), csh1, csc1)) @ w_fourier[j])
                xc = xc + cgt2 * moe_swiglu(modulate(rmsnorm(xc, g_ffn), csh2, csc2), w_router[j], b_router[j],
                                            moe_w1[j], moe_w3[j], moe_w2[j])
    return rmsnorm(x, final_g)


def setup_inputs(seed=0):
    out = dict(first_inputs(seed))
    for name, value in second_inputs(seed + 1).items():
        if name != "x":
            out[name + "_2"] = value
    return out


def reference(
    x, ret_w_in, ret_w_out, attn_w_in, attn_w_out, rel_bias, ffn_w_up, ffn_w_down, ln_gain,
    ln_bias, c_2, ctx_2, c_ctx_2, w_ada_2, b_ada_2, norm_g_2, w_in_2, hy_short_w_2,
    hy_short_b_2, hy_f_w1_2, hy_f_b1_2, hy_f_w2_2, hy_f_b2_2, hy_f_w3_2, hy_f_freq_2, hy_skip_2,
    na_rpb_2, w_mix_out_2, ffn_w1_2, ffn_w3_2, ffn_w2_2, w_fourier_2, w_router_2, b_router_2,
    moe_w1_2, moe_w3_2, moe_w2_2, final_g_2,
):
    x = first_block(
        x, ret_w_in, ret_w_out, attn_w_in, attn_w_out, rel_bias, ffn_w_up, ffn_w_down, ln_gain,
        ln_bias,
    )
    return second_block(
        x, c_2, ctx_2, c_ctx_2, w_ada_2, b_ada_2, norm_g_2, w_in_2, hy_short_w_2, hy_short_b_2,
        hy_f_w1_2, hy_f_b1_2, hy_f_w2_2, hy_f_b2_2, hy_f_w3_2, hy_f_freq_2, hy_skip_2, na_rpb_2,
        w_mix_out_2, ffn_w1_2, ffn_w3_2, ffn_w2_2, w_fourier_2, w_router_2, b_router_2,
        moe_w1_2, moe_w3_2, moe_w2_2, final_g_2,
    )


_drawn_inputs = setup_inputs


def setup_inputs(seed=0):
    import zlib

    import numpy as np

    out = dict(_drawn_inputs(seed))
    spreads = {}
    factors = {'rel_bias': 2.976,
     'hy_f_b1_2': 2.698,
     'hy_f_b2_2': 2.713,
     'hy_f_freq_2': 8.0,
     'na_rpb_2': 2.863,
     'b_router_2': 2.837,
     'final_g_2': 8.535,
     'hy_short_b_2': 2.808}
    for name, (base, spread) in spreads.items():
        noise = np.random.default_rng([zlib.crc32(name.encode()), seed]).standard_normal(out[name].shape)
        drawn = base * np.exp(spread * noise) if base else spread * noise
        out[name] = __import__('jax').numpy.asarray(drawn.astype(out[name].dtype))
    for name, factor in factors.items():
        out[name] = (out[name] * factor).astype(out[name].dtype)
    return out
```

```python
from contextlib import ExitStack

import numpy as np

import concourse.bass as bass
from concourse import mybir

F32 = mybir.dt.float32
ALU = mybir.AluOpType
ACT = mybir.ActivationFunctionType
AX_X = mybir.AxisListType.X

P = 128
T = 256
TT = T // P
D = 1024
KD = D // P
RING = 6
SLOT = 2048
BANK = 512
NEG = -1.0e30

RH, RDK, RDV = 4, 256, 512
AG, AH, AHD = 3, 16, 64
BUCKETS, MAX_DIST = 32, 2048
ROWS_W = 384
DILATIONS = ((128, 1), (512, 4), (2048, 16))
HC = 512
NH, NHD = 16, 32
WIN_R, WIN_C, GRID_W = 8, 16, 64
HID, EMB = 64, 33
FFN = 2816
EXPERTS, FEXP = 8, 3584
ALPHA = 4.0 ** 0.25
LN_EPS = 1e-5
RMS_EPS = 1e-6
ROUND = 1.5 * 2.0 ** 23
TWO_PI_HI = 6.28125
TWO_PI_MID = 0.0019350051879882812
TWO_PI_LO = 2.0 * np.pi - TWO_PI_HI - TWO_PI_MID

STREAM = [("ada", 48), ("ret_in", 24), ("ret_out", 8), ("ffn0", 33), ("att_in", 36), ("att_out", 4),
          ("ffn1", 33), ("w_in", 12), ("mix_out", 4), ("ffn2", 33), ("fourier", 4), ("moe", EXPERTS * 42)]
FIRST_BLOCK = {}
_n = 0
for _name, _count in STREAM:
    FIRST_BLOCK[_name] = _n
    _n += _count

COLS = [("c", 16), ("b_ada", 96), ("norm_g", 32), ("short_w", 36), ("short_b", 12), ("skip", 8),
        ("f_b1", 1), ("f_b2", 1), ("f_freq", 2)]
COL_AT = {}
_n = 0
for _name, _count in COLS:
    COL_AT[_name] = _n
    _n += _count
N_COLS = _n


class Signal:

    def __init__(self, sem, stages, credits=0):
        self.sem = sem
        self.base = {}
        total = credits
        for name, count in stages:
            self.base[name] = total
            total += count

    def after(self, stage, k=0):
        return self.base[stage] + k + 1


def build(nc, a, out):
    ctx = ExitStack()
    with ctx:
        def sb(name, shape, dt=F32):
            return ctx.enter_context(nc.sbuf_tensor(name, shape, dt))

        def sem(name):
            return ctx.enter_context(nc.semaphore(name))

        ring = sb("ring", [P, RING, SLOT])
        x_tok = sb("x_tok", [P, TT, D])
        x_fm = sb("x_fm", [P, KD, 2 * T])
        work = sb("work", [P, TT, D])
        silu_sb = sb("silu_sb", [P, 2, BANK])
        h_fm = sb("h_fm", [P, 2, 2, T])
        gate_row = sb("gate_row", [P, 4, D])
        ln_gb = sb("ln_gb", [P, 2, D])
        sq = sb("sq", [P, 3, P])
        cols = sb("cols", [P, N_COLS])
        silu_c = sb("silu_c", [P, KD, 2])
        silu_cb = sb("silu_cb", [P, KD, P])
        mod = sb("mod", [P, 4, 16, 2])
        mod_a = sb("mod_a", [P, KD, 2])
        stat = sb("stat", [P, 64])
        router_w = sb("router_w", [P, KD, EXPERTS])
        router_b = sb("router_b", [P, EXPERTS])
        route = sb("route", [P, TT, 4, EXPERTS])
        pairs = sb("pairs", [P, 2, EXPERTS, EXPERTS])
        gates = sb("gates", [P, TT, EXPERTS])
        BIG = 22336
        big = sb("big", [P, BIG])
        ps = ctx.enter_context(nc.psum_tensor("ps", [P, 8, BANK], F32))
        ident, rev, ones = sq[:, 0, :], sq[:, 1, :], sq[:, 2, :]
        psf = ps[:, :, :].rearrange("p b n -> p (b n)")

        def carve(at, *shape):
            n = int(np.prod(shape))
            assert at + n <= BIG
            v = big[:, at:at + n]
            if len(shape) == 1:
                return v
            names = "abcd"[:len(shape)]
            kw = {k: s for k, s in zip(names[1:], shape[1:])}
            return v.rearrange(f"p ({' '.join(names)}) -> p {' '.join(names)}", **kw)

        def col(name, i, n=1):
            return cols[:, COL_AT[name] + i:COL_AT[name] + i + n]

        r_raw = carve(0, 8, 2, T)
        r_rot = carve(4096, 8, 2, T)
        r_v = carve(8192, TT, RH * RDV)
        r_gate = carve(12288, TT, RH * RDV)
        r_decay = carve(16384, RH, 384)
        r_rope = carve(17920, 2, T)
        r_st = carve(18432, 2, 384)
        r_tmp = carve(19200, 2, T)
        r_y = carve(0, TT, RH * RDV)
        r_yfm = carve(4096, 2 * KD, T)
        a_q = carve(0, 24, T)
        a_k = carve(6144, 24, T)
        a_v = carve(12288, TT, AG * D)
        a_p = carve(18432, 1152)
        a_pt = carve(19584, 1152)
        a_bias = carve(20736, 2, AG, T)
        b_hot = carve(0, 384)
        b_tab = carve(384, 48)
        b_mask = carve(512, ROWS_W)
        b_rows = carve(1024, ROWS_W)
        y_k = carve(0, 2, 2, 2, HC)
        y_dft = carve(4096, 4, 2, T)
        y_win = carve(6144, 2, 2, HC)
        y_h = carve(8192, TT, 4, HC)
        y_abs = carve(12288, TT, 4, HC)
        y_w3 = carve(16384, 4, HC)
        y_w12 = carve(18432, 2, HID)
        y_feat = carve(18560, T)
        y_arg = carve(18816, 4, T)
        y_rn = carve(19840, 2, HC)
        z_raw = carve(6144, 12, T)
        z_u = carve(6144, TT, HC)
        z_y = carve(7168, 2, 2, HC)
        z = carve(9216, 12, T)
        n_q = carve(12288, 4, T)
        n_k = carve(13312, 4, 2 * T)
        n_v = carve(15360, 4, HC)
        ctx_tok = carve(20864 - 2048, TT, D)
        n_p = carve(17408, 2, BANK)
        n_pt = carve(18432, 2, BANK)
        n_bias = carve(19456, 2, 384)
        n_mask = carve(20224, 384)
        f_cs = carve(0, 4, BANK)
        f_a = carve(2048, TT, 4, BANK)
        m_acc = carve(8192, TT, D)

        rows_dram = nc.dram_tensor("bias_rows", [AG * AH, ROWS_W], F32, kind="Internal").ap()

        landed = [sem(f"landed{s}") for s in range(RING)]
        ring_free = sem("ring_free")
        consts_in = sem("consts_in")
        x_in = sem("x_in")
        aux_names = ["gate_bias", "router", "ret_consts", "bias_consts", "rows_out", "hyena_in", "ctx_in",
                     "n_mask", "fourier_in"]
        aux = {n: sem(f"in_{n}") for n in aux_names}
        bias_in = [sem(f"bias_in{i}") for i in range(2)]
        ln_in = sem("ln_in")
        out_done = sem("out_done")

        TR = [("x0", 4), ("ret", 8), ("x1", 4), ("x2", 4), ("att", 4), ("x3", 4), ("m0", 4), ("mc", 4),
              ("vtok", 2), ("ytok", 2), ("nat", 2), ("m1", 4), ("m2", 4), ("m3", 4)]
        transposed = Signal(sem("transposed"), TR)
        fm_saved = Signal(sem("fm_saved"), [s for s in TR if s[0] not in ("m0", "mc", "m1", "m2", "m3")])
        mod_saved = Signal(sem("mod_saved"), [(m, 8) for m in ("m0", "mc", "m1", "m2", "m3")])
        NORMS = ["ln0", "ln1", "ln2", "ln3", "m0", "mc", "m1", "m2", "m3", "fin"]
        moments = Signal(sem("moments"), [(n, 2) for n in NORMS])
        roots = Signal(sem("roots"), [(n, 2) for n in NORMS])
        squares = Signal(sem("squares"), [(n, 2) for n in NORMS[4:]])
        x_ready = Signal(sem("x_ready"), [("x1", 2), ("x2", 2), ("x3", 2), ("x4", 2)] +
                         [(n, 2) for n in NORMS[4:]])
        x_summed = Signal(sem("x_summed"), [(n, 2) for n in ("mix", "ffn2", "fourier", "moe")])
        acc_read = Signal(sem("acc_read"), [(n, 4) for n in
                          ("ret_out", "ffn0", "att_out", "ffn1", "mix_out", "ffn2", "fourier")] +
                          [("moe", 4 * EXPERTS)], credits=4)
        PROJ = [("ret_in", 24), ("att_in", 36), ("w_in", 16), ("four_a", 8), ("four_y", 4)]
        proj_saved = Signal(sem("proj_saved"), PROJ, credits=6)
        banked = Signal(sem("banked"), [("four_a", 8), ("four_y", 4)])
        GLU = [("ffn0", 11), ("ffn1", 11), ("ffn2", 11), ("moe", 14 * EXPERTS)]
        silu_done = Signal(sem("silu_done"), GLU)
        h_ready = Signal(sem("h_ready"), GLU, credits=2)
        ada_ready = sem("ada_ready")
        ada_saved = sem("ada_saved")
        rope_done = sem("rope_done")
        st_ready, st_saved, y_ready = sem("st_ready"), sem("st_saved"), sem("y_ready")
        y_var, y_root, y_read, y_gated = sem("y_var"), sem("y_root"), sem("y_read"), sem("y_gated")
        rows_ready, rows_saved = sem("rows_ready"), sem("rows_saved")
        HEADS = [("att", 2 * AH), ("nat", 2 * NH)]
        scored = Signal(sem("scored"), HEADS)
        negmax = Signal(sem("negmax"), HEADS)
        probs = Signal(sem("probs"), HEADS)
        probs_t = Signal(sem("probs_t"), HEADS)
        probs_fm = Signal(sem("probs_fm"), HEADS)
        mixed = Signal(sem("mixed"), HEADS)
        head_saved = Signal(sem("head_saved"), HEADS)
        masked = sem("masked")
        hy_pe, hy_dve, hy_act = sem("hy_pe"), sem("hy_dve"), sem("hy_act")
        conv_f, conv_y, conv_t, conv_out = sem("conv_f"), sem("conv_y"), sem("conv_t"), sem("conv_out")
        short_done = sem("short_done")
        routed, gates_ready, route_exp = sem("routed"), sem("gates_ready"), sem("route_exp")
        route_var = sem("route_var")
        dve_step, act_step = sem("dve_step"), sem("act_step")

        def stream_free(stage, n):
            return RING + FIRST_BLOCK[stage] + n + 1

        def slot_of(stage, n):
            return (FIRST_BLOCK[stage] + n) % RING

        def landings(stage, n):
            return 16 * ((FIRST_BLOCK[stage] + n) // RING + 1)

        block = ctx.enter_context(nc.Block())

        @block.sync
        def _(sp):
            def load(stage, n, src, i=0, e=0):
                s = slot_of(stage, n)
                k, w = src.shape[1], src.shape[2]
                dst = ring[:, s, :].rearrange("p (k w) -> p k w", k=k)
                sp.wait_ge(ring_free, FIRST_BLOCK[stage] + n + 1 + i * RING + e * 42)
                sp.dma_start(dst, src).then_inc(landed[s], 16)

            def wide(w, c0, half):
                return w.rearrange("(k p) n -> p k n", p=P)[:, 4 * half:4 * half + 4, bass.ds(c0, 512)]

            def narrow(w, c0):
                return w.rearrange("(k p) n -> p k n", p=P)[:, :, bass.ds(c0, 256)]

            def down(w, k0):
                return w.rearrange("(k p) n -> p k n", p=P)[:, bass.ds(k0, 2), :]

            def load_glu(stage, nj, gate, up, dn, e=0):
                load(stage, 0, gate(0), 0, e)
                load(stage, 1, up(0), 0, e)
                first = 2 + nj % 2

                def unit(j, n, i=0):
                    load(stage, n, gate(j), i, e)
                    load(stage, n + 1, up(j), i, e)
                    load(stage, n + 2, dn(j - 1), i, e)

                for j in range(1, first):
                    unit(j, 3 * j - 1)
                with sp.Fori(0, (nj - first) // 2) as i:
                    for u in range(2):
                        unit(first + u + i * 2, 3 * (first + u) - 1, i)
                load(stage, 3 * nj - 1, dn(nj - 1), 0, e)

            ada = a["w_ada_2"].rearrange("l (k p) n -> p (l k) n", p=P)
            for layer in range(2):
                with sp.Fori(0, 2) as i:
                    for b in range(12):
                        s = slot_of("ada", b)
                        k0 = layer * 8 + 4 * (b % 2)
                        sp.wait_ge(ring_free, 24 * layer + b + 1 + i * 12)
                        sp.dma_start(ring[:, s, :].rearrange("p (k w) -> p k w", k=4),
                                     ada[:, k0:k0 + 4, bass.ds(i * 3072 + (b // 2) * 512, 512)]
                                     ).then_inc(landed[s], 16)
            for b in range(8):
                load("ret_in", b, narrow(a["ret_w_in"], b * 256))
            for b in range(16):
                load("ret_in", 8 + b, wide(a["ret_w_in"], 2048 + (b // 2) * 512, b % 2))
            for b in range(8):
                load("ret_out", b, down(a["ret_w_out"], 2 * b))

            def ffn(stage, layer):
                up = a["ffn_w_up"][layer, :, :]
                dn = a["ffn_w_down"][layer, :, :]
                load_glu(stage, 11, lambda j: narrow(up, j * 256), lambda j: narrow(up, FFN + j * 256),
                         lambda j: down(dn, j * 2))

            ffn("ffn0", 0)
            with sp.Fori(0, 4) as i:
                for b in range(6):
                    load("att_in", b, narrow(a["attn_w_in"], i * 1536 + b * 256), i)
            with sp.Fori(0, 2) as i:
                for b in range(6):
                    load("att_in", 24 + b, wide(a["attn_w_in"], 6144 + i * 1536 + (b // 2) * 512, b % 2), i)
            for b in range(4):
                load("att_out", b, down(a["attn_w_out"], 2 * b))
            ffn("ffn1", 1)
            for b in range(10):
                load("w_in", b, narrow(a["w_in_2"], b * 256))
            for b in range(2):
                load("w_in", 10 + b, wide(a["w_in_2"], 2560, b))
            for b in range(4):
                load("mix_out", b, down(a["w_mix_out_2"], 2 * b))
            load_glu("ffn2", 11, lambda j: narrow(a["ffn_w1_2"], j * 256),
                     lambda j: narrow(a["ffn_w3_2"], j * 256), lambda j: down(a["ffn_w2_2"], j * 2))
            for b in range(4):
                load("fourier", b, down(a["w_fourier_2"], 2 * b))
            w1 = a["moe_w1_2"].rearrange("e (k p) n -> p (e k) n", p=P)
            w3 = a["moe_w3_2"].rearrange("e (k p) n -> p (e k) n", p=P)
            w2 = a["moe_w2_2"].rearrange("e (k p) n -> p (e k) n", p=P)
            with sp.Fori(0, EXPERTS) as e:
                load_glu("moe", 14, lambda j: w1[:, bass.ds(e * 8, 8), bass.ds(j * 256, 256)],
                         lambda j: w3[:, bass.ds(e * 8, 8), bass.ds(j * 256, 256)],
                         lambda j: w2[:, bass.ds(e * 28 + j * 2, 2), :], e)
            for t in range(TT):
                sp.wait_ge(x_ready.sem, x_ready.after("fin", t))
                sp.dma_start(out[t * P:(t + 1) * P, :], work[:, t, :]).then_inc(out_done, 16)
            sp.wait_ge(out_done, 16 * TT)

        @block.gpsimd
        def _(pool):
            pool.dma_start(sq[:, :, :], a["squares"]).then_inc(consts_in, 16)
            pool.dma_start(cols[:, :], a["cols"]).then_inc(consts_in, 16)
            pool.dma_start(x_tok[:, :, :], a["x"].rearrange("(t p) d -> p t d", p=P)).then_inc(x_in, 16)
            for hl in range(4):
                bias = a["b_ada_2"][hl // 2, (hl % 2) * 3072 + 2048:(hl % 2) * 3072 + 3072]
                pool.dma_start(gate_row[:, hl, :], bias.partition_broadcast(P)).then_inc(aux["gate_bias"], 16)
            pool.dma_start(r_decay, a["decay"]).then_inc(aux["ret_consts"], 16)
            pool.dma_start(r_rope, a["rope"]).then_inc(aux["ret_consts"], 16)
            pool.dma_start(router_w[:, :, :], a["w_router_2"].rearrange("(k p) e -> p k e", p=P)
                           ).then_inc(aux["router"], 16)
            pool.dma_start(router_b[:, :], a["b_router_2"].partition_broadcast(P)).then_inc(aux["router"], 16)

            def load_ln(n):
                if n:
                    pool.wait_ge(x_ready.sem, x_ready.after(f"x{n}", 1))
                pool.dma_start(ln_gb[:, 0, :], a["ln_gain"][n // 2, n % 2, :].partition_broadcast(P)
                               ).then_inc(ln_in, 16)
                pool.dma_start(ln_gb[:, 1, :], a["ln_bias"][n // 2, n % 2, :].partition_broadcast(P)
                               ).then_inc(ln_in, 16)

            load_ln(0)
            load_ln(1)
            pool.dma_start(b_hot[0:BUCKETS, :], a["bucket_hot"]).then_inc(aux["bias_consts"], 16)
            pool.dma_start(b_tab[0:BUCKETS, :], a["rel_bias"]).then_inc(aux["bias_consts"], 16)
            pool.dma_start(b_mask[0:AG * AH, :], a["rel_mask"]).then_inc(aux["bias_consts"], 16)
            pool.wait_ge(rows_saved, 1)
            pool.dma_start(rows_dram, b_rows[0:AG * AH, :]).then_inc(aux["rows_out"], 16)
            load_ln(2)
            pool.wait_ge(aux["rows_out"], 16)
            for h in range(AH):
                if h >= 2:
                    pool.wait_ge(scored.sem, scored.after("att", 2 * (h - 2) + 1))
                pool.dma_start(a_bias[:, h % 2, :, :],
                               bass.AP(rows_dram.tensor, h * ROWS_W, [[1, P], [AH * ROWS_W, AG], [1, T]])
                               ).then_inc(bias_in[h % 2], 16)
            load_ln(3)
            pool.wait_ge(fm_saved.sem, fm_saved.after("att", 3))
            pool.dma_start(y_dft, a["dft"]).then_inc(aux["hyena_in"], 16)
            pool.dma_start(y_win, a["window"]).then_inc(aux["hyena_in"], 16)
            pool.dma_start(y_w3[0:HID, :, :], a["hy_f_w3_2"].rearrange("h (n c) -> h n c", n=4)
                           ).then_inc(aux["hyena_in"], 16)
            pool.dma_start(y_w12[0:EMB, 0, :], a["hy_f_w1_2"]).then_inc(aux["hyena_in"], 16)
            pool.dma_start(y_w12[0:HID, 1, :], a["hy_f_w2_2"]).then_inc(aux["hyena_in"], 16)
            pool.dma_start(y_feat[0:EMB, :], a["features"]).then_inc(aux["hyena_in"], 16)
            pool.wait_ge(hy_dve, 17)
            pool.dma_start(ctx_tok, a["ctx_2"].rearrange("(t p) d -> p t d", p=P)).then_inc(aux["ctx_in"], 16)
            pool.wait_ge(x_ready.sem, x_ready.after("mc", 1))
            pool.dma_start(n_mask, a["window_mask"]).then_inc(aux["n_mask"], 16)
            for h in range(NH):
                if h >= 2:
                    pool.wait_ge(scored.sem, scored.after("nat", 2 * (h - 2) + 1))
                for r in range(2):
                    at = h * 15 * 31 + (WIN_R - 4 + r) * 31 + WIN_C - GRID_W
                    pool.dma_start(n_bias[64 * r:64 * r + 64, h % 2, :].rearrange("p (r c) -> p r c", c=GRID_W),
                                   bass.AP(a["na_rpb_2"].tensor, at, [[1, GRID_W], [31, 6], [1, GRID_W]])
                                   ).then_inc(bias_in[h % 2], 16)
                if h == 0:
                    pool.wait_ge(aux["n_mask"], 16)
                pool.wait_ge(bias_in[h % 2], 16 * (AH // 2) + 32 * (h // 2 + 1))
                nc.gpsimd.tensor_tensor(n_bias[:, h % 2, :], n_bias[:, h % 2, :], n_mask, ALU.add
                                        ).then_inc(masked, 1)
            pool.wait_ge(fm_saved.sem, fm_saved.after("nat", 1))
            pool.dma_start(f_cs, a["fourier"]).then_inc(aux["fourier_in"], 16)
            pool.dma_start(ln_gb[:, 0, :], a["final_g_2"].partition_broadcast(P)).then_inc(ln_in, 16)

        @block.tensor
        def _(pe):
            mm = nc.tensor.matmul

            def wait_block(stage, n, i=0, e=0):
                s = slot_of(stage, n)
                pe.wait_ge(landed[s], landings(stage, n) + i * 16 + e * (42 // RING * 16))
                return ring[:, s, :]

            def transposes(stage, src, chunks, first_bank=0):
                for q in range(chunks // 2):
                    if q >= 4:
                        pe.wait_ge(fm_saved.sem, fm_saved.after(stage, q - 4))
                    for c in (2 * q, 2 * q + 1):
                        for t in range(TT):
                            o = (c % 2) * T + t * P
                            last = nc.tensor.transpose(ps[:, first_bank + q % 4, o:o + P],
                                                       src[:, t, c * P:(c + 1) * P], ident)
                    last.then_inc(transposed.sem, 1)

            def project_wide(stage, n, g, lhs_fm, tiles):
                base = PROJ_BASE[stage]
                w = [wait_block(stage, n), wait_block(stage, n + 1)]
                for t in range(tiles):
                    pe.wait_ge(proj_saved.sem, base + g + t + 1)
                for half in range(2):
                    wv = w[half].rearrange("p (k w) -> p k w", k=4)
                    for t in range(tiles):
                        for k in range(4):
                            kk = 4 * half + k
                            last = mm(ps[:, 2 + (base + g + t) % 6, :], lhs_fm[:, kk, t * P:(t + 1) * P],
                                      wv[:, k, :], start=kk == 0, stop=kk == KD - 1)
                    last.then_inc(ring_free, 1)

            def accumulate(stage, n, lhs, kt, start, stop, i=0, e=0):
                w = wait_block(stage, n, i, e).rearrange("p (k w) -> p k w", k=2)
                for k in range(2):
                    for t in range(TT):
                        for half in range(2):
                            last = mm(ps[:, 2 * t + half, :], lhs(kt + k, t), w[:, k, half * 512:half * 512 + 512],
                                      start=start and k == 0, stop=stop and k == 1)
                last.then_inc(ring_free, 1)

            def wait_acc(stage, e=0):
                pe.wait_ge(acc_read.sem, acc_read.base[stage] + e * 4)

            def glu(stage, nj, e=0, ec=0):
                def ups(j, n, u, i=0):
                    pe.wait_ge(h_ready.sem, h_ready.base[stage] - 1 + u + i * 2 + e * 14)
                    for m in range(2):
                        w = wait_block(stage, n + m, i, e).rearrange("p (k w) -> p k w", k=KD)
                        for f in range(2):
                            for k in range(KD):
                                last = mm(ps[:, 4 + 2 * (u % 2) + m, f * T:(f + 1) * T],
                                          w[:, k, f * P:(f + 1) * P], x_fm[:, k, 0:T],
                                          start=k == 0, stop=k == KD - 1)
                        last.then_inc(ring_free, 1)

                def downs(u, n, start, stop, i=0):
                    pe.wait_ge(h_ready.sem, h_ready.after(stage, u) + i * 2 + e * 14)
                    accumulate(stage, n, lambda k, t: h_fm[:, u % 2, k, t * P:(t + 1) * P], 0, start, stop, i, e)

                ups(0, 0, 0)
                first = 2 + nj % 2
                for j in range(1, first):
                    ups(j, 3 * j - 1, j)
                    if j == 1:
                        wait_acc(stage, e)
                    downs(j - 1, 3 * j + 1, j == 1, False)
                with pe.Fori(0, (nj - first) // 2) as i:
                    for d in range(2):
                        j = first + d
                        ups(j, 3 * j - 1, j, i)
                        downs(j - 1, 3 * j + 1, False, False, i)
                downs(nj - 1, 3 * nj - 1, False, True)

            pe.wait_ge(ada_ready, 2)
            with pe.Fori(0, 4) as i:
                for nb in range(6):
                    w = []
                    for b in (2 * nb, 2 * nb + 1):
                        s = slot_of("ada", b)
                        pe.wait_ge(landed[s], landings("ada", b) + i * 32)
                        w.append(ring[:, s, :].rearrange("p (k w) -> p k w", k=4))
                    pe.wait_ge(ada_saved, nb + 1 + i * 6)
                    if nb < 4:
                        for f in range(4):
                            for k in range(KD):
                                last = mm(ps[:, nb, 2 * f:2 * f + 2], w[k // 4][:, k % 4, f * P:(f + 1) * P],
                                          silu_c[:, k, :], start=k == 0, stop=k == KD - 1)
                        last.then_inc(ring_free, 2)
                    else:
                        for k in range(KD):
                            last = mm(ps[:, nb, :], silu_cb[:, k, :], w[k // 4][:, k % 4, :],
                                      start=k == 0, stop=k == KD - 1)
                        last.then_inc(ring_free, 2)

            pe.wait_ge(x_in, 16)
            pe.wait_ge(ada_saved, 30)
            transposes("x0", x_tok, KD)
            pe.wait_ge(fm_saved.sem, fm_saved.after("x0", 3))
            for b in range(8):
                w = wait_block("ret_in", b).rearrange("p (k w) -> p k w", k=KD)
                g = PROJ_BASE["ret_in"] + b
                pe.wait_ge(proj_saved.sem, g + 1)
                for f in range(2):
                    for k in range(KD):
                        last = mm(ps[:, 2 + g % 6, f * T:(f + 1) * T], w[:, k, f:256:2], x_fm[:, k, 0:T],
                                  start=k == 0, stop=k == KD - 1)
                last.then_inc(ring_free, 1)
            for nb in range(8):
                project_wide("ret_in", 8 + 2 * nb, 8 + 2 * nb, x_fm, TT)
            pe.wait_ge(proj_saved.sem, proj_saved.after("ret_in", 23))
            for h in range(RH):
                pe.wait_ge(rope_done, 5 + h)
                if h:
                    pe.wait_ge(st_saved, h)
                for jt in range(TT):
                    n = T - jt * P
                    for f in range(2):
                        last = mm(ps[:, 0, jt * T:jt * T + n], r_rot[:, 4 + h, f, jt * P:(jt + 1) * P],
                                  r_rot[:, h, f, jt * P:T], start=f == 0, stop=f == 1)
                last.then_inc(st_ready, 1)
                pe.wait_ge(st_saved, h + 1)
                for t in range(TT):
                    bank = 1 + (2 * h + t) % 4
                    if 2 * h + t >= 4:
                        pe.wait_ge(y_read, 2 * h + t - 3)
                    v = r_v[:, :, h * RDV:(h + 1) * RDV]
                    st = r_st[:, h % 2, :]
                    if t == 0:
                        last = mm(ps[:, bank, :], st[:, 0:P], v[:, 0, :], start=True, stop=True)
                    else:
                        mm(ps[:, bank, :], st[:, P:T], v[:, 0, :], start=True, stop=False)
                        last = mm(ps[:, bank, :], st[:, T:T + P], v[:, 1, :], start=False, stop=True)
                    last.then_inc(y_ready, 1)
            pe.wait_ge(y_gated, 2 * RH)
            transposes("ret", r_y, 2 * KD)
            pe.wait_ge(fm_saved.sem, fm_saved.after("ret", 7))
            wait_acc("ret_out")
            for b in range(8):
                accumulate("ret_out", b, lambda k, t: r_yfm[:, k, t * P:(t + 1) * P], 2 * b, b == 0, b == 7)

            def first_block_ffn(xa, stage):
                pe.wait_ge(x_ready.sem, x_ready.after(xa, 1))
                transposes(xa, x_tok, KD)
                pe.wait_ge(fm_saved.sem, fm_saved.after(xa, 3))
                glu(stage, 11)

            first_block_ffn("x1", "ffn0")

            pe.wait_ge(aux["bias_consts"], 48)
            pe.wait_ge(x_ready.sem, x_ready.after("x2", 1))
            mm(ps[0:AG * AH, 7, 0:ROWS_W], b_tab[0:BUCKETS, 0:AG * AH], b_hot[0:BUCKETS, :],
               start=True, stop=True).then_inc(rows_ready, 1)
            transposes("x2", x_tok, KD)
            pe.wait_ge(fm_saved.sem, fm_saved.after("x2", 3))
            pe.wait_ge(rows_saved, 1)
            g0 = PROJ_BASE["att_in"]
            with pe.Fori(0, 4) as i:
                for b in range(6):
                    w = wait_block("att_in", b, i).rearrange("p (k w) -> p k w", k=KD)
                    pe.wait_ge(proj_saved.sem, g0 + b + 1 + i * 6)
                    for f in range(2):
                        for k in range(KD):
                            last = mm(ps[:, 2 + (g0 + b) % 6, f * T:(f + 1) * T], w[:, k, f * P:(f + 1) * P],
                                      x_fm[:, k, 0:T], start=k == 0, stop=k == KD - 1)
                    last.then_inc(ring_free, 1)
            with pe.Fori(0, 2) as i:
                for b in range(3):
                    w = [wait_block("att_in", 24 + 2 * b + m, i) for m in range(2)]
                    for t in range(TT):
                        pe.wait_ge(proj_saved.sem, g0 + 24 + 2 * b + t + 1 + i * 6)
                    for half in range(2):
                        wv = w[half].rearrange("p (k w) -> p k w", k=4)
                        for t in range(TT):
                            for k in range(4):
                                kk = 4 * half + k
                                last = mm(ps[:, 2 + (g0 + 24 + 2 * b + t) % 6, :], x_fm[:, kk, t * P:(t + 1) * P],
                                          wv[:, k, :], start=kk == 0, stop=kk == KD - 1)
                        last.then_inc(ring_free, 1)
            pe.wait_ge(proj_saved.sem, proj_saved.after("att_in", 35))

            def heads(stage, nh, scores, n_tr, pt_bank, probs_of, pt_of, mix):
                def score(h, it):
                    u = 2 * h + it
                    if h:
                        pe.wait_ge(probs.sem, probs.after(stage, u - 2))
                    scores(h, it).then_inc(scored.sem, 1)

                score(0, 0)
                score(0, 1)
                for h in range(nh):
                    for it in range(2):
                        u = 2 * h + it
                        pe.wait_ge(probs.sem, probs.after(stage, u))
                        if h:
                            pe.wait_ge(probs_fm.sem, probs_fm.after(stage, u - 2))
                        for q in range(n_tr[it]):
                            last = nc.tensor.transpose(psf[:, pt_bank[it] * BANK + q * P:pt_bank[it] * BANK + (q + 1) * P],
                                                       probs_of(it)[:, q * P:(q + 1) * P], ident)
                        last.then_inc(probs_t.sem, 1)
                        if h + 1 < nh:
                            score(h + 1, it)
                    for it in range(2):
                        u = 2 * h + it
                        pe.wait_ge(probs_fm.sem, probs_fm.after(stage, u))
                        if h:
                            pe.wait_ge(head_saved.sem, head_saved.after(stage, u - 2))
                        mix(h, it, pt_of(it)).then_inc(mixed.sem, 1)

            def att_scores(h, it):
                if it == 0:
                    pe.wait_ge(bias_in[h % 2], 16 * (h // 2 + 1))
                n = (it + 1) * P
                at = it * BANK
                for g in range(AG):
                    f, r = g * 8 + h // 2, (h % 2) * AHD
                    o = psf[:, at + g * n:at + (g + 1) * n]
                    mm(o, a_q[r:r + AHD, f, it * P:(it + 1) * P], a_k[r:r + AHD, f, 0:n], start=True, stop=False)
                    last = mm(o, rev, a_bias[:, h % 2, g, T - n:T], start=False, stop=True)
                return last

            def att_mix(h, it, pt):
                n = it + 1
                for g in range(AG):
                    for j in range(n):
                        q = g * n + j
                        last = mm(ps[:, 6 + it, 0:AHD], pt[:, q * P:(q + 1) * P],
                                  a_v[:, j, g * D + h * AHD:g * D + (h + 1) * AHD],
                                  start=q == 0, stop=q == AG * n - 1)
                return last

            heads("att", AH, att_scores, (3, 6), (3, 4), lambda it: a_p[:, 384 * it:384 + 768 * it],
                  lambda it: a_pt[:, 384 * it:384 + 768 * it], att_mix)
            pe.wait_ge(head_saved.sem, head_saved.after("att", 2 * AH - 1))
            transposes("att", work, KD)
            pe.wait_ge(fm_saved.sem, fm_saved.after("att", 3))
            wait_acc("att_out")
            for b in range(4):
                accumulate("att_out", b, lambda k, t: x_fm[:, k, t * P:(t + 1) * P], 2 * b, b == 0, b == 3)
            first_block_ffn("x3", "ffn1")

            pe.wait_ge(x_ready.sem, x_ready.after("x4", 1))
            pe.wait_ge(aux["hyena_in"], 96)
            mm(ps[0:HID, 0, 0:T], y_w12[0:EMB, 0, :], y_feat[0:EMB, :], start=True, stop=True).then_inc(hy_pe, 1)
            pe.wait_ge(hy_act, 1)
            mm(ps[0:HID, 1, 0:T], y_w12[0:HID, 1, :], y_arg[0:HID, 2, :], start=True, stop=True).then_inc(hy_pe, 1)
            pe.wait_ge(hy_act, 2)
            for n in range(4):
                for t in range(TT):
                    mm(ps[:, (2 * n + t + 2) % 8, :], y_arg[0:HID, 3, t * P:(t + 1) * P], y_w3[0:HID, n, :],
                       start=True, stop=True).then_inc(hy_pe, 1)
            for o in range(2):
                for side in range(2):
                    n = 2 * o + side
                    pe.wait_ge(hy_act, 2 + 2 * n + 2)
                    for t in range(TT):
                        last = mm(ps[:, 2 + o, :], ones, y_abs[:, t, n, :], start=n % 2 == 0 and t == 0,
                                  stop=n % 2 == 1 and t == 1)
                last.then_inc(hy_pe, 1)
            for o in range(2):
                pe.wait_ge(hy_dve, 13 + o)
                for part in range(2):
                    for f in range(2):
                        bank = 4 * (o % 2) + 2 * part + f
                        for t in range(TT):
                            last = mm(ps[:, bank, :], y_dft[:, part, t, f * P:(f + 1) * P],
                                      y_abs[:, t, 2 * o + part, :], start=t == 0, stop=t == TT - 1)
                last.then_inc(hy_pe, 1)

            def modulated(stage, extra=None):
                for t in range(TT):
                    pe.wait_ge(x_ready.sem, x_ready.after(stage, t))
                transposes(stage, work, KD)

            pe.wait_ge(hy_dve, 17)
            modulated("m0")
            pe.wait_ge(mod_saved.sem, mod_saved.after("m0", 7))
            modulated("mc")
            pe.wait_ge(mod_saved.sem, mod_saved.after("mc", 7))
            g0 = PROJ_BASE["w_in"]
            g = g0
            for b in range(10):
                w = wait_block("w_in", b).rearrange("p (k w) -> p k w", k=KD)
                wide_k = b >= 8
                pe.wait_ge(proj_saved.sem, g + 1)
                if wide_k:
                    pe.wait_ge(proj_saved.sem, g + 2)
                for f in range(2):
                    dst = ps[:, 2 + (g + f) % 6, :] if wide_k else ps[:, 2 + g % 6, f * T:(f + 1) * T]
                    for k in range(KD):
                        last = mm(dst, w[:, k, f * P:(f + 1) * P], x_fm[:, k, 0:2 * T if wide_k else T],
                                  start=k == 0, stop=k == KD - 1)
                last.then_inc(ring_free, 1)
                g += 2 if wide_k else 1
            project_wide("w_in", 10, g - g0, x_fm, 4)

            pe.wait_ge(short_done, 4)
            for t in range(TT):
                for c in range(4):
                    last = nc.tensor.transpose(ps[:, t, c * P:(c + 1) * P], z[:, c, t * P:(t + 1) * P], ident)
                last.then_inc(transposed.sem, 1)
            for o in range(2):
                pe.wait_ge(fm_saved.sem, fm_saved.after("vtok" if o == 0 else "ytok", 1))
                pe.wait_ge(proj_saved.sem, proj_saved.after("w_in", 15))
                for part in range(2):
                    for f in range(2):
                        for t in range(TT):
                            last = mm(ps[:, 4 + 2 * part + f, :], y_dft[:, part, t, f * P:(f + 1) * P], z_u[:, t, :],
                                      start=t == 0, stop=t == TT - 1)
                last.then_inc(conv_f, 1)
                pe.wait_ge(conv_y, o + 1)
                for c in range(4):
                    for part in range(2):
                        for f in range(2):
                            last = mm(ps[:, 2 + c // 2, (c % 2) * T:(c % 2 + 1) * T], z_y[:, part, f, c * P:(c + 1) * P],
                                      y_dft[:, 2 + part, f, :], start=part == 0 and f == 0, stop=part == 1 and f == 1)
                    if c % 2:
                        last.then_inc(conv_t, 1)
                if o == 0:
                    pe.wait_ge(conv_out, 4)
                    for t in range(TT):
                        for c in range(4):
                            last = nc.tensor.transpose(ps[:, t, c * P:(c + 1) * P], z[:, c, t * P:(t + 1) * P], ident)
                        last.then_inc(transposed.sem, 1)

            pe.wait_ge(conv_out, 8)

            def nat_scores(h, it):
                if it == 0:
                    pe.wait_ge(masked, h + 1)
                f, r = h // 4, (h % 4) * NHD
                mm(ps[:, it, :], n_q[r:r + NHD, f, it * P:(it + 1) * P], n_k[r:r + NHD, f, :], start=True, stop=False)
                return mm(ps[:, it, 0:T], rev, n_bias[:, h % 2, (1 - it) * P:(1 - it) * P + T],
                          start=False, stop=True)

            def nat_mix(h, it, pt):
                for q in range(4):
                    last = mm(ps[:, 4 + it, 0:NHD], pt[:, q * P:(q + 1) * P], n_v[:, q, h * NHD:(h + 1) * NHD],
                              start=q == 0, stop=q == 3)
                return last

            heads("nat", NH, nat_scores, (4, 4), (2, 3), lambda it: n_p[:, it, :], lambda it: n_pt[:, it, :], nat_mix)
            pe.wait_ge(head_saved.sem, head_saved.after("nat", 2 * NH - 1))
            transposes("nat", work, 4, first_bank=6)
            pe.wait_ge(fm_saved.sem, fm_saved.after("nat", 1))
            wait_acc("mix_out")
            for b in range(4):
                accumulate("mix_out", b, lambda k, t: x_fm[:, k, t * P:(t + 1) * P], 2 * b, b == 0, b == 3)

            modulated("m1")
            pe.wait_ge(mod_saved.sem, mod_saved.after("m1", 7))
            glu("ffn2", 11)

            modulated("m2")
            pe.wait_ge(mod_saved.sem, mod_saved.after("m2", 7))
            pe.wait_ge(aux["fourier_in"], 16)
            for g in range(4):
                for t in range(TT):
                    q = PROJ_BASE["four_a"] + 2 * g + t
                    pe.wait_ge(proj_saved.sem, q + 1)
                    for k in range(2):
                        last = mm(ps[:, 2 + q % 6, :], x_fm[:, 2 * g + k, t * P:(t + 1) * P], f_cs[:, k, :],
                                  start=k == 0, stop=k == 1)
                    last.then_inc(banked.sem, 1)
            pe.wait_ge(proj_saved.sem, proj_saved.after("four_a", 7))
            for d in range(KD):
                q = PROJ_BASE["four_y"] + d // 2
                if d % 2 == 0:
                    pe.wait_ge(proj_saved.sem, q + 1)
                for part in range(2):
                    for t in range(TT):
                        c = part * T + (d % 2) * P
                        last = mm(ps[:, 2 + q % 6, (d % 2) * T:(d % 2 + 1) * T], f_a[:, t, d // 2, c:c + P],
                                  f_cs[:, 2 + t, part * T:(part + 1) * T], start=part == 0 and t == 0,
                                  stop=part == 1 and t == 1)
                if d % 2:
                    last.then_inc(banked.sem, 1)
            pe.wait_ge(proj_saved.sem, proj_saved.after("four_y", 3))
            wait_acc("fourier")
            for b in range(4):
                accumulate("fourier", b, lambda k, t: x_fm[:, k, t * P:(t + 1) * P], 2 * b, b == 0, b == 3)

            modulated("m3")
            pe.wait_ge(mod_saved.sem, mod_saved.after("m3", 7))
            pe.wait_ge(aux["router"], 32)
            for t in range(TT):
                for k in range(KD):
                    last = mm(ps[:, 4 + t, 0:EXPERTS], x_fm[:, k, t * P:(t + 1) * P], router_w[:, k, :],
                              start=k == 0, stop=k == KD - 1)
            last.then_inc(routed, 1)
            pe.wait_ge(gates_ready, 1)
            with pe.Fori(0, EXPERTS) as e:
                glu("moe", 14, e)

        @block.scalar
        def _(act):
            steps = [0]

            def link(ins):
                steps[0] += 1
                ins.then_inc(act_step, 1)
                act.wait_ge(act_step, steps[0])

            def save_fm(stage, dst, n, first_bank=0):
                for q in range(n):
                    act.wait_ge(transposed.sem, transposed.after(stage, q))
                    nc.scalar.activation(dst(q), ps[:, first_bank + q % 4, :], ACT.Copy).then_inc(fm_saved.sem, 1)

            def x_fm_pair(q):
                return x_fm[:, 2 * q:2 * q + 2, 0:T]

            def root(stage):
                for t in range(TT):
                    act.wait_ge(moments.sem, moments.after(stage, t))
                    nc.scalar.activation(stat[:, 20 + t:21 + t], stat[:, 16 + t:17 + t], ACT.Sqrt
                                         ).then_inc(roots.sem, 1)

            def rms(stage, src, ready):
                for t in range(TT):
                    ready(t)
                    nc.scalar.activation(work[:, t, :], src[:, t, :], ACT.Square, accum_out=stat[:, 24 + t:25 + t]
                                         ).then_inc(squares.sem, 1)
                root(stage)

            def glu(stage, nj, e=0):
                def unit(u, n, i=0):
                    act.wait_ge(ring_free, stream_free(stage, n) + i * RING + e * 42)
                    act.wait_ge(h_ready.sem, h_ready.base[stage] - 1 + u + i * 2 + e * 14)
                    nc.scalar.activation(silu_sb[:, u % 2, :], ps[:, 4 + 2 * (u % 2), :], ACT.Silu
                                         ).then_inc(silu_done.sem, 1)
                unit(0, 0)
                first = 2 + nj % 2
                for j in range(1, first):
                    unit(j, 3 * j - 1)
                with act.Fori(0, (nj - first) // 2) as i:
                    for d in range(2):
                        unit(first + d, 3 * (first + d) - 1, i)

            act.wait_ge(consts_in, 32)
            nc.scalar.activation(silu_c[:, :, :].rearrange("p k c -> p (k c)"), col("c", 0, 16), ACT.Silu
                                 ).then_inc(ada_ready, 1)
            save_fm("x0", x_fm_pair, 4)
            g0 = PROJ_BASE["ret_in"]
            for b in range(8):
                act.wait_ge(ring_free, stream_free("ret_in", b))
                nc.scalar.activation(r_raw[:, b, :, :].rearrange("p f t -> p (f t)"), ps[:, 2 + (g0 + b) % 6, :],
                                     ACT.Copy).then_inc(proj_saved.sem, 1)
            for nb in range(8):
                act.wait_ge(ring_free, stream_free("ret_in", 8 + 2 * nb + 1))
                for t in range(TT):
                    dst = (r_v if nb < 4 else r_gate)[:, t, (nb % 4) * BANK:(nb % 4 + 1) * BANK]
                    nc.scalar.activation(dst, ps[:, 2 + (g0 + 8 + 2 * nb + t) % 6, :],
                                         ACT.Copy if nb < 4 else ACT.Silu).then_inc(proj_saved.sem, 1)
            for u in range(2 * RH):
                act.wait_ge(y_var, u + 1)
                nc.scalar.activation(stat[:, 34 + u % 2:35 + u % 2], stat[:, 32 + u % 2:33 + u % 2], ACT.Sqrt
                                     ).then_inc(y_root, 1)
            save_fm("ret", lambda q: r_yfm[:, 2 * q:2 * q + 2, :], 8)
            root("ln0")
            save_fm("x1", x_fm_pair, 4)
            glu("ffn0", 11)
            root("ln1")
            save_fm("x2", x_fm_pair, 4)
            g0 = PROJ_BASE["att_in"]
            act.wait_ge(aux["rows_out"], 16)
            for part in range(2):
                with act.Fori(0, 2) as i:
                    for b in range(6):
                        act.wait_ge(ring_free, stream_free("att_in", 12 * part + b) + i * RING)
                        dst = (a_k if part else a_q).rearrange("p f t -> p (f t)")
                        nc.scalar.activation(dst[:, bass.ds(i * 3072 + b * BANK, BANK)], ps[:, 2 + (g0 + b) % 6, :],
                                             ACT.Copy, scale=1.0 if part else AHD ** -0.5).then_inc(proj_saved.sem, 1)
            v_flat = a_v.rearrange("p t n -> p (t n)")
            with act.Fori(0, 2) as i:
                for b in range(3):
                    act.wait_ge(ring_free, stream_free("att_in", 24 + 2 * b + 1) + i * RING)
                    for t in range(TT):
                        nc.scalar.activation(v_flat[:, bass.ds(i * 1536 + t * AG * D + b * BANK, BANK)],
                                             ps[:, 2 + (g0 + 24 + 2 * b + t) % 6, :], ACT.Copy
                                             ).then_inc(proj_saved.sem, 1)

            def heads(stage, nh, scores_of, probs_of):
                for h in range(nh):
                    for it in range(2):
                        u = 2 * h + it
                        act.wait_ge(negmax.sem, negmax.after(stage, u))
                        if h:
                            act.wait_ge(probs_t.sem, probs_t.after(stage, u - 2))
                            act.wait_ge(head_saved.sem, head_saved.after(stage, u - 2))
                        nc.scalar.activation(probs_of(it), scores_of(it), ACT.Exp, bias=stat[:, 40 + it:41 + it],
                                             accum_out=stat[:, 42 + it:43 + it]).then_inc(probs.sem, 1)

            heads("att", AH, lambda it: psf[:, BANK * it:BANK * it + 384 * (it + 1)],
                  lambda it: a_p[:, 384 * it:384 + 768 * it])
            save_fm("att", x_fm_pair, 4)
            root("ln2")
            save_fm("x3", x_fm_pair, 4)
            glu("ffn1", 11)
            root("ln3")
            for m in range(2):
                act.wait_ge(hy_dve, m + 1)
                nc.scalar.activation(y_arg[0:HID, 2 + m, :], y_arg[0:HID, 0, :], ACT.Sin).then_inc(hy_act, 1)
            for n in range(4):
                for t in range(TT):
                    act.wait_ge(hy_dve, 2 + 2 * n + t + 1)
                    nc.scalar.activation(y_abs[:, t, n, :], y_h[:, t, n, :], ACT.Abs).then_inc(hy_act, 1)

            def x_of(stage, n):
                def ready(t):
                    act.wait_ge(x_summed.sem, x_summed.after(stage, t))
                return ready

            rms("m0", x_tok, lambda t: act.wait_ge(x_ready.sem, x_ready.after("x4", t)))

            def ctx_ready(t):
                act.wait_ge(aux["ctx_in"], 16)
                act.wait_ge(transposed.sem, transposed.after("m0", 3))
            rms("mc", ctx_tok, ctx_ready)
            g = PROJ_BASE["w_in"]
            act.wait_ge(x_ready.sem, x_ready.after("mc", 1))
            for b in range(10):
                act.wait_ge(ring_free, stream_free("w_in", b))
                if b < 8:
                    dst = z_raw[:, 2 * b:2 * b + 2, :] if b < 6 else n_q[:, 2 * (b - 6):2 * (b - 6) + 2, :]
                    nc.scalar.activation(dst.rearrange("p f t -> p (f t)"), ps[:, 2 + g % 6, :], ACT.Copy,
                                         scale=1.0 if b < 6 else NHD ** -0.5).then_inc(proj_saved.sem, 1)
                    g += 1
                else:
                    for f in range(2):
                        nc.scalar.activation(n_k[:, 2 * (b - 8) + f, :], ps[:, 2 + g % 6, :], ACT.Copy
                                             ).then_inc(proj_saved.sem, 1)
                        g += 1
            act.wait_ge(ring_free, stream_free("w_in", 11))
            for t in range(4):
                nc.scalar.activation(n_v[:, t, :], ps[:, 2 + g % 6, :], ACT.Copy).then_inc(proj_saved.sem, 1)
                g += 1
            act.wait_ge(short_done, 12)
            for stage in ("vtok", "ytok"):
                if stage == "ytok":
                    act.wait_ge(conv_f, 1)
                for t in range(TT):
                    act.wait_ge(transposed.sem, transposed.after(stage, t))
                    nc.scalar.activation(z_u[:, t, :], ps[:, t, :], ACT.Copy).then_inc(fm_saved.sem, 1)
            heads("nat", NH, lambda it: ps[:, it, :], lambda it: n_p[:, it, :])
            save_fm("nat", lambda q: x_fm[:, 4 + 2 * q:6 + 2 * q, 0:T], 2, first_bank=6)
            rms("m1", x_tok, x_of("mix", 0))
            glu("ffn2", 11)
            rms("m2", x_tok, x_of("ffn2", 0))
            for q in range(8):
                act.wait_ge(banked.sem, banked.after("four_a", q))
                nc.scalar.activation(f_a[:, q % 2, q // 2, :], ps[:, 2 + (PROJ_BASE["four_a"] + q) % 6, :], ACT.Copy
                                     ).then_inc(proj_saved.sem, 1)
            for q in range(4):
                act.wait_ge(banked.sem, banked.after("four_y", q))
                nc.scalar.activation(x_fm_pair(q), ps[:, 2 + (PROJ_BASE["four_y"] + q) % 6, :], ACT.Copy
                                     ).then_inc(proj_saved.sem, 1)
            rms("m3", x_tok, x_of("fourier", 0))
            act.wait_ge(route_var, 1)
            nc.scalar.activation(stat[:, 50:52], stat[:, 48:50], ACT.Exp).then_inc(route_exp, 1)
            with act.Fori(0, EXPERTS) as e:
                glu("moe", 14, e)
            rms("fin", x_tok, x_of("moe", 0))

        @block.vector
        def _(dve):
            V = nc.vector
            steps = [0]

            def link(ins):
                steps[0] += 1
                ins.then_inc(dve_step, 1)
                dve.wait_ge(dve_step, steps[0])

            V.memset(stat[:, 0:1], 0.0).then_inc(ring_free, RING)
            V.memset(stat[:, 1:2], 0.0).then_inc(ada_saved, 6)
            V.memset(stat[:, 2:3], 0.0).then_inc(proj_saved.sem, 6)
            V.memset(stat[:, 3:4], 0.0).then_inc(h_ready.sem, 2)
            V.memset(stat[:, 4:5], 0.0).then_inc(acc_read.sem, 4)

            def layer_norm(stage, xs, n, acc):
                dve.wait_ge(ring_free, acc)
                for t in range(TT):
                    for half in range(2):
                        c = slice(half * 512, half * 512 + 512)
                        V.scalar_tensor_tensor(work[:, t, c], x_tok[:, t, c], ALPHA, ps[:, 2 * t + half, :],
                                               ALU.mult, ALU.add).then_inc(acc_read.sem, 1)
                dve.wait_ge(ln_in, 32 * (n + 1))
                for t in range(TT):
                    dve.wait_ge(acc_read.sem, acc_read.after(stage, 2 * t + 1))
                    V.bn_stats(stat[:, 0:6], work[:, t, 0:512])
                    link(V.bn_stats(stat[:, 6:12], work[:, t, 512:1024]))
                    link(V.bn_aggr(stat[:, 12 + 2 * t:14 + 2 * t], stat[:, 0:12]))
                    V.tensor_scalar(stat[:, 16 + t:17 + t], stat[:, 13 + 2 * t:14 + 2 * t], LN_EPS, None, ALU.add
                                    ).then_inc(moments.sem, 1)
                for t in range(TT):
                    dve.wait_ge(roots.sem, roots.after(f"ln{n}", t))
                    link(V.reciprocal(stat[:, 22 + t:23 + t], stat[:, 20 + t:21 + t]))
                    link(V.scalar_tensor_tensor(work[:, t, :], work[:, t, :], stat[:, 12 + 2 * t:13 + 2 * t],
                                                ln_gb[:, 0, :], ALU.subtract, ALU.mult))
                    V.scalar_tensor_tensor(x_tok[:, t, :], work[:, t, :], stat[:, 22 + t:23 + t], ln_gb[:, 1, :],
                                           ALU.mult, ALU.add).then_inc(x_ready.sem, 1)
                dve.wait_ge(x_ready.sem, x_ready.after(xs, 1))

            def rms_scale(stage, src, dst):
                for t in range(TT):
                    dve.wait_ge(squares.sem, squares.after(stage, t))
                    V.tensor_scalar(stat[:, 16 + t:17 + t], stat[:, 24 + t:25 + t], 1.0 / D, RMS_EPS, ALU.mult,
                                    ALU.add).then_inc(moments.sem, 1)
                for t in range(TT):
                    dve.wait_ge(roots.sem, roots.after(stage, t))
                    link(V.reciprocal(stat[:, 22 + t:23 + t], stat[:, 20 + t:21 + t]))
                    ins = V.tensor_scalar(dst[:, t, :], src[:, t, :], stat[:, 22 + t:23 + t], None, ALU.mult)
                    if stage == "fin":
                        link(ins)
                        ins = V.tensor_tensor(dst[:, t, :], dst[:, t, :], ln_gb[:, 0, :], ALU.mult)
                    ins.then_inc(x_ready.sem, 1)

            def modulate(stage, src, hl, which, lo):
                g = col("norm_g", hl * 8, 8)
                link(V.tensor_scalar(mod_a[:, :, 0], mod[:, hl, 8:16, which], 1.0, None, ALU.add))
                link(V.tensor_tensor(mod_a[:, :, 1], mod_a[:, :, 0], g, ALU.mult))
                rms_scale(stage, src, work)
                for c in range(KD):
                    if c % 2 == 0:
                        dve.wait_ge(transposed.sem, transposed.after(stage, c // 2))
                    V.tensor_scalar(x_fm[:, c, lo:lo + T], ps[:, c // 2, (c % 2) * T:(c % 2 + 1) * T],
                                    mod_a[:, c, 1:2], mod[:, hl, c, which:which + 1], ALU.mult, ALU.add
                                    ).then_inc(mod_saved.sem, 1)

            def residual(stage, xs, acc, hl):
                dve.wait_ge(ring_free, acc)
                for t in range(TT):
                    for half in range(2):
                        c = slice(half * 512, half * 512 + 512)
                        V.tensor_tensor(work[:, t, c], ps[:, 2 * t + half, :], gate_row[:, hl, c], ALU.mult
                                        ).then_inc(acc_read.sem, 1)
                for t in range(TT):
                    dve.wait_ge(acc_read.sem, acc_read.after(stage, 2 * t + 1))
                    V.tensor_tensor(x_tok[:, t, :], x_tok[:, t, :], work[:, t, :], ALU.add
                                    ).then_inc(x_summed.sem, 1)
                dve.wait_ge(x_summed.sem, x_summed.after(xs, 1))

            def glu(stage, nj, e=0):
                def unit(u, n, i=0):
                    dve.wait_ge(ring_free, stream_free(stage, n + 1) + i * RING + e * 42)
                    dve.wait_ge(silu_done.sem, silu_done.after(stage, u) + i * 2 + e * 14)
                    if u >= 2:
                        dve.wait_ge(ring_free, stream_free(stage, 3 * u - 2) + i * RING + e * 42)
                    V.tensor_tensor(h_fm[:, u % 2, :, :].rearrange("p k t -> p (k t)"), silu_sb[:, u % 2, :],
                                    ps[:, 5 + 2 * (u % 2), :], ALU.mult).then_inc(h_ready.sem, 1)
                unit(0, 0)
                first = 2 + nj % 2
                for j in range(1, first):
                    unit(j, 3 * j - 1)
                with dve.Fori(0, (nj - first) // 2) as i:
                    for d in range(2):
                        unit(first + d, 3 * (first + d) - 1, i)

            dve.wait_ge(ada_ready, 1)
            V.tensor_copy(silu_cb[:, :, :], silu_c[:, :, 0:1].broadcast_to([P, KD, P])).then_inc(ada_ready, 1)
            dve.wait_ge(aux["gate_bias"], 64)
            mod_flat = mod[:, :, :, :].rearrange("p l f c -> p (l f) c")
            gate_flat = gate_row[:, :, :].rearrange("p l n -> p (l n)")
            with dve.Fori(0, 4) as i:
                for nb in range(6):
                    dve.wait_ge(ring_free, stream_free("ada", 2 * nb + 1) + i * 12)
                    if nb < 4:
                        V.tensor_tensor(mod_flat[:, bass.ds(i * 16 + nb * 4, 4), :],
                                        ps[:, nb, 0:8].rearrange("p (f c) -> p f c", c=2),
                                        cols[:, bass.ds(i * 24 + COL_AT["b_ada"] + nb * 4, 4)].unsqueeze(2)
                                        .broadcast_to([P, 4, 2]), ALU.add).then_inc(ada_saved, 1)
                    else:
                        at = bass.ds(i * D + (nb - 4) * BANK, BANK)
                        V.tensor_tensor(gate_flat[:, at], ps[:, nb, :], gate_flat[:, at], ALU.add
                                        ).then_inc(ada_saved, 1)
            dve.wait_ge(ada_saved, 30)

            dve.wait_ge(aux["ret_consts"], 32)
            cos, sin = r_rope[:, 0, :], r_rope[:, 1, :]
            for b in range(8):
                dve.wait_ge(proj_saved.sem, proj_saved.after("ret_in", b))
                if b:
                    dve.wait_ge(rope_done, b)
                ev, od = r_raw[:, b, 0, :], r_raw[:, b, 1, :]
                V.tensor_tensor(r_rot[:, b, 0, :], ev, cos, ALU.mult)
                V.tensor_tensor(r_rot[:, b, 1, :], ev, sin, ALU.mult)
                V.tensor_tensor(r_tmp[:, 0, :], od, sin, ALU.mult)
                link(V.tensor_tensor(r_tmp[:, 1, :], od, cos, ALU.mult))
                link(V.tensor_tensor(r_rot[:, b, 0, :], r_rot[:, b, 0, :], r_tmp[:, 0, :], ALU.subtract))
                V.tensor_tensor(r_rot[:, b, 1, :], r_rot[:, b, 1, :], r_tmp[:, 1, :], ALU.add
                                ).then_inc(rope_done, 1)
            dve.wait_ge(rope_done, 8)
            dve.wait_ge(proj_saved.sem, proj_saved.after("ret_in", 23))

            def group_norm(u):
                h, t = u // 2, u % 2
                bank = 1 + u % 4
                y = r_y[:, t, h * RDV:(h + 1) * RDV]
                dve.wait_ge(y_ready, u + 1)
                link(V.bn_stats(stat[:, 0:6], ps[:, bank, :]))
                link(V.bn_aggr(stat[:, 12:14], stat[:, 0:6]))
                V.tensor_scalar(stat[:, 32 + u % 2:33 + u % 2], stat[:, 13:14], LN_EPS, None, ALU.add
                                ).then_inc(y_var, 1)
                dve.wait_ge(y_root, u + 1)
                link(V.reciprocal(stat[:, 14:15], stat[:, 34 + u % 2:35 + u % 2]))
                V.tensor_scalar(y, ps[:, bank, :], stat[:, 12:13], stat[:, 14:15], ALU.subtract, ALU.mult
                                ).then_inc(y_read, 1)
                dve.wait_ge(y_read, u + 1)
                V.tensor_tensor(y, y, r_gate[:, t, h * RDV:(h + 1) * RDV], ALU.mult).then_inc(y_gated, 1)

            for h in range(RH):
                dve.wait_ge(st_ready, h + 1)
                V.tensor_tensor(r_st[:, h % 2, :], ps[:, 0, 0:384], r_decay[:, h, :], ALU.mult
                                ).then_inc(st_saved, 1)
                if h:
                    for t in range(TT):
                        group_norm(2 * (h - 1) + t)
            for t in range(TT):
                group_norm(2 * (RH - 1) + t)
            layer_norm("ret_out", "x1", 0, stream_free("ret_out", 7))
            glu("ffn0", 11)
            layer_norm("ffn0", "x2", 1, stream_free("ffn0", 32))

            dve.wait_ge(rows_ready, 1)
            V.tensor_tensor(b_rows[0:AG * AH, :], ps[0:AG * AH, 7, 0:ROWS_W], b_mask[0:AG * AH, :], ALU.add
                            ).then_inc(rows_saved, 1)

            def heads(stage, nh, hd, scores_of, pt_psum, pt_of, out_bank, dst):
                def row_max(h, it):
                    dve.wait_ge(scored.sem, scored.after(stage, 2 * h + it))
                    if h:
                        dve.wait_ge(probs.sem, probs.after(stage, 2 * (h - 1) + it))
                    link(V.reduce_max(stat[:, 44 + it:45 + it], scores_of(it), AX_X))
                    V.tensor_scalar(stat[:, 40 + it:41 + it], stat[:, 44 + it:45 + it], -1.0, None, ALU.mult
                                    ).then_inc(negmax.sem, 1)

                row_max(0, 0)
                row_max(0, 1)
                for h in range(nh):
                    for it in range(2):
                        u = 2 * h + it
                        dve.wait_ge(probs_t.sem, probs_t.after(stage, u))
                        if h:
                            dve.wait_ge(mixed.sem, mixed.after(stage, u - 2))
                        V.tensor_copy(pt_of(it), pt_psum(it)).then_inc(probs_fm.sem, 1)
                        if h + 1 < nh:
                            row_max(h + 1, it)
                    for it in range(2):
                        u = 2 * h + it
                        link(V.reciprocal(stat[:, 46 + it:47 + it], stat[:, 42 + it:43 + it]))
                        dve.wait_ge(mixed.sem, mixed.after(stage, u))
                        V.tensor_scalar(dst(h, it), ps[:, out_bank + it, 0:hd], stat[:, 46 + it:47 + it], None,
                                        ALU.mult).then_inc(head_saved.sem, 1)

            heads("att", AH, AHD, lambda it: psf[:, BANK * it:BANK * it + 384 * (it + 1)],
                  lambda it: psf[:, (3 + it) * BANK:(3 + it) * BANK + 384 * (it + 1)],
                  lambda it: a_pt[:, 384 * it:384 + 768 * it], 6,
                  lambda h, it: work[:, it, h * AHD:(h + 1) * AHD])
            layer_norm("att_out", "x3", 2, stream_free("att_out", 3))
            glu("ffn1", 11)
            layer_norm("ffn1", "x4", 3, stream_free("ffn1", 32))

            dve.wait_ge(aux["hyena_in"], 96)
            for m in range(2):
                dve.wait_ge(hy_pe, m + 1)
                arg, turns = y_arg[0:HID, 0, :], y_arg[0:HID, 1, :]
                if m:
                    dve.wait_ge(hy_act, 1)
                link(V.tensor_scalar(arg, ps[0:HID, m, 0:T], col("f_b1" if m == 0 else "f_b2", 0)[0:HID, :],
                                     col("f_freq", m)[0:HID, :], ALU.add, ALU.mult))
                link(V.tensor_scalar(turns, arg, 1.0 / (2.0 * np.pi), ROUND, ALU.mult, ALU.add))
                link(V.tensor_scalar(turns, turns, -ROUND, None, ALU.add))
                for part in (TWO_PI_HI, TWO_PI_MID, TWO_PI_LO):
                    link(V.scalar_tensor_tensor(arg, turns, -float(part), arg, ALU.mult, ALU.add))
                V.tensor_scalar(arg, arg, 3.1415925, -3.1415925, ALU.min, ALU.max).then_inc(hy_dve, 1)
            for n in range(4):
                for t in range(TT):
                    dve.wait_ge(hy_pe, 3 + 2 * n + t)
                    V.tensor_tensor(y_h[:, t, n, :], ps[:, (2 * n + t + 2) % 8, :], y_win[:, n % 2, t, :], ALU.mult
                                    ).then_inc(hy_dve, 1)
            for o in range(2):
                dve.wait_ge(hy_pe, 11 + o)
                link(V.tensor_scalar(y_rn[:, o, :], ps[:, 2 + o, :], RMS_EPS, None, ALU.add))
                V.reciprocal(y_rn[:, o, :], y_rn[:, o, :]).then_inc(hy_dve, 1)
            dve.wait_ge(hy_pe, 12)
            for o in range(2):
                V.tensor_tensor(y_abs[:, :, 2 * o, :], y_h[:, :, 2 * o, :], y_h[:, :, 2 * o + 1, :], ALU.add)
                V.tensor_tensor(y_abs[:, :, 2 * o + 1, :], y_h[:, :, 2 * o, :], y_h[:, :, 2 * o + 1, :],
                                ALU.subtract).then_inc(hy_dve, 1)
            for o in range(2):
                dve.wait_ge(hy_pe, 13 + o)
                for part in range(2):
                    for f in range(2):
                        ins = V.tensor_tensor(y_k[:, o, part, f, :], ps[:, 4 * (o % 2) + 2 * part + f, :],
                                              y_rn[:, o, :], ALU.mult)
                ins.then_inc(hy_dve, 1)

            link(V.memset(stat[:, 0:1], 0.0))
            V.memset(stat[:, 1:2], 0.0).then_inc(hy_dve, 1)
            modulate("m0", x_tok, 0, 0, 0)
            modulate("mc", ctx_tok, 0, 1, T)
            dve.wait_ge(mod_saved.sem, mod_saved.after("mc", 7))
            for c in range(12):
                dve.wait_ge(proj_saved.sem, proj_saved.after("w_in", c // 2))
                wc = [col("short_w", 3 * c + j) for j in range(3)]
                link(V.tensor_scalar(z[:, c, :], z_raw[:, c, :], wc[1], col("short_b", c), ALU.mult, ALU.add))
                link(V.scalar_tensor_tensor(z[:, c, 1:T], z_raw[:, c, 0:T - 1], wc[0], z[:, c, 1:T],
                                            ALU.mult, ALU.add))
                V.scalar_tensor_tensor(z[:, c, 0:T - 1], z_raw[:, c, 1:T], wc[2], z[:, c, 0:T - 1],
                                       ALU.mult, ALU.add).then_inc(short_done, 1)
            dve.wait_ge(short_done, 12)
            w_flat = work[:, :, :].rearrange("p t n -> p (t n)")
            for o in range(2):
                dve.wait_ge(conv_f, o + 1)
                u_re, u_im = psf[:, 4 * BANK:6 * BANK], psf[:, 6 * BANK:8 * BANK]
                k_re = y_k[:, o, 0, :, :].rearrange("p f c -> p (f c)")
                k_im = y_k[:, o, 1, :, :].rearrange("p f c -> p (f c)")
                v_re = z_y[:, 0, :, :].rearrange("p f c -> p (f c)")
                v_im = z_y[:, 1, :, :].rearrange("p f c -> p (f c)")
                V.tensor_tensor(v_re, u_re, k_re, ALU.mult)
                V.tensor_tensor(w_flat[:, 0:D], u_im, k_im, ALU.mult)
                V.tensor_tensor(v_im, u_re, k_im, ALU.mult)
                link(V.tensor_tensor(w_flat[:, D:2 * D], u_im, k_re, ALU.mult))
                V.tensor_tensor(v_re, v_re, w_flat[:, 0:D], ALU.subtract)
                V.tensor_tensor(v_im, v_im, w_flat[:, D:2 * D], ALU.add).then_inc(conv_y, 1)
                for c in range(4):
                    if c % 2 == 0:
                        dve.wait_ge(conv_t, 2 * o + c // 2 + 1)
                    dst = z[:, c, :] if o == 0 else x_fm[:, c, 0:T]
                    link(V.scalar_tensor_tensor(z[:, c, :], z[:, c, :], col("skip", 4 * o + c),
                                                ps[:, 2 + c // 2, (c % 2) * T:(c % 2 + 1) * T], ALU.mult, ALU.add))
                    V.tensor_tensor(dst, z[:, c, :], z[:, 4 + 4 * o + c, :], ALU.mult).then_inc(conv_out, 1)
                dve.wait_ge(conv_out, 4 * o + 4)
            heads("nat", NH, NHD, lambda it: ps[:, it, :], lambda it: ps[:, 2 + it, :], lambda it: n_pt[:, it, :], 4,
                  lambda h, it: work[:, it, h * NHD:(h + 1) * NHD])
            residual("mix_out", "mix", stream_free("mix_out", 3), 0)
            modulate("m1", x_tok, 1, 0, 0)
            glu("ffn2", 11)
            residual("ffn2", "ffn2", stream_free("ffn2", 32), 1)
            modulate("m2", x_tok, 2, 0, 0)
            residual("fourier", "fourier", stream_free("fourier", 3), 2)
            modulate("m3", x_tok, 3, 0, 0)

            dve.wait_ge(routed, 1)
            for t in range(TT):
                link(V.tensor_tensor(route[:, t, 0, :], ps[:, 4 + t, 0:EXPERTS], router_b[:, :], ALU.add))
            link(V.memset(pairs[:, 1, :, :], 0.0))
            for e in range(1, EXPERTS):
                ins = V.memset(pairs[:, 1, e, 0:e], 1.0)
            link(ins)
            for t in range(TT):
                lf = route[:, t, 0, :].unsqueeze(1).broadcast_to([P, EXPERTS, EXPERTS])
                le = route[:, t, 0, :].unsqueeze(2).broadcast_to([P, EXPERTS, EXPERTS])
                link(V.tensor_tensor(pairs[:, 0, :, :], lf, le, ALU.is_equal))
                link(V.tensor_tensor(pairs[:, 0, :, :], pairs[:, 0, :, :], pairs[:, 1, :, :], ALU.mult))
                link(V.reduce_sum(route[:, t, 1, :], pairs[:, 0, :, :], AX_X))
                link(V.tensor_tensor(pairs[:, 0, :, :], lf, le, ALU.is_gt))
                link(V.reduce_sum(route[:, t, 2, :], pairs[:, 0, :, :], AX_X))
                link(V.tensor_tensor(route[:, t, 1, :], route[:, t, 1, :], route[:, t, 2, :], ALU.add))
                link(V.tensor_scalar(route[:, t, 2, :], route[:, t, 1, :], 0.0, None, ALU.is_equal))
                link(V.tensor_scalar(route[:, t, 3, :], route[:, t, 1, :], 1.0, None, ALU.is_equal))
                link(V.tensor_tensor(pairs[:, 0, 0, :], route[:, t, 2, :], route[:, t, 0, :], ALU.mult))
                link(V.reduce_sum(stat[:, 52:53], pairs[:, 0, 0, :], AX_X))
                link(V.tensor_tensor(pairs[:, 0, 0, :], route[:, t, 3, :], route[:, t, 0, :], ALU.mult))
                link(V.reduce_sum(stat[:, 53:54], pairs[:, 0, 0, :], AX_X))
                ins = V.tensor_tensor(stat[:, 48 + t:49 + t], stat[:, 53:54], stat[:, 52:53], ALU.subtract)
                if t == 0:
                    link(ins)
            ins.then_inc(route_var, 1)
            dve.wait_ge(route_exp, 1)
            link(V.tensor_scalar(stat[:, 54:56], stat[:, 50:52], 1.0, None, ALU.add))
            link(V.reciprocal(stat[:, 56:58], stat[:, 54:56]))
            link(V.tensor_tensor(stat[:, 58:60], stat[:, 50:52], stat[:, 56:58], ALU.mult))
            link(V.memset(m_acc, 0.0))
            for t in range(TT):
                link(V.tensor_scalar(gates[:, t, :], route[:, t, 2, :], stat[:, 56 + t:57 + t], None, ALU.mult))
                ins = V.scalar_tensor_tensor(gates[:, t, :], route[:, t, 3, :], stat[:, 58 + t:59 + t], gates[:, t, :],
                                             ALU.mult, ALU.add)
                if t == 0:
                    link(ins)
            ins.then_inc(gates_ready, 1)
            dve.wait_ge(gates_ready, 1)
            gates_flat = gates[:, :, :].rearrange("p t e -> p (t e)")
            with dve.Fori(0, EXPERTS) as e:
                glu("moe", 14, e)
                dve.wait_ge(ring_free, stream_free("moe", 41) + e * 42)
                for t in range(TT):
                    for half in range(2):
                        c = slice(half * 512, half * 512 + 512)
                        dve.wait_ge(acc_read.sem, acc_read.base["moe"] + 2 * t + half - 3 + e * 4)
                        V.scalar_tensor_tensor(m_acc[:, t, c], ps[:, 2 * t + half, :],
                                               gates_flat[:, bass.ds(e + t * EXPERTS, 1)], m_acc[:, t, c],
                                               ALU.mult, ALU.add).then_inc(acc_read.sem, 1)
            for t in range(TT):
                dve.wait_ge(acc_read.sem, acc_read.after("moe", 4 * EXPERTS - 1))
                link(V.tensor_tensor(work[:, t, :], m_acc[:, t, :], gate_row[:, 3, :], ALU.mult))
                V.tensor_tensor(x_tok[:, t, :], x_tok[:, t, :], work[:, t, :], ALU.add).then_inc(x_summed.sem, 1)
            dve.wait_ge(ln_in, 32 * 4 + 16)
            rms_scale("fin", x_tok, work)


PROJ_BASE = {"ret_in": 0, "att_in": 24, "w_in": 60, "four_a": 76, "four_y": 84}


def constants():
    f32 = np.float32
    k = {}
    k["squares"] = np.stack([np.eye(P), np.eye(P)[::-1], np.ones((P, P))], 1).astype(f32)
    inv = f32(1.0) / np.power(f32(10000.0), np.linspace(0.0, 1.0, RDK // 2, dtype=f32))
    ang = (np.arange(T, dtype=f32)[:, None] * inv[None, :]).astype(f32).astype(np.float64)
    k["rope"] = np.stack([np.cos(ang).T, np.sin(ang).T], 1).astype(f32)
    lg = np.log(1.0 - 2.0 ** (-5.0 - np.arange(RH)))
    j, i = np.arange(T)[:, None], np.arange(T)[None, :]
    dec = np.where(i >= j, np.exp(np.maximum(i - j, 0)[None] * lg[:, None, None]), 0.0) * RDK ** -0.5
    k["decay"] = np.concatenate([dec[:, 0:P, :], dec[:, P:T, P:T]], 2).transpose(1, 0, 2).astype(f32)
    dist = 255 - np.arange(ROWS_W)
    exact = BUCKETS // 2
    big = exact + (np.log(np.maximum(dist, 1).astype(f32) / f32(exact)) / f32(np.log(MAX_DIST / exact))
                   * f32(BUCKETS - exact)).astype(np.int32)
    bucket = np.where(dist < exact, dist, np.minimum(big, BUCKETS - 1))
    k["bucket_hot"] = ((bucket[None, :] == np.arange(BUCKETS)[:, None]) & (dist >= 0)[None, :]).astype(f32)
    rows = [np.where((dist >= 0) & (dist % dil == 0) & (dist <= win), 0.0, NEG) for win, dil in DILATIONS]
    k["rel_mask"] = np.repeat(np.stack(rows), AH, 0).astype(f32)
    t = np.linspace(0.0, 1.0, T, dtype=f32)[:, None]
    bands = np.linspace(1e-4, (EMB - 1) // 2 - 1, (EMB - 1) // 2, dtype=f32)
    ang = (f32(2.0 * np.pi / T) * np.arange(T, dtype=f32)[:, None] * bands[None, :]).astype(f32)
    k["features"] = np.concatenate([t, np.cos(ang), -np.sin(ang)], 1).T.astype(f32)
    deltas = np.abs(np.linspace(np.log(1e-2) / 1.5, np.log(1e-2) / 0.3, HC, dtype=f32))
    win = np.exp(-t * deltas[None, :]).astype(f32)
    later = win.copy()
    later[0] = 0.0
    k["window"] = np.stack([win, later]).reshape(2, TT, P, HC).transpose(2, 0, 1, 3)
    w = 2.0 * np.pi * (np.arange(T) + 0.5)[None, :] * np.arange(T)[:, None] / (2 * T)
    dft = [np.cos(w), np.sin(w), np.cos(w).T / T, np.sin(w).T / T]
    k["dft"] = np.stack(dft).reshape(4, TT, P, T).transpose(2, 0, 1, 3).astype(f32)
    c = 63 - np.arange(P) % 64
    start = np.clip(c - WIN_C // 2, 0, GRID_W - WIN_C)[:, None]
    cc = np.arange(GRID_W)[None, :]
    mask = np.where((cc >= start) & (cc < start + WIN_C), 0.0, NEG)
    k["window_mask"] = np.tile(mask, (1, 6)).astype(f32)
    w = 2.0 * np.pi * ((np.arange(T)[:, None] * np.arange(T)[None, :]) % T) / T
    cs = np.concatenate([np.cos(w), np.sin(w)], 1).reshape(2, P, 512)
    cl = np.concatenate([np.cos(w), -np.sin(w)], 1).reshape(2, P, 512)
    k["fourier"] = (np.concatenate([cs, cl], 0).transpose(1, 0, 2) / 16.0).astype(f32)
    return {n: np.ascontiguousarray(v, dtype=f32) for n, v in k.items()}


def by_partition(v, parts=P):
    v = v.reshape(-1, parts)
    return v.T


def kernel(**inputs):
    import numpy as _np
    import concourse.bacc as _bacc
    from concourse import mybir as _mybir
    from concourse.bass_utils import run_bass_kernel_spmd as _run

    x = {n: _np.asarray(v) for n, v in inputs.items()}

    def padded(v):
        o = _np.zeros((P, v.shape[1]), v.dtype)
        o[0:v.shape[0]] = v
        return o

    c2 = _np.stack([x["c_2"].reshape(-1), x["c_ctx_2"].reshape(-1)])
    parts = {
        "c": c2.reshape(2, KD, P).transpose(2, 1, 0).reshape(P, 16),
        "b_ada": by_partition(x["b_ada_2"]),
        "norm_g": by_partition(x["norm_g_2"]),
        "short_w": x["hy_short_w_2"][0].reshape(3, 12, P).transpose(2, 1, 0).reshape(P, 36),
        "short_b": by_partition(x["hy_short_b_2"]),
        "skip": by_partition(x["hy_skip_2"]),
        "f_b1": padded(x["hy_f_b1_2"].reshape(HID, 1)),
        "f_b2": padded(x["hy_f_b2_2"].reshape(HID, 1)),
        "f_freq": padded(x["hy_f_freq_2"][0].T),
    }
    arrays = dict(constants())
    arrays["cols"] = _np.concatenate([parts[n] for n, _ in COLS], 1)
    arrays["rel_bias"] = _np.ascontiguousarray(x["rel_bias"].T)
    arrays["x"] = x["x"][0]
    arrays["ctx_2"] = x["ctx_2"][0]
    for n in ("ret_w_in", "ret_w_out", "attn_w_in", "attn_w_out", "w_in_2", "w_mix_out_2", "ffn_w1_2", "ffn_w3_2",
              "ffn_w2_2", "w_fourier_2", "w_router_2", "b_router_2", "moe_w1_2", "moe_w3_2", "moe_w2_2",
              "hy_f_w1_2", "hy_f_w2_2", "hy_f_w3_2", "na_rpb_2"):
        arrays[n] = x[n][0]
    for n in ("ffn_w_up", "ffn_w_down", "ln_gain", "ln_bias", "w_ada_2", "b_ada_2", "final_g_2"):
        arrays[n] = x[n]
    arrays = {n: _np.ascontiguousarray(v) for n, v in arrays.items()}

    nc = _bacc.Bacc("TRN2", target_bir_lowering=False, num_devices=1)
    ins = {n: nc.dram_tensor(f"in_{n}", v.shape, _mybir.dt.float32, kind="ExternalInput").ap()
           for n, v in arrays.items()}
    out = nc.dram_tensor("out", (T, D), _mybir.dt.float32, kind="ExternalOutput").ap()
    build(nc, ins, out)
    r = _run(nc, [{f"in_{n}": v for n, v in arrays.items()}], core_ids=[0])
    return r.results[0]["out"].reshape(1, T, D)
```

```python
from contextlib import ExitStack

import numpy as np

import concourse.bass as bass
from concourse import mybir

F32 = mybir.dt.float32
ALU = mybir.AluOpType
ACT = mybir.ActivationFunctionType
AX_X = mybir.AxisListType.X

P = 128
T = 256
TT = T // P
D = 1024
KD = D // P
RING = 3
RING_E = 6
SPLIT = 4
HALF = 1024
AHEAD = 2
ITEMS = 12
SLOT = 2048
BANK = 512
NEG = -1.0e30

RH, RDK, RDV = 4, 256, 512
AG, AH, AHD = 3, 16, 64
BUCKETS, MAX_DIST = 32, 2048
ROWS_W = 384
DILATIONS = ((128, 1), (512, 4), (2048, 16))
HC = 512
NH, NHD = 16, 32
WIN_R, WIN_C, GRID_W = 8, 16, 64
HID, EMB = 64, 33
FFN = 2816
EXPERTS, FEXP = 8, 3584
ALPHA = 4.0 ** 0.25
LN_EPS = 1e-5
RMS_EPS = 1e-6
ROUND = 1.5 * 2.0 ** 23
TWO_PI_HI = 6.28125
TWO_PI_MID = 0.0019350051879882812
TWO_PI_LO = 2.0 * np.pi - TWO_PI_HI - TWO_PI_MID

STREAM = [("ret_in", 24), ("ret_out", 8), ("ffn0", 33), ("att_in", 36), ("att_out", 4),
          ("ffn1", 33), ("w_in", 12), ("mix_out", 4), ("ffn2", 33), ("fourier", 4), ("moe", EXPERTS * 42)]
FIRST_BLOCK = {}
_n = 0
for _name, _count in STREAM:
    FIRST_BLOCK[_name] = _n
    _n += _count
ADA_SLOTS = 3
SLOT_OF, LANDING = [], []
_seen = [0] * RING_E
for _b in range(FIRST_BLOCK["moe"] + 42 + AHEAD):
    _s = _b % RING if _b < FIRST_BLOCK["moe"] else (_b - FIRST_BLOCK["moe"]) % RING_E
    _seen[_s] += 16
    SLOT_OF.append(_s)
    LANDING.append(_seen[_s])

COLS = [("c", 16), ("b_ada", 96), ("norm_g", 32), ("short_w", 36), ("short_b", 12), ("skip", 8),
        ("f_b1", 1), ("f_b2", 1), ("f_freq", 2)]
COL_AT = {}
_n = 0
for _name, _count in COLS:
    COL_AT[_name] = _n
    _n += _count
N_COLS = _n


class At:

    def __init__(self, i=None, e=None):
        self.i, self.e = i, e

    def plus(self, value, per_i, per_e=0):
        if self.i is not None:
            value = value + self.i * per_i
        if self.e is not None:
            value = value + self.e * per_e
        return value


HERE = At()


class Signal:

    def __init__(self, sem, stages, credits=0):
        self.sem = sem
        self.base = {}
        total = credits
        for name, count in stages:
            self.base[name] = total
            total += count

    def after(self, stage, k=0):
        return self.base[stage] + k + 1


def build(nc, a, out):
    ctx = ExitStack()
    with ctx:
        def sb(name, shape, dt=F32):
            return ctx.enter_context(nc.sbuf_tensor(name, shape, dt))

        def sem(name):
            return ctx.enter_context(nc.semaphore(name))

        FR = mybir.dt.float32r
        raw3 = sb("raw3", [P, RING, SLOT])
        w_hi = sb("w_hi", [P, SPLIT, HALF], FR)
        w_lo = sb("w_lo", [P, SPLIT, HALF], FR)
        x_hi = sb("x_hi", [P, KD, T], FR)
        x_lo = sb("x_lo", [P, KD, T], FR)
        h_hi = sb("h_hi", [P, KD, T], FR)
        h_lo = sb("h_lo", [P, KD, T], FR)
        x_tok = sb("x_tok", [P, TT, D])
        work = sb("work", [P, TT, D])
        hid = sb("hid", [P, 2304])
        silu_sb = hid[:, 0:1024].rearrange("p (t n) -> p t n", t=2)
        h_tok = hid[:, 1024:2048].rearrange("p (t n) -> p t n", t=2)
        ln_gb = sb("ln_gb", [P, 2, D])
        sq = sb("sq", [P, 5, P])
        cols = sb("cols", [P, N_COLS])
        silu_c = sb("silu_c", [P, KD, 2])
        mod = sb("mod", [P, 4, 24, 2])
        mod_a = sb("mod_a", [P, KD, 2])
        stat = sb("stat", [P, 64])
        router_w = sb("router_w", [P, KD, EXPERTS])
        router_b = sb("router_b", [P, EXPERTS])
        router_hi = sb("router_hi", [P, KD, EXPERTS], FR)
        router_lo = sb("router_lo", [P, KD, EXPERTS], FR)
        route = sb("route", [P, TT, 4, EXPERTS])
        over = sb("over", [P, 4, EXPERTS])
        item_pos = sb("item_pos", [P, TT, ITEMS])
        item_gate = sb("item_gate", [P, TT, ITEMS])
        table_f = sb("table_f", [P, ITEMS])
        table = sb("table", [P, ITEMS], mybir.dt.int32)
        pairs = sb("pairs", [P, 2, EXPERTS, EXPERTS])
        gates = sb("gates", [P, TT, EXPERTS])
        BIG = 20032
        big = sb("big", [P, BIG])
        ps = ctx.enter_context(nc.psum_tensor("ps", [P, 8, BANK], F32))
        ident, rev, ones, tri, iota = (sq[:, i, :] for i in range(5))
        psf = ps[:, :, :].rearrange("p b n -> p (b n)")

        def carve(at, *shape):
            n = int(np.prod(shape))
            assert at + n <= BIG
            v = big[:, at:at + n]
            if len(shape) == 1:
                return v
            names = "abcd"[:len(shape)]
            kw = {k: s for k, s in zip(names[1:], shape[1:])}
            return v.rearrange(f"p ({' '.join(names)}) -> p {' '.join(names)}", **kw)

        def col(name, i, n=1):
            return cols[:, COL_AT[name] + i:COL_AT[name] + i + n]

        r_raw = carve(0, 8, 2, T)
        r_rot = carve(4096, 8, 2, T)
        r_v = carve(8192, TT, RH * RDV)
        r_gate = carve(12288, TT, RH * RDV)
        r_decay = carve(16384, RH, 384)
        r_rope = carve(17920, 2, T)
        r_st = carve(18432, 2, 384)
        r_tmp = carve(19200, 2, T)
        r_y = carve(0, TT, RH * RDV)
        ada_raw = carve(8192, ADA_SLOTS, SLOT)
        ada_rows = carve(0, 3 * D)

        def ada_acc(hl, bank):
            return carve((0 if hl == 2 else 4096) + bank * BANK, BANK)

        a_q = carve(0, 24, T)
        a_k = carve(6144, 24, T)
        a_v = carve(12288, TT, AG * D)
        a_p = hid[:, 0:1152]
        a_pt = hid[:, 1152:2304]
        a_bias = carve(18432, 2, AG, T)
        b_hot = carve(0, 384)
        b_tab = carve(384, 48)
        b_mask = carve(512, ROWS_W)
        b_rows = carve(1024, ROWS_W)
        y_k = carve(0, 2, 2, 2, HC)
        y_dft = carve(4096, 4, 2, T)
        y_win = carve(6144, 2, 2, HC)
        y_h = carve(8192, TT, 4, HC)
        y_abs = carve(12288, TT, 4, HC)
        y_w3 = carve(16384, 4, HC)
        y_w12 = carve(18432, 2, HID)
        y_feat = carve(18560, T)
        y_arg = carve(18816, 4, T)
        y_rn = hid[:, 0:D].rearrange("p (o c) -> p o c", o=2)
        z_raw = carve(6144, 12, T)
        z_u = carve(6144, TT, HC)
        z_y = carve(7168, 2, 2, HC)
        z = carve(9216, 12, T)
        n_q = carve(12288, 4, T)
        n_k = carve(13312, 4, 2 * T)
        n_v = carve(15360, 4, HC)
        ctx_tok = carve(17984, TT, D)
        n_p = hid[:, 0:1024].rearrange("p (t n) -> p t n", t=2)
        n_pt = hid[:, 1024:2048].rearrange("p (t n) -> p t n", t=2)
        n_bias = carve(17408, 2, 384)
        n_mask = carve(18176, 384)
        f_cs = carve(0, 4, BANK)
        f_a = carve(2048, TT, 4, BANK)
        f_x = carve(6144, KD, T)
        mod_tmp = hid[:, 0:2048].rearrange("p (k t) -> p k t", k=KD)
        m_acc = carve(0, TT, D)
        m_yc = carve(2048, D)
        m_sel = carve(3072, TT, P)
        m_selg = carve(3328, TT, P)
        m_selt = carve(3584, T)
        m_x = carve(4096, KD, P)
        m_raw = carve(12288, RING_E - RING, SLOT)

        def raw(s):
            return raw3[:, s, :] if s < RING else m_raw[:, s - RING, :]

        gates_dram = nc.dram_tensor("gate_rows", [1, 4 * D], F32, kind="Internal").ap()
        rows_dram = nc.dram_tensor("bias_rows", [AG * AH, ROWS_W], F32, kind="Internal").ap()

        landed = [sem(f"landed{s}") for s in range(RING_E)]
        ada_in = [sem(f"ada_in{s}") for s in range(ADA_SLOTS)]
        ada_first = [sem(f"ada_first{s}") for s in range(ADA_SLOTS)]
        ada_used = sem("ada_used")
        ada_step = sem("ada_step")
        ada_turned = sem("ada_turned")
        hi_ready = sem("hi_ready")
        split_ready = sem("split_ready")
        split_free = sem("split_free")
        consts_in = sem("consts_in")
        x_in = sem("x_in")
        aux_names = ["gates_out", "router", "ret_consts", "bias_consts", "rows_out", "hyena_in", "ctx_in",
                     "n_mask", "fourier_in"]
        aux = {n: sem(f"in_{n}") for n in aux_names}
        bias_in = [sem(f"bias_in{i}") for i in range(2)]
        ln_in = sem("ln_in")
        out_done = sem("out_done")

        TR = [("x0", 4), ("ret0", 4), ("ret1", 4), ("x1", 4), ("x2", 4), ("att", 4), ("x3", 4), ("m0", 4), ("mc", 4),
              ("vtok", 2), ("ytok", 2), ("nat", 2), ("m1", 4), ("m2", 4), ("m3", 4)]
        CUT = [("x0", 4), ("ret0", 4), ("ret1", 4), ("x1", 4), ("x2", 4), ("att", 4), ("x3", 4), ("m0", 4),
               ("mc", 4), ("hy", 4), ("nat", 2), ("m1", 4), ("m3", 4)]
        transposed = Signal(sem("transposed"), TR)
        fm_hi = Signal(sem("fm_hi"), CUT)
        fm_saved = Signal(sem("fm_saved"), CUT)
        modulated = Signal(sem("modulated"), [(m, 4) for m in ("m0", "mc", "m1", "m2", "m3")])
        NORMS = ["ln0", "ln1", "ln2", "ln3", "m0", "mc", "m1", "m2", "m3", "fin"]
        moments = Signal(sem("moments"), [(n, 2) for n in NORMS])
        roots = Signal(sem("roots"), [(n, 2) for n in NORMS])
        squares = Signal(sem("squares"), [(n, 2) for n in NORMS[4:]])
        x_ready = Signal(sem("x_ready"), [("x1", 2), ("x2", 2), ("x3", 2), ("x4", 2)] +
                         [(n, 2) for n in NORMS[4:]])
        x_summed = Signal(sem("x_summed"), [(n, 2) for n in ("mix", "ffn2", "fourier", "moe")])
        acc_read = Signal(sem("acc_read"), [(n, 4) for n in
                          ("ret_out", "ffn0", "att_out", "ffn1", "mix_out", "ffn2", "fourier")] +
                          [], credits=4)
        PROJ = [("ret_in", 24), ("att_in", 36), ("w_in", 16), ("four_a", 8), ("four_y", 4)]
        proj_saved = Signal(sem("proj_saved"), PROJ, credits=6)
        banked = Signal(sem("banked"), [("four_a", 8), ("four_y", 4)])
        four_hi = sem("four_hi")
        GLU = [("ffn0", 6), ("ffn1", 6), ("ffn2", 6), ("moe", 7)]
        silu_done = Signal(sem("silu_done"), GLU, credits=1)
        h_ready = Signal(sem("h_ready"), GLU)
        h_turned = Signal(sem("h_turned"), GLU)
        h_high = Signal(sem("h_high"), GLU)
        h_cut = Signal(sem("h_cut"), GLU, credits=1)
        table_ready, ranked = sem("table_ready"), sem("ranked")
        sel_ready = sem("sel_ready")
        gathered = sem("gathered")
        m_x_ready = sem("m_x_ready")
        m_x_scaled = sem("m_x_scaled")
        m_x_high = sem("m_x_high")
        m_x_cut = sem("m_x_cut")
        sel_turned = sem("sel_turned")
        yc_ready = sem("yc_ready")
        scattered = sem("scattered")
        shares_added = sem("shares_added")
        ada_ready = sem("ada_ready")
        ada_saved = sem("ada_saved")
        rope_done = sem("rope_done")
        st_ready, st_saved, y_ready = sem("st_ready"), sem("st_saved"), sem("y_ready")
        y_var, y_root, y_read, y_gated = sem("y_var"), sem("y_root"), sem("y_read"), sem("y_gated")
        rows_ready, rows_saved = sem("rows_ready"), sem("rows_saved")
        HEADS = [("att", 2 * AH), ("nat", 2 * NH)]
        scored = Signal(sem("scored"), HEADS)
        negmax = Signal(sem("negmax"), HEADS)
        probs = Signal(sem("probs"), HEADS)
        probs_t = Signal(sem("probs_t"), HEADS)
        probs_fm = Signal(sem("probs_fm"), HEADS)
        mixed = Signal(sem("mixed"), HEADS)
        head_saved = Signal(sem("head_saved"), HEADS)
        masked = sem("masked")
        hy_pe, hy_dve, hy_act = sem("hy_pe"), sem("hy_dve"), sem("hy_act")
        tok_saved = sem("tok_saved")
        router_cut = sem("router_cut")
        selg_ready = sem("selg_ready")
        conv_f, conv_y, conv_t, conv_out = sem("conv_f"), sem("conv_y"), sem("conv_t"), sem("conv_out")
        short_done = sem("short_done")
        routed, route_exp = sem("routed"), sem("route_exp")
        route_var = sem("route_var")
        dve_step, act_step = sem("dve_step"), sem("act_step")

        def used(stage, n):
            return SPLIT + 2 * (FIRST_BLOCK[stage] + n) + 2

        block = ctx.enter_context(nc.Block())

        @block.sync
        def _(sp):
            def load(stage, n, src, at=HERE):
                b = FIRST_BLOCK[stage] + n
                if b < RING:
                    pass
                elif b < FIRST_BLOCK["moe"]:
                    sp.wait_ge(split_ready, at.plus(2 * (b - RING) + 2, 12))
                elif n < RING_E and at.e is None:
                    sp.wait_ge(split_ready, 2 * (b - n))
                    if n == 0:
                        sp.wait_ge(x_ready.sem, x_ready.after("m2", 1))
                else:
                    sp.wait_ge(split_ready, at.plus(2 * (b - RING_E) + 2, 12, 84))
                k = src.shape[1]
                sp.dma_start(raw(SLOT_OF[b]).rearrange("p (k w) -> p k w", k=k), src
                             ).then_inc(landed[SLOT_OF[b]], 16)

            def wide(w, c0, half):
                return w.rearrange("(k p) n -> p k n", p=P)[:, 4 * half:4 * half + 4, bass.ds(c0, 512)]

            def narrow(w, c0):
                return w.rearrange("(k p) n -> p k n", p=P)[:, :, bass.ds(c0, 256)]

            def down(w, k0):
                return w.rearrange("(k p) n -> p k n", p=P)[:, bass.ds(k0, 2), :]

            def load_glu(stage, units, odd, gate, up, dn, at=HERE):
                def unit(j, n, at):
                    for m, half in ((gate, 0), (gate, 1), (up, 0), (up, 1)):
                        load(stage, n, m(j, half), at)
                        n += 1
                    return n

                n = unit(0, 0, at)
                n = unit(1, n, at)
                for half in range(2):
                    load(stage, n + half, dn(half), at)
                with sp.Fori(0, units - 2) as i:
                    here = At(i, at.e)
                    n = unit(i + 2, 10, here)
                    for half in range(2):
                        load(stage, n + half, dn((i + 1) * 2 + half), here)
                n = 10 + 6 * (units - 2)
                if odd:
                    load(stage, n, odd[0], at)
                    load(stage, n + 1, odd[1], at)
                    n += 2
                for half in range(2):
                    load(stage, n + half, dn(2 * (units - 1) + half), at)
                if odd:
                    load(stage, n + 2, odd[2], at)

            ada = a["w_ada_2"].rearrange("l (k p) n -> p l k n", p=P)
            for b in range(12):
                if b >= ADA_SLOTS:
                    sp.wait_ge(ada_used, b - ADA_SLOTS + 1)
                sp.dma_start(ada_raw[:, b % ADA_SLOTS, :].rearrange("p (k w) -> p k w", k=4),
                             ada[:, 0, 4 * (b % 2):4 * (b % 2) + 4, (b // 2) * BANK:(b // 2 + 1) * BANK]
                             ).then_inc(ada_first[b % ADA_SLOTS], 16)
            for b in range(8):
                load("ret_in", b, narrow(a["ret_w_in"], b * 256))
            for b in range(16):
                load("ret_in", 8 + b, wide(a["ret_w_in"], 2048 + (b // 2) * 512, b % 2))
            for b in range(8):
                load("ret_out", b, down(a["ret_w_out"], 2 * b))

            def ffn(stage, layer):
                up = a["ffn_w_up"][layer, :, :]
                dn = a["ffn_w_down"][layer, :, :]
                load_glu(stage, 5, (narrow(up, 2560), narrow(up, FFN + 2560), down(dn, 20)),
                         lambda j, half: wide(up, j * 512, half), lambda j, half: wide(up, j * 512 + FFN, half),
                         lambda k: down(dn, k * 2))

            ffn("ffn0", 0)
            with sp.Fori(0, 4) as i:
                for b in range(6):
                    load("att_in", b, narrow(a["attn_w_in"], i * 1536 + b * 256), At(i))
            with sp.Fori(0, 2) as i:
                for b in range(6):
                    load("att_in", 24 + b, wide(a["attn_w_in"], i * 1536 + (6144 + (b // 2) * 512), b % 2), At(i))
            for b in range(4):
                load("att_out", b, down(a["attn_w_out"], 2 * b))
            ffn("ffn1", 1)
            for b in range(10):
                load("w_in", b, narrow(a["w_in_2"], b * 256))
            for b in range(2):
                load("w_in", 10 + b, wide(a["w_in_2"], 2560, b))
            for b in range(4):
                load("mix_out", b, down(a["w_mix_out_2"], 2 * b))
            load_glu("ffn2", 5, (narrow(a["ffn_w1_2"], 2560), narrow(a["ffn_w3_2"], 2560), down(a["ffn_w2_2"], 20)),
                     lambda j, half: wide(a["ffn_w1_2"], j * 512, half),
                     lambda j, half: wide(a["ffn_w3_2"], j * 512, half), lambda k: down(a["ffn_w2_2"], k * 2))
            for b in range(4):
                load("fourier", b, down(a["w_fourier_2"], 2 * b))
            w1 = a["moe_w1_2"].rearrange("e (k p) n -> p (e k) n", p=P)
            w3 = a["moe_w3_2"].rearrange("e (k p) n -> p (e k) n", p=P)
            w2 = a["moe_w2_2"].rearrange("e (k p) n -> p (e k) n", p=P)

            def load_item(x, at):
                load_glu("moe", 7, None,
                         lambda j, half: w1[:, bass.ds(x * 8 + 4 * half, 4), bass.ds(j * 512, 512)],
                         lambda j, half: w3[:, bass.ds(x * 8 + 4 * half, 4), bass.ds(j * 512, 512)],
                         lambda k: w2[:, bass.ds(x * 28 + k * 2, 2), :], at)

            load_item(0, HERE)
            sp.wait_ge(table_ready, 1)
            count = sp.value_load(table[0:1, ITEMS - 1:ITEMS], min_val=EXPERTS, max_val=ITEMS - 1)
            with sp.Fori(1, count) as e:
                x = sp.value_load(table[0:1, bass.ds(e, 1)], min_val=0, max_val=EXPERTS - 1)
                load_item(x, At(None, e))
            for b in range(AHEAD):
                sp.wait_ge(split_ready, count * 84 + (2 * (FIRST_BLOCK["moe"] + b - RING_E) + 2))
                sp.dma_start(raw(b).rearrange("p (k w) -> p k w", k=4), w1[:, 0:4, 0:512]).then_inc(landed[b], 16)
            for t in range(TT):
                sp.wait_ge(x_ready.sem, x_ready.after("fin", t))
                sp.dma_start(out[t * P:(t + 1) * P, :], work[:, t, :]).then_inc(out_done, 16)
            sp.wait_ge(out_done, 16 * TT)

        @block.gpsimd
        def _(pool):
            pool.dma_start(sq[:, :, :], a["squares"]).then_inc(consts_in, 16)
            pool.dma_start(cols[:, :], a["cols"]).then_inc(consts_in, 16)
            pool.dma_start(x_tok[:, :, :], a["x"].rearrange("(t p) d -> p t d", p=P)).then_inc(x_in, 16)
            pool.dma_start(r_decay, a["decay"]).then_inc(aux["ret_consts"], 16)
            pool.dma_start(r_rope, a["rope"]).then_inc(aux["ret_consts"], 16)
            pool.dma_start(router_w[:, :, :], a["w_router_2"].rearrange("(k p) e -> p k e", p=P)
                           ).then_inc(aux["router"], 16)
            pool.dma_start(router_b[:, :], a["b_router_2"].partition_broadcast(P)).then_inc(aux["router"], 16)

            ada = a["w_ada_2"].rearrange("l (k p) n -> p l k n", p=P)
            steps = [0]

            def link(ins):
                steps[0] += 1
                ins.then_inc(ada_step, 1)
                pool.wait_ge(ada_step, steps[0])

            def load_ada(hl, b):
                c0 = (hl % 2) * 3 * D + (b // 2) * BANK
                pool.dma_start(ada_raw[:, b % ADA_SLOTS, :].rearrange("p (k w) -> p k w", k=4),
                               ada[:, hl // 2, 4 * (b % 2):4 * (b % 2) + 4, c0:c0 + BANK]
                               ).then_inc(ada_in[b % ADA_SLOTS], 16)

            def modulation(hl):
                for b in range(ADA_SLOTS):
                    load_ada(hl, b)
                for b in range(12):
                    pool.wait_ge(ada_in[b % ADA_SLOTS], 16 * ((hl - 1) * 12 // ADA_SLOTS + b // ADA_SLOTS + 1))
                    w = ada_raw[:, b % ADA_SLOTS, :]
                    w4 = w.rearrange("p (k n) -> p k n", k=4)
                    acc = ada_acc(hl, b // 2)
                    link(nc.gpsimd.tensor_tensor(w4, w4, silu_c[:, 4 * (b % 2):4 * (b % 2) + 4, 0:1]
                                                 .broadcast_to([P, 4, BANK]), ALU.mult))
                    link(nc.gpsimd.tensor_tensor(w[:, 0:1024], w[:, 0:1024], w[:, 1024:2048], ALU.add))
                    if b % 2:
                        link(nc.gpsimd.tensor_tensor(w[:, 0:512], w[:, 0:512], w[:, 512:1024], ALU.add))
                        link(nc.gpsimd.tensor_tensor(acc, acc, w[:, 0:512], ALU.add))
                    else:
                        link(nc.gpsimd.tensor_tensor(acc, w[:, 0:512], w[:, 512:1024], ALU.add))
                    if b + ADA_SLOTS < 12:
                        load_ada(hl, b + ADA_SLOTS)

            def save_gate(hl):
                pool.wait_ge(ada_saved, 7 + hl)
                pool.dma_start(gates_dram[0, hl * D:(hl + 1) * D].rearrange("(k p) -> p k", p=P),
                               mod[:, hl, 16:24, 0], allow_slow_non_contiguous=True).then_inc(aux["gates_out"], 16)
                pool.wait_ge(aux["gates_out"], 16 * (hl + 1))

            def load_gate(hl, used_by):
                pool.wait_ge(*used_by)
                pool.dma_start(ln_gb[:, 0, :], gates_dram[0, hl * D:(hl + 1) * D].partition_broadcast(P)
                               ).then_inc(ln_in, 16)
                bias = a["b_ada_2"][hl // 2, (hl % 2) * 3072 + 2048:(hl % 2) * 3072 + 3072]
                pool.dma_start(ln_gb[:, 1, :], bias.partition_broadcast(P)).then_inc(ln_in, 16)

            def load_ln(n):
                if n:
                    pool.wait_ge(x_ready.sem, x_ready.after(f"x{n}", 1))
                pool.dma_start(ln_gb[:, 0, :], a["ln_gain"][n // 2, n % 2, :].partition_broadcast(P)
                               ).then_inc(ln_in, 16)
                pool.dma_start(ln_gb[:, 1, :], a["ln_bias"][n // 2, n % 2, :].partition_broadcast(P)
                               ).then_inc(ln_in, 16)

            load_ln(0)
            load_ln(1)
            pool.dma_start(b_hot[0:BUCKETS, :], a["bucket_hot"]).then_inc(aux["bias_consts"], 16)
            pool.dma_start(b_tab[0:BUCKETS, :], a["rel_bias"]).then_inc(aux["bias_consts"], 16)
            pool.dma_start(b_mask[0:AG * AH, :], a["rel_mask"]).then_inc(aux["bias_consts"], 16)
            pool.wait_ge(ada_ready, 1)
            modulation(1)
            pool.wait_ge(rows_saved, 1)
            pool.dma_start(rows_dram, b_rows[0:AG * AH, :]).then_inc(aux["rows_out"], 16)
            load_ln(2)
            pool.wait_ge(aux["rows_out"], 16)
            for h in range(AH):
                if h >= 2:
                    pool.wait_ge(scored.sem, scored.after("att", 2 * (h - 2) + 1))
                pool.dma_start(a_bias[:, h % 2, :, :],
                               bass.AP(rows_dram.tensor, h * ROWS_W, [[1, P], [AH * ROWS_W, AG], [1, T]])
                               ).then_inc(bias_in[h % 2], 16)
            load_ln(3)
            save_gate(0)
            save_gate(1)
            pool.wait_ge(fm_saved.sem, fm_saved.after("att", 3))
            pool.dma_start(y_dft, a["dft"]).then_inc(aux["hyena_in"], 16)
            pool.dma_start(y_win, a["window"]).then_inc(aux["hyena_in"], 16)
            pool.dma_start(y_w3[0:HID, :, :], a["hy_f_w3_2"].rearrange("h (n c) -> h n c", n=4)
                           ).then_inc(aux["hyena_in"], 16)
            pool.dma_start(y_w12[0:EMB, 0, :], a["hy_f_w1_2"]).then_inc(aux["hyena_in"], 16)
            pool.dma_start(y_w12[0:HID, 1, :], a["hy_f_w2_2"]).then_inc(aux["hyena_in"], 16)
            pool.dma_start(y_feat[0:EMB, :], a["features"]).then_inc(aux["hyena_in"], 16)
            modulation(2)
            load_gate(0, (x_ready.sem, x_ready.after("x4", 1)))
            save_gate(2)
            pool.wait_ge(hy_dve, 17)
            pool.dma_start(ctx_tok, a["ctx_2"].rearrange("(t p) d -> p t d", p=P)).then_inc(aux["ctx_in"], 16)
            pool.wait_ge(x_ready.sem, x_ready.after("mc", 1))
            pool.dma_start(n_mask, a["window_mask"]).then_inc(aux["n_mask"], 16)
            for h in range(NH):
                if h >= 2:
                    pool.wait_ge(scored.sem, scored.after("nat", 2 * (h - 2) + 1))
                for r in range(2):
                    at = h * 15 * 31 + (WIN_R - 4 + r) * 31 + WIN_C - GRID_W
                    pool.dma_start(n_bias[64 * r:64 * r + 64, h % 2, :].rearrange("p (r c) -> p r c", c=GRID_W),
                                   bass.AP(a["na_rpb_2"].tensor, at, [[1, GRID_W], [31, 6], [1, GRID_W]])
                                   ).then_inc(bias_in[h % 2], 16)
                if h == 0:
                    pool.wait_ge(aux["n_mask"], 16)
                pool.wait_ge(bias_in[h % 2], 16 * (AH // 2) + 32 * (h // 2 + 1))
                nc.gpsimd.tensor_tensor(n_bias[:, h % 2, :], n_bias[:, h % 2, :], n_mask, ALU.add
                                        ).then_inc(masked, 1)
            pool.wait_ge(fm_saved.sem, fm_saved.after("nat", 1))
            pool.dma_start(f_cs, a["fourier"]).then_inc(aux["fourier_in"], 16)
            load_gate(1, (x_summed.sem, x_summed.after("mix", 1)))
            modulation(3)
            load_gate(2, (x_summed.sem, x_summed.after("ffn2", 1)))
            save_gate(3)
            load_gate(3, (x_summed.sem, x_summed.after("fourier", 1)))
            pool.wait_ge(x_summed.sem, x_summed.after("moe", 1))
            pool.dma_start(ln_gb[:, 0, :], a["final_g_2"].partition_broadcast(P)).then_inc(ln_in, 16)

        @block.tensor
        def _(pe):
            mm = nc.tensor.matmul

            def half_block(stage, n, half, at=HERE):
                m = 2 * (FIRST_BLOCK[stage] + n) + half
                pe.wait_ge(split_ready, at.plus(m + 1, 12, 84))
                return w_hi[:, m % SPLIT, :], w_lo[:, m % SPLIT, :]

            def cut_block(stage, n, at=HERE):
                return [[v.rearrange("p (k w) -> p k w", k=4) for v in half_block(stage, n, h, at)] for h in range(2)]

            def mm3(dst, lhs, rhs, start, stop):
                mm(dst, lhs[0], rhs[0], start=start, stop=False)
                mm(dst, lhs[0], rhs[1], start=False, stop=False)
                return mm(dst, lhs[1], rhs[0], start=False, stop=stop)

            def x_tile(k, t):
                return x_hi[:, k, t * P:(t + 1) * P], x_lo[:, k, t * P:(t + 1) * P]

            def x_all(k):
                return x_hi[:, k, :], x_lo[:, k, :]

            def column_tile(w, k, cols):
                return w[k // 4][0][:, k % 4, cols], w[k // 4][1][:, k % 4, cols]

            def transposes(stage, src, chunks, first_bank=0):
                for q in range(chunks // 2):
                    if q >= 4:
                        pe.wait_ge(fm_saved.sem, fm_saved.after(stage, q - 4))
                    for c in (2 * q, 2 * q + 1):
                        for t in range(TT):
                            o = (c % 2) * T + t * P
                            last = nc.tensor.transpose(ps[:, first_bank + q % 4, o:o + P],
                                                       src[:, t, c * P:(c + 1) * P], ident)
                    last.then_inc(transposed.sem, 1)

            def project_wide(stage, n, g, tiles, free=True, at=HERE):
                base = PROJ_BASE[stage]
                for t in range(len(tiles)):
                    pe.wait_ge(proj_saved.sem, at.plus(base + g + t + 1, 6))
                for q in range(4):
                    hi, lo = (v.rearrange("p (k w) -> p k w", k=2) for v in half_block(stage, n + q // 2, q % 2, at))
                    for t, tile in enumerate(tiles):
                        for k in range(2):
                            kk = 2 * q + k
                            last = mm3(ps[:, 2 + (base + g + t) % 6, :], tile(kk), (hi[:, k, :], lo[:, k, :]),
                                       kk == 0, kk == KD - 1)
                    last.then_inc(split_free, 1)

            def accumulate(stage, n, lhs, k0, start, stop, at=HERE, tiles=TT):
                for k in range(2):
                    hi, lo = half_block(stage, n, k, at)
                    for t in range(tiles):
                        for half in range(2):
                            c = slice(half * 512, half * 512 + 512)
                            last = mm3(ps[:, 2 * t + half, :], lhs(k0 + k, t), (hi[:, c], lo[:, c]),
                                       start and k == 0, stop and k == 1)
                    last.then_inc(split_free, 1)

            def wait_acc(stage):
                pe.wait_ge(acc_read.sem, acc_read.base[stage])

            def glu(stage, units, odd, tiles, lhs, at=HERE, per_item=0, after_second=None,
                    before_last=None):
                def h_tile(k, t):
                    return h_hi[:, k, t * P:(t + 1) * P], h_lo[:, k, t * P:(t + 1) * P]

                def columns(n, q0, bank, at):
                    for q in (q0, q0 + 1):
                        hi, lo = (v.rearrange("p (k w) -> p k w", k=2) for v in half_block(stage, n, q % 2, at))
                        for t in range(tiles):
                            for k in range(2):
                                kk = 2 * q + k
                                last = mm3(ps[:, bank + t, :], lhs(kk, t), (hi[:, k, :], lo[:, k, :]),
                                           kk == 0, kk == KD - 1)
                        last.then_inc(split_free, 1)

                def turn(u, at, width=4):
                    pe.wait_ge(h_ready.sem, at.plus(h_ready.after(stage, u), 1, per_item))
                    for f in range(width):
                        for t in range(tiles):
                            o = 6 * BANK + f * tiles * P + t * P
                            last = nc.tensor.transpose(psf[:, o:o + P], h_tok[:, t, f * P:(f + 1) * P], ident)
                    last.then_inc(h_turned.sem, 1)

                def gate_free(u, at):
                    pe.wait_ge(silu_done.sem, at.plus(silu_done.after(stage, u) - 1, 1, per_item))

                def up_free(u, at):
                    pe.wait_ge(h_cut.sem, at.plus(h_cut.after(stage, u) - 1, 1, per_item))

                def downs(u, n, start, stop, at, count=2):
                    pe.wait_ge(h_cut.sem, at.plus(h_cut.after(stage, u), 1, per_item))
                    for b in range(count):
                        accumulate(stage, n + b, h_tile, 2 * b, start and b == 0, stop and b == count - 1, at, tiles)

                def unit(u, n, at, first=False):
                    gate_free(u, at)
                    columns(n, 0, 4, at)
                    if u:
                        turn(u - 1, at)
                    columns(n + 1, 2, 4, at)
                    up_free(u, at)
                    columns(n + 2, 0, 6, at)
                    columns(n + 3, 2, 6, at)

                unit(0, 0, at)
                unit(1, 4, at)
                if after_second:
                    after_second()
                if per_item:
                    pe.wait_ge(yc_ready, at.plus(1, 0, 1))
                else:
                    wait_acc(stage)
                downs(0, 8, True, False, at)
                with pe.Fori(0, units - 2) as i:
                    here = At(i, at.e)
                    unit(2, 10, here)
                    downs(1, 14, False, False, here)
                n = 10 + 6 * (units - 2)
                if odd:
                    gate_free(units, at)
                    w = cut_block(stage, n, at)
                    for t in range(tiles):
                        for k in range(KD):
                            last = mm3(ps[:, 4 + t, 0:T], lhs(k, t), column_tile(w, k, slice(0, T)), k == 0, k == KD - 1)
                    last.then_inc(split_free, 2)
                    turn(units - 1, at)
                    up_free(units, at)
                    w = cut_block(stage, n + 1, at)
                    for t in range(tiles):
                        for k in range(KD):
                            last = mm3(ps[:, 6 + t, 0:T], lhs(k, t), column_tile(w, k, slice(0, T)), k == 0, k == KD - 1)
                    last.then_inc(split_free, 2)
                    downs(units - 1, n + 2, False, False, at)
                    turn(units, at, 2)
                    downs(units, n + 4, False, True, at, 1)
                else:
                    if before_last:
                        before_last()
                    turn(units - 1, at)
                    downs(units - 1, n, False, True, at)

            pe.wait_ge(ada_ready, 1)
            for b in range(12):
                pe.wait_ge(ada_first[b % ADA_SLOTS], 16 * (b // ADA_SLOTS + 1))
                w = ada_raw[:, b % ADA_SLOTS, :].rearrange("p (k w) -> p k w", k=4)
                for k in range(4):
                    last = mm(ps[0:2, b // 2, :], silu_c[:, 4 * (b % 2) + k, :], w[:, k, :],
                              start=b % 2 == 0 and k == 0, stop=b % 2 == 1 and k == 3)
                last.then_inc(ada_used, 1)
            for nb in range(6):
                pe.wait_ge(ada_saved, nb + 1)
                for f in range(4 * nb, 4 * nb + 4):
                    last = nc.tensor.transpose(ps[:, 6, 2 * f:2 * f + 2], ada_rows[0:2, f * P:(f + 1) * P],
                                               ident[0:2, 0:2])
            last.then_inc(ada_turned, 1)

            def modulation(hl, stage):
                pe.wait_ge(silu_done.sem, silu_done.after(stage, 5))
                pe.wait_ge(ada_step, 42 * hl)
                for f in range(24):
                    last = mm(ps[:, 4, 2 * f:2 * f + 1], ada_acc(hl, f // 4)[:, (f % 4) * P:(f % 4 + 1) * P],
                              ones[:, 0:1], start=True, stop=True)
                last.then_inc(ada_turned, 1)

            pe.wait_ge(x_in, 16)
            transposes("x0", x_tok, KD)
            pe.wait_ge(ada_saved, 7)
            pe.wait_ge(fm_saved.sem, fm_saved.after("x0", 3))
            for b in range(8):
                w = cut_block("ret_in", b)
                g = PROJ_BASE["ret_in"] + b
                pe.wait_ge(proj_saved.sem, g + 1)
                for f in range(2):
                    for k in range(KD):
                        last = mm3(ps[:, 2 + g % 6, f * T:(f + 1) * T], column_tile(w, k, slice(f, 256, 2)), x_all(k),
                                   k == 0, k == KD - 1)
                last.then_inc(split_free, 2)
            tok_tiles = [lambda k, t=t: x_tile(k, t) for t in range(TT)]
            for nb in range(8):
                project_wide("ret_in", 8 + 2 * nb, 8 + 2 * nb, tok_tiles)
            pe.wait_ge(proj_saved.sem, proj_saved.after("ret_in", 23))
            for h in range(RH):
                pe.wait_ge(rope_done, 5 + h)
                if h:
                    pe.wait_ge(st_saved, h)
                for jt in range(TT):
                    n = T - jt * P
                    for f in range(2):
                        last = mm(ps[:, 0, jt * T:jt * T + n], r_rot[:, 4 + h, f, jt * P:(jt + 1) * P],
                                  r_rot[:, h, f, jt * P:T], start=f == 0, stop=f == 1)
                last.then_inc(st_ready, 1)
                pe.wait_ge(st_saved, h + 1)
                for t in range(TT):
                    bank = 1 + (2 * h + t) % 4
                    if 2 * h + t >= 4:
                        pe.wait_ge(y_read, 2 * h + t - 3)
                    v = r_v[:, :, h * RDV:(h + 1) * RDV]
                    st = r_st[:, h % 2, :]
                    if t == 0:
                        last = mm(ps[:, bank, :], st[:, 0:P], v[:, 0, :], start=True, stop=True)
                    else:
                        mm(ps[:, bank, :], st[:, P:T], v[:, 0, :], start=True, stop=False)
                        last = mm(ps[:, bank, :], st[:, T:T + P], v[:, 1, :], start=False, stop=True)
                    last.then_inc(y_ready, 1)
            pe.wait_ge(y_gated, 2 * RH)
            wait_acc("ret_out")
            for part in range(2):
                transposes(f"ret{part}", r_y[:, :, part * D:(part + 1) * D], KD, first_bank=4)
                pe.wait_ge(fm_saved.sem, fm_saved.after(f"ret{part}", 3))
                for b in range(4 * part, 4 * part + 4):
                    accumulate("ret_out", b, x_tile, 2 * (b % 4), b == 0, b == 7)

            def first_block_ffn(xa, stage):
                pe.wait_ge(x_ready.sem, x_ready.after(xa, 1))
                transposes(xa, x_tok, KD)
                pe.wait_ge(fm_saved.sem, fm_saved.after(xa, 3))
                glu(stage, 5, True, TT, x_tile)

            first_block_ffn("x1", "ffn0")
            modulation(1, "ffn0")

            pe.wait_ge(aux["bias_consts"], 48)
            pe.wait_ge(x_ready.sem, x_ready.after("x2", 1))
            mm(ps[0:AG * AH, 7, 0:ROWS_W], b_tab[0:BUCKETS, 0:AG * AH], b_hot[0:BUCKETS, :],
               start=True, stop=True).then_inc(rows_ready, 1)
            transposes("x2", x_tok, KD)
            pe.wait_ge(fm_saved.sem, fm_saved.after("x2", 3))
            pe.wait_ge(rows_saved, 1)
            pe.wait_ge(ada_saved, 8)
            g0 = PROJ_BASE["att_in"]
            with pe.Fori(0, 4) as i:
                for b in range(6):
                    w = cut_block("att_in", b, At(i))
                    pe.wait_ge(proj_saved.sem, g0 + b + 1 + i * 6)
                    for f in range(2):
                        for k in range(KD):
                            last = mm3(ps[:, 2 + (g0 + b) % 6, f * T:(f + 1) * T],
                                       column_tile(w, k, slice(f * P, (f + 1) * P)), x_all(k), k == 0, k == KD - 1)
                    last.then_inc(split_free, 2)
            with pe.Fori(0, 2) as i:
                for b in range(3):
                    project_wide("att_in", 24 + 2 * b, 24 + 2 * b, tok_tiles, at=At(i))
            pe.wait_ge(proj_saved.sem, proj_saved.after("att_in", 35))

            def heads(stage, nh, scores, n_tr, pt_bank, probs_of, pt_of, mix):
                def score(h, it):
                    u = 2 * h + it
                    if h:
                        pe.wait_ge(probs.sem, probs.after(stage, u - 2))
                    scores(h, it).then_inc(scored.sem, 1)

                score(0, 0)
                score(0, 1)
                for h in range(nh):
                    for it in range(2):
                        u = 2 * h + it
                        pe.wait_ge(probs.sem, probs.after(stage, u))
                        if h:
                            pe.wait_ge(probs_fm.sem, probs_fm.after(stage, u - 2))
                        for q in range(n_tr[it]):
                            last = nc.tensor.transpose(psf[:, pt_bank[it] * BANK + q * P:pt_bank[it] * BANK + (q + 1) * P],
                                                       probs_of(it)[:, q * P:(q + 1) * P], ident)
                        last.then_inc(probs_t.sem, 1)
                        if h + 1 < nh:
                            score(h + 1, it)
                    for it in range(2):
                        u = 2 * h + it
                        pe.wait_ge(probs_fm.sem, probs_fm.after(stage, u))
                        if h:
                            pe.wait_ge(head_saved.sem, head_saved.after(stage, u - 2))
                        mix(h, it, pt_of(it)).then_inc(mixed.sem, 1)

            def att_scores(h, it):
                if it == 0:
                    pe.wait_ge(bias_in[h % 2], 16 * (h // 2 + 1))
                n = (it + 1) * P
                at = it * BANK
                for g in range(AG):
                    f, r = g * 8 + h // 2, (h % 2) * AHD
                    o = psf[:, at + g * n:at + (g + 1) * n]
                    mm(o, a_q[r:r + AHD, f, it * P:(it + 1) * P], a_k[r:r + AHD, f, 0:n], start=True, stop=False)
                    last = mm(o, rev, a_bias[:, h % 2, g, T - n:T], start=False, stop=True)
                return last

            def att_mix(h, it, pt):
                n = it + 1
                for g in range(AG):
                    for j in range(n):
                        q = g * n + j
                        last = mm(ps[:, 6 + it, 0:AHD], pt[:, q * P:(q + 1) * P],
                                  a_v[:, j, g * D + h * AHD:g * D + (h + 1) * AHD],
                                  start=q == 0, stop=q == AG * n - 1)
                return last

            heads("att", AH, att_scores, (3, 6), (3, 4), lambda it: a_p[:, 384 * it:384 + 768 * it],
                  lambda it: a_pt[:, 384 * it:384 + 768 * it], att_mix)
            pe.wait_ge(head_saved.sem, head_saved.after("att", 2 * AH - 1))
            transposes("att", work, KD)
            pe.wait_ge(fm_saved.sem, fm_saved.after("att", 3))
            wait_acc("att_out")
            for b in range(4):
                accumulate("att_out", b, x_tile, 2 * b, b == 0, b == 3)
            first_block_ffn("x3", "ffn1")
            modulation(2, "ffn1")

            pe.wait_ge(x_ready.sem, x_ready.after("x4", 1))
            pe.wait_ge(aux["hyena_in"], 96)
            pe.wait_ge(ada_saved, 9)
            mm(ps[0:HID, 0, 0:T], y_w12[0:EMB, 0, :], y_feat[0:EMB, :], start=True, stop=True).then_inc(hy_pe, 1)
            pe.wait_ge(hy_act, 1)
            mm(ps[0:HID, 1, 0:T], y_w12[0:HID, 1, :], y_arg[0:HID, 2, :], start=True, stop=True).then_inc(hy_pe, 1)
            pe.wait_ge(hy_act, 2)
            for n in range(4):
                for t in range(TT):
                    mm(ps[:, (2 * n + t + 2) % 8, :], y_arg[0:HID, 3, t * P:(t + 1) * P], y_w3[0:HID, n, :],
                       start=True, stop=True).then_inc(hy_pe, 1)
            for o in range(2):
                for side in range(2):
                    n = 2 * o + side
                    pe.wait_ge(hy_act, 2 + 2 * n + 2)
                    for t in range(TT):
                        last = mm(ps[:, 2 + o, :], ones, y_abs[:, t, n, :], start=n % 2 == 0 and t == 0,
                                  stop=n % 2 == 1 and t == 1)
                last.then_inc(hy_pe, 1)
            for o in range(2):
                pe.wait_ge(hy_dve, 13 + o)
                for part in range(2):
                    for f in range(2):
                        bank = 4 * (o % 2) + 2 * part + f
                        for t in range(TT):
                            last = mm(ps[:, bank, :], y_dft[:, part, t, f * P:(f + 1) * P],
                                      y_abs[:, t, 2 * o + part, :], start=t == 0, stop=t == TT - 1)
                last.then_inc(hy_pe, 1)

            def modulated_input(stage):
                for t in range(TT):
                    pe.wait_ge(x_ready.sem, x_ready.after(stage, t))
                transposes(stage, work, KD)

            pe.wait_ge(hy_dve, 17)
            modulated_input("m0")
            pe.wait_ge(fm_saved.sem, fm_saved.after("m0", 3))
            modulated_input("mc")
            pe.wait_ge(fm_saved.sem, fm_saved.after("mc", 3))
            g0 = PROJ_BASE["w_in"]
            g = g0
            for b in range(10):
                w = cut_block("w_in", b)
                wide_k = b >= 8
                pe.wait_ge(proj_saved.sem, g + 1)
                if wide_k:
                    pe.wait_ge(proj_saved.sem, g + 2)
                for f in range(2):
                    wf = [column_tile(w, k, slice(f * P, (f + 1) * P)) for k in range(KD)]
                    dst = ps[:, 2 + (g + f) % 6, 0:T] if wide_k else ps[:, 2 + g % 6, f * T:(f + 1) * T]
                    for k in range(KD):
                        last = mm3(dst, wf[k], x_all(k), k == 0, k == KD - 1)
                    if wide_k:
                        for k in range(KD):
                            last = mm3(ps[:, 2 + (g + f) % 6, T:2 * T], wf[k], (h_hi[:, k, :], h_lo[:, k, :]),
                                       k == 0, k == KD - 1)
                last.then_inc(split_free, 2)
                g += 2 if wide_k else 1
            ctx_tiles = [lambda k, t=t: (h_hi[:, k, t * P:(t + 1) * P], h_lo[:, k, t * P:(t + 1) * P])
                         for t in range(TT)]
            project_wide("w_in", 10, g - g0, tok_tiles + ctx_tiles)

            pe.wait_ge(short_done, 4)
            for t in range(TT):
                for c in range(4):
                    last = nc.tensor.transpose(ps[:, t, c * P:(c + 1) * P], z[:, c, t * P:(t + 1) * P], ident)
                last.then_inc(transposed.sem, 1)
            for o in range(2):
                pe.wait_ge(tok_saved, 2 * o + 2)
                pe.wait_ge(proj_saved.sem, proj_saved.after("w_in", 15))
                for part in range(2):
                    for f in range(2):
                        for t in range(TT):
                            last = mm(ps[:, 4 + 2 * part + f, :], y_dft[:, part, t, f * P:(f + 1) * P], z_u[:, t, :],
                                      start=t == 0, stop=t == TT - 1)
                last.then_inc(conv_f, 1)
                pe.wait_ge(conv_y, o + 1)
                for c in range(4):
                    for part in range(2):
                        for f in range(2):
                            last = mm(ps[:, 2 + c // 2, (c % 2) * T:(c % 2 + 1) * T], z_y[:, part, f, c * P:(c + 1) * P],
                                      y_dft[:, 2 + part, f, :], start=part == 0 and f == 0, stop=part == 1 and f == 1)
                    if c % 2:
                        last.then_inc(conv_t, 1)
                if o == 0:
                    pe.wait_ge(conv_out, 4)
                    for t in range(TT):
                        for c in range(4):
                            last = nc.tensor.transpose(ps[:, t, c * P:(c + 1) * P], z[:, c, t * P:(t + 1) * P], ident)
                        last.then_inc(transposed.sem, 1)

            pe.wait_ge(conv_out, 8)

            def nat_scores(h, it):
                if it == 0:
                    pe.wait_ge(masked, h + 1)
                f, r = h // 4, (h % 4) * NHD
                mm(ps[:, it, :], n_q[r:r + NHD, f, it * P:(it + 1) * P], n_k[r:r + NHD, f, :], start=True, stop=False)
                return mm(ps[:, it, 0:T], rev, n_bias[:, h % 2, (1 - it) * P:(1 - it) * P + T],
                          start=False, stop=True)

            def nat_mix(h, it, pt):
                for q in range(4):
                    last = mm(ps[:, 4 + it, 0:NHD], pt[:, q * P:(q + 1) * P], n_v[:, q, h * NHD:(h + 1) * NHD],
                              start=q == 0, stop=q == 3)
                return last

            heads("nat", NH, nat_scores, (4, 4), (2, 3), lambda it: n_p[:, it, :], lambda it: n_pt[:, it, :], nat_mix)
            pe.wait_ge(head_saved.sem, head_saved.after("nat", 2 * NH - 1))
            pe.wait_ge(fm_saved.sem, fm_saved.after("hy", 3))
            transposes("nat", work, 4, first_bank=6)
            pe.wait_ge(fm_saved.sem, fm_saved.after("nat", 1))
            wait_acc("mix_out")
            for b in range(4):
                accumulate("mix_out", b, x_tile, 2 * b, b == 0, b == 3)

            modulated_input("m1")
            pe.wait_ge(fm_saved.sem, fm_saved.after("m1", 3))
            glu("ffn2", 5, True, TT, x_tile)
            modulation(3, "ffn2")

            modulated_input("m2")
            pe.wait_ge(ada_saved, 10)
            pe.wait_ge(modulated.sem, modulated.after("m2", 3))
            pe.wait_ge(aux["fourier_in"], 16)
            for g in range(4):
                for t in range(TT):
                    q = PROJ_BASE["four_a"] + 2 * g + t
                    pe.wait_ge(proj_saved.sem, q + 1)
                    for k in range(2):
                        last = mm(ps[:, 2 + q % 6, :], f_x[:, 2 * g + k, t * P:(t + 1) * P], f_cs[:, k, :],
                                  start=k == 0, stop=k == 1)
                    last.then_inc(banked.sem, 1)
            pe.wait_ge(proj_saved.sem, proj_saved.after("four_a", 7))
            for d in range(KD):
                q = PROJ_BASE["four_y"] + d // 2
                if d % 2 == 0:
                    pe.wait_ge(proj_saved.sem, q + 1)
                for part in range(2):
                    for t in range(TT):
                        c = part * T + (d % 2) * P
                        last = mm(ps[:, 2 + q % 6, (d % 2) * T:(d % 2 + 1) * T], f_a[:, t, d // 2, c:c + P],
                                  f_cs[:, 2 + t, part * T:(part + 1) * T], start=part == 0 and t == 0,
                                  stop=part == 1 and t == 1)
                if d % 2:
                    last.then_inc(banked.sem, 1)
            pe.wait_ge(proj_saved.sem, proj_saved.after("four_y", 3))
            wait_acc("fourier")
            for b in range(4):
                accumulate("fourier", b, x_tile, 2 * b, b == 0, b == 3)

            modulated_input("m3")
            pe.wait_ge(fm_saved.sem, fm_saved.after("m3", 3))
            pe.wait_ge(router_cut, 2)
            for t in range(TT):
                for k in range(KD):
                    last = mm3(ps[:, 4 + t, 0:EXPERTS], x_tile(k, t), (router_hi[:, k, :], router_lo[:, k, :]),
                               k == 0, k == KD - 1)
            last.then_inc(routed, 1)
            pe.wait_ge(ranked, 1)
            m0, m1 = route[:, 0, 1, :], route[:, 1, 1, :]
            mm(ps[:, 4, 0:8], tri, m0, start=True, stop=True)
            mm(ps[:, 4, 8:16], ones, m0, start=True, stop=False)
            mm(ps[:, 4, 8:16], tri, m1, start=False, stop=True)
            mm(ps[:, 4, 16:24], ones, m0, start=True, stop=False)
            mm(ps[:, 4, 16:24], ones, m1, start=False, stop=True).then_inc(routed, 1)
            pe.wait_ge(table_ready, 1)
            count = pe.value_load(table[0:1, ITEMS - 1:ITEMS], min_val=EXPERTS, max_val=ITEMS - 1)

            def gather(nth):
                pe.wait_ge(sel_ready, nth)
                for k in range(KD):
                    for t in range(TT):
                        last = mm(psf[:, 2 * BANK + k * P:2 * BANK + (k + 1) * P], work[:, t, k * P:(k + 1) * P],
                                  m_sel[:, t, :], start=t == 0, stop=t == TT - 1)
                last.then_inc(gathered, 1)

            def scatter(nth):
                pe.wait_ge(yc_ready, nth + 1)
                for t in range(TT):
                    for half in range(2):
                        bank = (2, 3, 5, 7)[2 * t + half]
                        last = mm(ps[:, bank, :], m_selt[:, t * P:(t + 1) * P], m_yc[:, half * 512:half * 512 + 512],
                                  start=True, stop=True)
                    last.then_inc(scattered, 1)

            gather(1)
            with pe.Fori(0, count) as e:
                at = At(None, e)

                def next_rows():
                    pe.wait_ge(shares_added, e * 2 + 1)
                    gather(e + 2)

                def last_scatter():
                    pe.wait_ge(m_x_ready, e + 2)
                    scatter(e)

                pe.wait_ge(m_x_cut, e + 1)
                glu("moe", 7, None, 1, lambda k, t: x_tile(k, 0), at, per_item=7, after_second=next_rows,
                    before_last=last_scatter)
                pe.wait_ge(selg_ready, e + 1)
                pe.wait_ge(shares_added, e * 2 + 3)
                for t in range(TT):
                    last = nc.tensor.transpose(ps[:, 7, t * P:(t + 1) * P], m_selg[:, t, :], ident)
                last.then_inc(sel_turned, 1)
            scatter(count)

        @block.scalar
        def _(act):
            steps = [0]

            def link(ins):
                steps[0] += 1
                ins.then_inc(act_step, 1)
                act.wait_ge(act_step, steps[0])

            def ahead(stage, n, at=HERE):
                b = FIRST_BLOCK[stage] + n + AHEAD
                act.wait_ge(landed[SLOT_OF[b]],
                            at.plus(LANDING[b], 32 if b < FIRST_BLOCK["moe"] else 16, 112))
                for h in range(2):
                    m = 2 * (b) + h
                    act.wait_ge(split_free, at.plus(m + 1, 12, 84))
                    nc.scalar.activation(w_hi[:, m % SPLIT, :], raw(SLOT_OF[b])[:, h * HALF:(h + 1) * HALF], ACT.Copy
                                         ).then_inc(hi_ready, 1)

            def save_fm(stage, n, first_bank=0, k0=0, hi=x_hi):
                for q in range(n):
                    act.wait_ge(transposed.sem, transposed.after(stage, q))
                    nc.scalar.activation(hi[:, k0 + 2 * q:k0 + 2 * q + 2, :], ps[:, first_bank + q % 4, :], ACT.Copy
                                         ).then_inc(fm_hi.sem, 1)

            def save_modulated(stage, hi=x_hi):
                for q in range(4):
                    act.wait_ge(modulated.sem, modulated.after(stage, q))
                    nc.scalar.activation(hi[:, 2 * q:2 * q + 2, :], mod_tmp[:, 2 * q:2 * q + 2, :], ACT.Copy
                                         ).then_inc(fm_hi.sem, 1)

            def root(stage):
                for t in range(TT):
                    act.wait_ge(moments.sem, moments.after(stage, t))
                    nc.scalar.activation(stat[:, 20 + t:21 + t], stat[:, 16 + t:17 + t], ACT.Sqrt
                                         ).then_inc(roots.sem, 1)

            def rms(stage, src, ready):
                for t in range(TT):
                    ready(t)
                    nc.scalar.activation(work[:, t, :], src[:, t, :], ACT.Square, accum_out=stat[:, 24 + t:25 + t]
                                         ).then_inc(squares.sem, 1)
                root(stage)

            def glu(stage, units, odd, tiles, at=HERE, per_item=0, before_last=None):
                def high(u, at, width=4):
                    act.wait_ge(h_turned.sem, at.plus(h_turned.after(stage, u), 1, per_item))
                    src = psf[:, 6 * BANK:6 * BANK + width * tiles * P].rearrange("p (f t) -> p f t", f=width)
                    nc.scalar.activation(h_hi[:, 0:width, 0:tiles * P], src, ACT.Copy).then_inc(h_high.sem, 1)

                def silu(u, n, at, width=512):
                    act.wait_ge(split_free, at.plus(used(stage, n), 12, 84))
                    nc.scalar.activation(silu_sb[:, 0:tiles, 0:width], ps[:, 4:4 + tiles, 0:width], ACT.Silu
                                         ).then_inc(silu_done.sem, 1)

                def unit(u, n, at):
                    if u:
                        high(u - 1, at)
                    ahead(stage, n, at)
                    ahead(stage, n + 1, at)
                    silu(u, n + 1, at)
                    for b in range(2, 6 if u else 4):
                        ahead(stage, n + b, at)

                unit(0, 0, at)
                unit(1, 4, at)
                with act.Fori(0, units - 2) as i:
                    unit(2, 10, At(i, at.e))
                n = 10 + 6 * (units - 2)
                if odd:
                    high(units - 1, at)
                    silu(units, n, at, 256)
                    for b in range(4):
                        ahead(stage, n + b, at)
                    high(units, at, 2)
                else:
                    high(units - 1, at)
                    if before_last:
                        before_last()
                    ahead(stage, n, at)
                    ahead(stage, n + 1, at)

            act.wait_ge(consts_in, 32)
            nc.scalar.activation(silu_c[:, :, :].rearrange("p k c -> p (k c)"), col("c", 0, 16), ACT.Silu
                                 ).then_inc(ada_ready, 1)
            for b in range(AHEAD):
                ahead("ret_in", b - AHEAD)
            save_fm("x0", 4)
            g0 = PROJ_BASE["ret_in"]
            for b in range(8):
                ahead("ret_in", b)
                act.wait_ge(split_free, used("ret_in", b))
                nc.scalar.activation(r_raw[:, b, :, :].rearrange("p f t -> p (f t)"), ps[:, 2 + (g0 + b) % 6, :],
                                     ACT.Copy).then_inc(proj_saved.sem, 1)
            for nb in range(8):
                ahead("ret_in", 8 + 2 * nb)
                ahead("ret_in", 9 + 2 * nb)
                act.wait_ge(split_free, used("ret_in", 8 + 2 * nb + 1))
                for t in range(TT):
                    dst = (r_v if nb < 4 else r_gate)[:, t, (nb % 4) * BANK:(nb % 4 + 1) * BANK]
                    nc.scalar.activation(dst, ps[:, 2 + (g0 + 8 + 2 * nb + t) % 6, :],
                                         ACT.Copy if nb < 4 else ACT.Silu).then_inc(proj_saved.sem, 1)
            for u in range(2 * RH):
                act.wait_ge(y_var, u + 1)
                nc.scalar.activation(stat[:, 34 + u % 2:35 + u % 2], stat[:, 32 + u % 2:33 + u % 2], ACT.Sqrt
                                     ).then_inc(y_root, 1)
            save_fm("ret0", 4, first_bank=4)
            for b in range(4):
                ahead("ret_out", b)
            save_fm("ret1", 4, first_bank=4)
            for b in range(4, 7):
                ahead("ret_out", b)
            root("ln0")
            ahead("ret_out", 7)
            save_fm("x1", 4)
            glu("ffn0", 5, True, TT)
            root("ln1")
            ahead("ffn0", 32)
            save_fm("x2", 4)
            g0 = PROJ_BASE["att_in"]
            act.wait_ge(aux["rows_out"], 16)
            for part in range(2):
                with act.Fori(0, 2) as i:
                    for b in range(6):
                        ahead("att_in", 12 * part + b, At(i))
                        act.wait_ge(split_free, used("att_in", 12 * part + b) + i * 12)
                        dst = (a_k if part else a_q).rearrange("p f t -> p (f t)")
                        nc.scalar.activation(dst[:, bass.ds(i * 3072 + b * BANK, BANK)], ps[:, 2 + (g0 + b) % 6, :],
                                             ACT.Copy, scale=1.0 if part else AHD ** -0.5).then_inc(proj_saved.sem, 1)
            v_flat = a_v.rearrange("p t n -> p (t n)")
            with act.Fori(0, 2) as i:
                for b in range(3):
                    ahead("att_in", 24 + 2 * b, At(i))
                    ahead("att_in", 25 + 2 * b, At(i))
                    act.wait_ge(split_free, used("att_in", 24 + 2 * b + 1) + i * 12)
                    for t in range(TT):
                        nc.scalar.activation(v_flat[:, bass.ds(i * 1536 + t * AG * D + b * BANK, BANK)],
                                             ps[:, 2 + (g0 + 24 + 2 * b + t) % 6, :], ACT.Copy
                                             ).then_inc(proj_saved.sem, 1)

            def heads(stage, nh, scores_of, probs_of):
                for h in range(nh):
                    for it in range(2):
                        u = 2 * h + it
                        act.wait_ge(negmax.sem, negmax.after(stage, u))
                        if h:
                            act.wait_ge(probs_t.sem, probs_t.after(stage, u - 2))
                            act.wait_ge(head_saved.sem, head_saved.after(stage, u - 2))
                        nc.scalar.activation(probs_of(it), scores_of(it), ACT.Exp, bias=stat[:, 40 + it:41 + it],
                                             accum_out=stat[:, 42 + it:43 + it]).then_inc(probs.sem, 1)

            heads("att", AH, lambda it: psf[:, BANK * it:BANK * it + 384 * (it + 1)],
                  lambda it: a_p[:, 384 * it:384 + 768 * it])
            save_fm("att", 4)
            for b in range(3):
                ahead("att_out", b)
            root("ln2")
            ahead("att_out", 3)
            save_fm("x3", 4)
            glu("ffn1", 5, True, TT)
            root("ln3")
            ahead("ffn1", 32)
            for m in range(2):
                act.wait_ge(hy_dve, m + 1)
                nc.scalar.activation(y_arg[0:HID, 2 + m, :], y_arg[0:HID, 0, :], ACT.Sin).then_inc(hy_act, 1)
            for n in range(4):
                for t in range(TT):
                    act.wait_ge(hy_dve, 2 + 2 * n + t + 1)
                    nc.scalar.activation(y_abs[:, t, n, :], y_h[:, t, n, :], ACT.Abs).then_inc(hy_act, 1)

            def x_of(stage, n):
                def ready(t):
                    act.wait_ge(x_summed.sem, x_summed.after(stage, t))
                return ready

            rms("m0", x_tok, lambda t: act.wait_ge(x_ready.sem, x_ready.after("x4", t)))

            def ctx_ready(t):
                act.wait_ge(aux["ctx_in"], 16)
                act.wait_ge(transposed.sem, transposed.after("m0", 3))
            save_modulated("m0")
            rms("mc", ctx_tok, ctx_ready)
            save_modulated("mc", h_hi)
            g = PROJ_BASE["w_in"]
            act.wait_ge(x_ready.sem, x_ready.after("mc", 1))
            for b in range(10):
                ahead("w_in", b)
                act.wait_ge(split_free, used("w_in", b))
                if b < 8:
                    dst = z_raw[:, 2 * b:2 * b + 2, :] if b < 6 else n_q[:, 2 * (b - 6):2 * (b - 6) + 2, :]
                    nc.scalar.activation(dst.rearrange("p f t -> p (f t)"), ps[:, 2 + g % 6, :], ACT.Copy,
                                         scale=1.0 if b < 6 else NHD ** -0.5).then_inc(proj_saved.sem, 1)
                    g += 1
                else:
                    for f in range(2):
                        nc.scalar.activation(n_k[:, 2 * (b - 8) + f, :], ps[:, 2 + g % 6, :], ACT.Copy
                                             ).then_inc(proj_saved.sem, 1)
                        g += 1
            ahead("w_in", 10)
            ahead("w_in", 11)
            act.wait_ge(split_free, used("w_in", 11))
            for t in range(4):
                nc.scalar.activation(n_v[:, t, :], ps[:, 2 + g % 6, :], ACT.Copy).then_inc(proj_saved.sem, 1)
                g += 1
            act.wait_ge(short_done, 12)
            for stage in ("vtok", "ytok"):
                if stage == "ytok":
                    act.wait_ge(conv_f, 1)
                for t in range(TT):
                    act.wait_ge(transposed.sem, transposed.after(stage, t))
                    nc.scalar.activation(z_u[:, t, :], ps[:, t, :], ACT.Copy).then_inc(tok_saved, 1)
            for c in range(4):
                act.wait_ge(conv_out, 4 + c + 1)
                nc.scalar.activation(x_hi[:, c, :], z[:, c, :], ACT.Copy).then_inc(fm_hi.sem, 1)
            heads("nat", NH, lambda it: ps[:, it, :], lambda it: n_p[:, it, :])
            save_fm("nat", 2, first_bank=6, k0=4)
            for b in range(4):
                ahead("mix_out", b)
            rms("m1", x_tok, x_of("mix", 0))
            save_modulated("m1")
            glu("ffn2", 5, True, TT)
            ahead("ffn2", 32)
            rms("m2", x_tok, x_of("ffn2", 0))
            for q in range(8):
                act.wait_ge(banked.sem, banked.after("four_a", q))
                nc.scalar.activation(f_a[:, q % 2, q // 2, :], ps[:, 2 + (PROJ_BASE["four_a"] + q) % 6, :], ACT.Copy
                                     ).then_inc(proj_saved.sem, 1)
            for q in range(4):
                act.wait_ge(banked.sem, banked.after("four_y", q))
                nc.scalar.activation(x_hi[:, 2 * q:2 * q + 2, :], ps[:, 2 + (PROJ_BASE["four_y"] + q) % 6, :], ACT.Copy
                                     ).then_inc(four_hi, 1)
            for b in range(4):
                ahead("fourier", b)
            rms("m3", x_tok, x_of("fourier", 0))
            save_modulated("m3")
            act.wait_ge(aux["router"], 32)
            nc.scalar.activation(router_hi[:, :, :], router_w[:, :, :], ACT.Copy).then_inc(router_cut, 1)
            act.wait_ge(route_var, 1)
            nc.scalar.activation(stat[:, 50:52], stat[:, 48:50], ACT.Exp).then_inc(route_exp, 1)

            def item_high(nth):
                act.wait_ge(m_x_ready, nth)
                nc.scalar.activation(x_hi[:, :, 0:P], m_x, ACT.Copy).then_inc(m_x_high, 1)

            act.wait_ge(table_ready, 1)
            count = act.value_load(table[0:1, ITEMS - 1:ITEMS], min_val=EXPERTS, max_val=ITEMS - 1)
            item_high(1)
            with act.Fori(0, count) as e:
                at = At(None, e)

                def next_high():
                    act.wait_ge(split_free, at.plus(used("moe", 37), 0, 84))
                    item_high(e + 2)

                glu("moe", 7, False, 1, at, per_item=7, before_last=next_high)
                act.wait_ge(split_free, at.plus(used("moe", 41), 0, 84))
                act.wait_ge(shares_added, e * 2 + 3)
                nc.scalar.activation(m_yc, ps[:, 0:2, :].rearrange("p b n -> p (b n)"), ACT.Copy)
                act.wait_ge(sel_turned, e + 1)
                nc.scalar.activation(m_selt, ps[:, 7, 0:T], ACT.Copy).then_inc(yc_ready, 1)
            rms("fin", x_tok, x_of("moe", 0))

        @block.vector
        def _(dve):
            V = nc.vector
            steps = [0]

            def link(ins):
                steps[0] += 1
                ins.then_inc(dve_step, 1)
                dve.wait_ge(dve_step, steps[0])

            V.memset(stat[:, 5:6], 0.0).then_inc(split_free, SPLIT)
            V.memset(stat[:, 6:7], 0.0).then_inc(silu_done.sem, 1)
            V.memset(stat[:, 7:8], 0.0).then_inc(h_cut.sem, 1)
            V.memset(stat[:, 9:10], 0.0).then_inc(shares_added, 1)
            V.memset(stat[:, 2:3], 0.0).then_inc(proj_saved.sem, 6)
            V.memset(stat[:, 4:5], 0.0).then_inc(acc_read.sem, 4)

            def ahead(stage, n, at=HERE):
                b = FIRST_BLOCK[stage] + n + AHEAD
                for h in range(2):
                    m = 2 * (b) + h
                    dve.wait_ge(hi_ready, at.plus(m + 1, 12, 84))
                    V.tensor_tensor(w_lo[:, m % SPLIT, :], raw(SLOT_OF[b])[:, h * HALF:(h + 1) * HALF],
                                    w_hi[:, m % SPLIT, :].bitcast(F32), ALU.subtract).then_inc(split_ready, 1)

            def save_fm(stage, n, first_bank=0, k0=0):
                for q in range(n):
                    dve.wait_ge(fm_hi.sem, fm_hi.after(stage, q))
                    V.tensor_tensor(x_lo[:, k0 + 2 * q:k0 + 2 * q + 2, :],
                                    ps[:, first_bank + q % 4, :].rearrange("p (k t) -> p k t", k=2),
                                    x_hi[:, k0 + 2 * q:k0 + 2 * q + 2, :].bitcast(F32), ALU.subtract
                                    ).then_inc(fm_saved.sem, 1)

            def layer_norm(stage, xs, n, acc):
                dve.wait_ge(split_free, acc)
                for t in range(TT):
                    for half in range(2):
                        c = slice(half * 512, half * 512 + 512)
                        V.scalar_tensor_tensor(work[:, t, c], x_tok[:, t, c], ALPHA, ps[:, 2 * t + half, :],
                                               ALU.mult, ALU.add).then_inc(acc_read.sem, 1)
                dve.wait_ge(ln_in, 32 * (n + 1))
                for t in range(TT):
                    dve.wait_ge(acc_read.sem, acc_read.after(stage, 2 * t + 1))
                    V.bn_stats(stat[:, 0:6], work[:, t, 0:512])
                    link(V.bn_stats(stat[:, 6:12], work[:, t, 512:1024]))
                    link(V.bn_aggr(stat[:, 12 + 2 * t:14 + 2 * t], stat[:, 0:12]))
                    V.tensor_scalar(stat[:, 16 + t:17 + t], stat[:, 13 + 2 * t:14 + 2 * t], LN_EPS, None, ALU.add
                                    ).then_inc(moments.sem, 1)
                for t in range(TT):
                    dve.wait_ge(roots.sem, roots.after(f"ln{n}", t))
                    link(V.reciprocal(stat[:, 22 + t:23 + t], stat[:, 20 + t:21 + t]))
                    link(V.scalar_tensor_tensor(work[:, t, :], work[:, t, :], stat[:, 12 + 2 * t:13 + 2 * t],
                                                ln_gb[:, 0, :], ALU.subtract, ALU.mult))
                    V.scalar_tensor_tensor(x_tok[:, t, :], work[:, t, :], stat[:, 22 + t:23 + t], ln_gb[:, 1, :],
                                           ALU.mult, ALU.add).then_inc(x_ready.sem, 1)
                dve.wait_ge(x_ready.sem, x_ready.after(xs, 1))

            def rms_scale(stage, src, dst):
                for t in range(TT):
                    dve.wait_ge(squares.sem, squares.after(stage, t))
                    V.tensor_scalar(stat[:, 16 + t:17 + t], stat[:, 24 + t:25 + t], 1.0 / D, RMS_EPS, ALU.mult,
                                    ALU.add).then_inc(moments.sem, 1)
                for t in range(TT):
                    dve.wait_ge(roots.sem, roots.after(stage, t))
                    link(V.reciprocal(stat[:, 22 + t:23 + t], stat[:, 20 + t:21 + t]))
                    ins = V.tensor_scalar(dst[:, t, :], src[:, t, :], stat[:, 22 + t:23 + t], None, ALU.mult)
                    if stage == "fin":
                        link(ins)
                        ins = V.tensor_tensor(dst[:, t, :], dst[:, t, :], ln_gb[:, 0, :], ALU.mult)
                    ins.then_inc(x_ready.sem, 1)

            def modulate(stage, src, hl, which, hi, lo):
                g = col("norm_g", hl * 8, 8)
                link(V.tensor_scalar(mod_a[:, :, 0], mod[:, hl, 8:16, which], 1.0, None, ALU.add))
                link(V.tensor_tensor(mod_a[:, :, 1], mod_a[:, :, 0], g, ALU.mult))
                rms_scale(stage, src, work)
                dst = f_x if hi is None else mod_tmp
                for q in range(4):
                    dve.wait_ge(transposed.sem, transposed.after(stage, q))
                    for c in (2 * q, 2 * q + 1):
                        ins = V.tensor_scalar(dst[:, c, :], ps[:, q, (c % 2) * T:(c % 2 + 1) * T],
                                              mod_a[:, c, 1:2], mod[:, hl, c, which:which + 1], ALU.mult, ALU.add)
                    ins.then_inc(modulated.sem, 1)
                if hi is not None:
                    for q in range(4):
                        dve.wait_ge(fm_hi.sem, fm_hi.after(stage, q))
                        dve.wait_ge(modulated.sem, modulated.after(stage, q))
                        c = slice(2 * q, 2 * q + 2)
                        V.tensor_tensor(lo[:, c, :], mod_tmp[:, c, :], hi[:, c, :].bitcast(F32), ALU.subtract
                                        ).then_inc(fm_saved.sem, 1)
                    dve.wait_ge(fm_saved.sem, fm_saved.after(stage, 3))

            def residual(stage, xs, acc, hl):
                dve.wait_ge(split_free, acc)
                dve.wait_ge(ln_in, 32 * (5 + hl))
                link(V.tensor_tensor(ln_gb[:, 0, :], ln_gb[:, 0, :], ln_gb[:, 1, :], ALU.add))
                for t in range(TT):
                    for half in range(2):
                        c = slice(half * 512, half * 512 + 512)
                        V.tensor_tensor(work[:, t, c], ps[:, 2 * t + half, :], ln_gb[:, 0, c], ALU.mult
                                        ).then_inc(acc_read.sem, 1)
                for t in range(TT):
                    dve.wait_ge(acc_read.sem, acc_read.after(stage, 2 * t + 1))
                    V.tensor_tensor(x_tok[:, t, :], x_tok[:, t, :], work[:, t, :], ALU.add
                                    ).then_inc(x_summed.sem, 1)
                dve.wait_ge(x_summed.sem, x_summed.after(xs, 1))

            def glu(stage, units, odd, tiles, at=HERE, per_item=0, after_first=None, after_second=None,
                    before_last=None):
                def low(u, at, width=4):
                    dve.wait_ge(h_high.sem, at.plus(h_high.after(stage, u), 1, per_item))
                    src = psf[:, 6 * BANK:6 * BANK + width * tiles * P].rearrange("p (f t) -> p f t", f=width)
                    V.tensor_tensor(h_lo[:, 0:width, 0:tiles * P], src, h_hi[:, 0:width, 0:tiles * P].bitcast(F32),
                                    ALU.subtract).then_inc(h_cut.sem, 1)

                def hidden(u, n, at, width=512):
                    dve.wait_ge(split_free, at.plus(used(stage, n), 12, 84))
                    dve.wait_ge(silu_done.sem, at.plus(silu_done.after(stage, u), 1, per_item))
                    V.tensor_tensor(h_tok[:, 0:tiles, 0:width], silu_sb[:, 0:tiles, 0:width],
                                    ps[:, 6:6 + tiles, 0:width], ALU.mult).then_inc(h_ready.sem, 1)

                def unit(u, n, at):
                    if u:
                        low(u - 1, at)
                    for b in range(4):
                        ahead(stage, n + b, at)
                    hidden(u, n + 3, at)
                    if u == 1 and after_second:
                        after_second()
                    if u:
                        ahead(stage, n + 4, at)
                        ahead(stage, n + 5, at)

                unit(0, 0, at)
                if after_first:
                    after_first()
                unit(1, 4, at)
                with dve.Fori(0, units - 2) as i:
                    unit(2, 10, At(i, at.e))
                n = 10 + 6 * (units - 2)
                if odd:
                    low(units - 1, at)
                    ahead(stage, n, at)
                    ahead(stage, n + 1, at)
                    hidden(units, n + 1, at, 256)
                    ahead(stage, n + 2, at)
                    ahead(stage, n + 3, at)
                    low(units, at, 2)
                else:
                    low(units - 1, at)
                    if before_last:
                        before_last()
                    ahead(stage, n, at)
                    ahead(stage, n + 1, at)

            dve.wait_ge(consts_in, 32)
            b_ada = cols[:, COL_AT["b_ada"]:COL_AT["b_ada"] + 96].rearrange("p (l f) -> p l f", l=4)

            def save_modulation(hl):
                dve.wait_ge(ada_turned, hl + 1)
                n = 1 if hl else 2
                src = ps[:, 4 if hl else 6, 0:48].rearrange("p (f c) -> p f c", c=2)
                V.tensor_tensor(mod[:, hl, 0:16, 0:n], src[:, 0:16, 0:n],
                                b_ada[:, hl, 0:16].unsqueeze(2).broadcast_to([P, 16, n]), ALU.add)
                V.tensor_copy(mod[:, hl, 16:24, 0:1], src[:, 16:24, 0:1]).then_inc(ada_saved, 1)
                dve.wait_ge(ada_saved, 7 + hl)

            for nb in range(6):
                dve.wait_ge(ada_used, 2 * nb + 2)
                V.tensor_copy(ada_rows[0:2, nb * BANK:(nb + 1) * BANK], ps[0:2, nb, :]).then_inc(ada_saved, 1)
            save_modulation(0)
            for b in range(AHEAD):
                ahead("ret_in", b - AHEAD)
            save_fm("x0", 4)

            dve.wait_ge(aux["ret_consts"], 32)
            cos, sin = r_rope[:, 0, :], r_rope[:, 1, :]
            for b in range(8):
                ahead("ret_in", b)
                dve.wait_ge(proj_saved.sem, proj_saved.after("ret_in", b))
                if b:
                    dve.wait_ge(rope_done, b)
                ev, od = r_raw[:, b, 0, :], r_raw[:, b, 1, :]
                V.tensor_tensor(r_rot[:, b, 0, :], ev, cos, ALU.mult)
                V.tensor_tensor(r_rot[:, b, 1, :], ev, sin, ALU.mult)
                V.tensor_tensor(r_tmp[:, 0, :], od, sin, ALU.mult)
                link(V.tensor_tensor(r_tmp[:, 1, :], od, cos, ALU.mult))
                link(V.tensor_tensor(r_rot[:, b, 0, :], r_rot[:, b, 0, :], r_tmp[:, 0, :], ALU.subtract))
                V.tensor_tensor(r_rot[:, b, 1, :], r_rot[:, b, 1, :], r_tmp[:, 1, :], ALU.add
                                ).then_inc(rope_done, 1)
            for b in range(16):
                ahead("ret_in", 8 + b)
            dve.wait_ge(rope_done, 8)
            dve.wait_ge(proj_saved.sem, proj_saved.after("ret_in", 23))

            def group_norm(u):
                h, t = u // 2, u % 2
                bank = 1 + u % 4
                y = r_y[:, t, h * RDV:(h + 1) * RDV]
                dve.wait_ge(y_ready, u + 1)
                link(V.bn_stats(stat[:, 0:6], ps[:, bank, :]))
                link(V.bn_aggr(stat[:, 12:14], stat[:, 0:6]))
                V.tensor_scalar(stat[:, 32 + u % 2:33 + u % 2], stat[:, 13:14], LN_EPS, None, ALU.add
                                ).then_inc(y_var, 1)
                dve.wait_ge(y_root, u + 1)
                link(V.reciprocal(stat[:, 14:15], stat[:, 34 + u % 2:35 + u % 2]))
                V.tensor_scalar(y, ps[:, bank, :], stat[:, 12:13], stat[:, 14:15], ALU.subtract, ALU.mult
                                ).then_inc(y_read, 1)
                dve.wait_ge(y_read, u + 1)
                V.tensor_tensor(y, y, r_gate[:, t, h * RDV:(h + 1) * RDV], ALU.mult).then_inc(y_gated, 1)

            for h in range(RH):
                dve.wait_ge(st_ready, h + 1)
                V.tensor_tensor(r_st[:, h % 2, :], ps[:, 0, 0:384], r_decay[:, h, :], ALU.mult
                                ).then_inc(st_saved, 1)
                if h:
                    for t in range(TT):
                        group_norm(2 * (h - 1) + t)
            for t in range(TT):
                group_norm(2 * (RH - 1) + t)
            save_fm("ret0", 4, first_bank=4)
            for b in range(4):
                ahead("ret_out", b)
            save_fm("ret1", 4, first_bank=4)
            for b in range(4, 7):
                ahead("ret_out", b)
            layer_norm("ret_out", "x1", 0, used("ret_out", 7))
            ahead("ret_out", 7)
            save_fm("x1", 4)
            glu("ffn0", 5, True, TT)
            layer_norm("ffn0", "x2", 1, used("ffn0", 32))
            save_modulation(1)
            ahead("ffn0", 32)

            dve.wait_ge(rows_ready, 1)
            V.tensor_tensor(b_rows[0:AG * AH, :], ps[0:AG * AH, 7, 0:ROWS_W], b_mask[0:AG * AH, :], ALU.add
                            ).then_inc(rows_saved, 1)
            save_fm("x2", 4)
            with dve.Fori(0, 6) as i:
                for b in range(6):
                    ahead("att_in", b, At(i))

            def heads(stage, nh, hd, scores_of, pt_psum, pt_of, out_bank, dst):
                def row_max(h, it):
                    dve.wait_ge(scored.sem, scored.after(stage, 2 * h + it))
                    if h:
                        dve.wait_ge(probs.sem, probs.after(stage, 2 * (h - 1) + it))
                    link(V.reduce_max(stat[:, 44 + it:45 + it], scores_of(it), AX_X))
                    V.tensor_scalar(stat[:, 40 + it:41 + it], stat[:, 44 + it:45 + it], -1.0, None, ALU.mult
                                    ).then_inc(negmax.sem, 1)

                row_max(0, 0)
                row_max(0, 1)
                for h in range(nh):
                    for it in range(2):
                        u = 2 * h + it
                        dve.wait_ge(probs_t.sem, probs_t.after(stage, u))
                        if h:
                            dve.wait_ge(mixed.sem, mixed.after(stage, u - 2))
                        V.tensor_copy(pt_of(it), pt_psum(it)).then_inc(probs_fm.sem, 1)
                        if h + 1 < nh:
                            row_max(h + 1, it)
                    for it in range(2):
                        u = 2 * h + it
                        link(V.reciprocal(stat[:, 46 + it:47 + it], stat[:, 42 + it:43 + it]))
                        dve.wait_ge(mixed.sem, mixed.after(stage, u))
                        V.tensor_scalar(dst(h, it), ps[:, out_bank + it, 0:hd], stat[:, 46 + it:47 + it], None,
                                        ALU.mult).then_inc(head_saved.sem, 1)

            heads("att", AH, AHD, lambda it: psf[:, BANK * it:BANK * it + 384 * (it + 1)],
                  lambda it: psf[:, (3 + it) * BANK:(3 + it) * BANK + 384 * (it + 1)],
                  lambda it: a_pt[:, 384 * it:384 + 768 * it], 6,
                  lambda h, it: work[:, it, h * AHD:(h + 1) * AHD])
            save_fm("att", 4)
            for b in range(3):
                ahead("att_out", b)
            layer_norm("att_out", "x3", 2, used("att_out", 3))
            ahead("att_out", 3)
            save_fm("x3", 4)
            glu("ffn1", 5, True, TT)
            layer_norm("ffn1", "x4", 3, used("ffn1", 32))
            save_modulation(2)
            ahead("ffn1", 32)

            dve.wait_ge(aux["hyena_in"], 96)
            for m in range(2):
                dve.wait_ge(hy_pe, m + 1)
                arg, turns = y_arg[0:HID, 0, :], y_arg[0:HID, 1, :]
                if m:
                    dve.wait_ge(hy_act, 1)
                link(V.tensor_scalar(arg, ps[0:HID, m, 0:T], col("f_b1" if m == 0 else "f_b2", 0)[0:HID, :],
                                     col("f_freq", m)[0:HID, :], ALU.add, ALU.mult))
                link(V.tensor_scalar(turns, arg, 1.0 / (2.0 * np.pi), ROUND, ALU.mult, ALU.add))
                link(V.tensor_scalar(turns, turns, -ROUND, None, ALU.add))
                for part in (TWO_PI_HI, TWO_PI_MID, TWO_PI_LO):
                    link(V.scalar_tensor_tensor(arg, turns, -float(part), arg, ALU.mult, ALU.add))
                V.tensor_scalar(arg, arg, 3.1415925, -3.1415925, ALU.min, ALU.max).then_inc(hy_dve, 1)
            for n in range(4):
                for t in range(TT):
                    dve.wait_ge(hy_pe, 3 + 2 * n + t)
                    V.tensor_tensor(y_h[:, t, n, :], ps[:, (2 * n + t + 2) % 8, :], y_win[:, n % 2, t, :], ALU.mult
                                    ).then_inc(hy_dve, 1)
            for o in range(2):
                dve.wait_ge(hy_pe, 11 + o)
                link(V.tensor_scalar(y_rn[:, o, :], ps[:, 2 + o, :], RMS_EPS, None, ALU.add))
                V.reciprocal(y_rn[:, o, :], y_rn[:, o, :]).then_inc(hy_dve, 1)
            dve.wait_ge(hy_pe, 12)
            for o in range(2):
                V.tensor_tensor(y_abs[:, :, 2 * o, :], y_h[:, :, 2 * o, :], y_h[:, :, 2 * o + 1, :], ALU.add)
                V.tensor_tensor(y_abs[:, :, 2 * o + 1, :], y_h[:, :, 2 * o, :], y_h[:, :, 2 * o + 1, :],
                                ALU.subtract).then_inc(hy_dve, 1)
            for o in range(2):
                dve.wait_ge(hy_pe, 13 + o)
                for part in range(2):
                    for f in range(2):
                        ins = V.tensor_tensor(y_k[:, o, part, f, :], ps[:, 4 * (o % 2) + 2 * part + f, :],
                                              y_rn[:, o, :], ALU.mult)
                ins.then_inc(hy_dve, 1)

            link(V.memset(stat[:, 0:1], 0.0))
            V.memset(stat[:, 1:2], 0.0).then_inc(hy_dve, 1)
            modulate("m0", x_tok, 0, 0, x_hi, x_lo)
            modulate("mc", ctx_tok, 0, 1, h_hi, h_lo)
            for c in range(12):
                if c % 2 == 0:
                    ahead("w_in", c // 2)
                dve.wait_ge(proj_saved.sem, proj_saved.after("w_in", c // 2))
                wc = [col("short_w", 3 * c + j) for j in range(3)]
                link(V.tensor_scalar(z[:, c, :], z_raw[:, c, :], wc[1], col("short_b", c), ALU.mult, ALU.add))
                link(V.scalar_tensor_tensor(z[:, c, 1:T], z_raw[:, c, 0:T - 1], wc[0], z[:, c, 1:T],
                                            ALU.mult, ALU.add))
                V.scalar_tensor_tensor(z[:, c, 0:T - 1], z_raw[:, c, 1:T], wc[2], z[:, c, 0:T - 1],
                                       ALU.mult, ALU.add).then_inc(short_done, 1)
            for b in range(6, 12):
                ahead("w_in", b)
            dve.wait_ge(short_done, 12)
            w_flat = work[:, :, :].rearrange("p t n -> p (t n)")
            for o in range(2):
                dve.wait_ge(conv_f, o + 1)
                u_re, u_im = psf[:, 4 * BANK:6 * BANK], psf[:, 6 * BANK:8 * BANK]
                k_re = y_k[:, o, 0, :, :].rearrange("p f c -> p (f c)")
                k_im = y_k[:, o, 1, :, :].rearrange("p f c -> p (f c)")
                v_re = z_y[:, 0, :, :].rearrange("p f c -> p (f c)")
                v_im = z_y[:, 1, :, :].rearrange("p f c -> p (f c)")
                V.tensor_tensor(v_re, u_re, k_re, ALU.mult)
                V.tensor_tensor(w_flat[:, 0:D], u_im, k_im, ALU.mult)
                V.tensor_tensor(v_im, u_re, k_im, ALU.mult)
                link(V.tensor_tensor(w_flat[:, D:2 * D], u_im, k_re, ALU.mult))
                V.tensor_tensor(v_re, v_re, w_flat[:, 0:D], ALU.subtract)
                V.tensor_tensor(v_im, v_im, w_flat[:, D:2 * D], ALU.add).then_inc(conv_y, 1)
                for c in range(4):
                    if c % 2 == 0:
                        dve.wait_ge(conv_t, 2 * o + c // 2 + 1)
                    link(V.scalar_tensor_tensor(z[:, c, :], z[:, c, :], col("skip", 4 * o + c),
                                                ps[:, 2 + c // 2, (c % 2) * T:(c % 2 + 1) * T], ALU.mult, ALU.add))
                    V.tensor_tensor(z[:, c, :], z[:, c, :], z[:, 4 + 4 * o + c, :], ALU.mult).then_inc(conv_out, 1)
                dve.wait_ge(conv_out, 4 * o + 4)
            for c in range(4):
                dve.wait_ge(fm_hi.sem, fm_hi.after("hy", c))
                V.tensor_tensor(x_lo[:, c, :], z[:, c, :], x_hi[:, c, :].bitcast(F32), ALU.subtract
                                ).then_inc(fm_saved.sem, 1)
            heads("nat", NH, NHD, lambda it: ps[:, it, :], lambda it: ps[:, 2 + it, :], lambda it: n_pt[:, it, :], 4,
                  lambda h, it: work[:, it, h * NHD:(h + 1) * NHD])
            save_fm("nat", 2, first_bank=6, k0=4)
            for b in range(3):
                ahead("mix_out", b)
            residual("mix_out", "mix", used("mix_out", 3), 0)
            ahead("mix_out", 3)
            modulate("m1", x_tok, 1, 0, x_hi, x_lo)
            glu("ffn2", 5, True, TT)
            residual("ffn2", "ffn2", used("ffn2", 32), 1)
            save_modulation(3)
            ahead("ffn2", 32)
            modulate("m2", x_tok, 2, 0, None, None)
            for q in range(4):
                dve.wait_ge(four_hi, q + 1)
                c = slice(2 * q, 2 * q + 2)
                V.tensor_tensor(x_lo[:, c, :], ps[:, 2 + (PROJ_BASE["four_y"] + q) % 6, :]
                                .rearrange("p (k t) -> p k t", k=2), x_hi[:, c, :].bitcast(F32), ALU.subtract
                                ).then_inc(proj_saved.sem, 1)
            for b in range(3):
                ahead("fourier", b)
            residual("fourier", "fourier", used("fourier", 3), 2)
            ahead("fourier", 3)
            modulate("m3", x_tok, 3, 0, x_hi, x_lo)
            dve.wait_ge(router_cut, 1)
            V.tensor_tensor(router_lo[:, :, :], router_w[:, :, :], router_hi[:, :, :].bitcast(F32), ALU.subtract
                            ).then_inc(router_cut, 1)

            dve.wait_ge(routed, 1)
            for t in range(TT):
                link(V.tensor_tensor(route[:, t, 0, :], ps[:, 4 + t, 0:EXPERTS], router_b[:, :], ALU.add))
            link(V.memset(pairs[:, 1, :, :], 0.0))
            for e in range(1, EXPERTS):
                ins = V.memset(pairs[:, 1, e, 0:e], 1.0)
            link(ins)
            for t in range(TT):
                lf = route[:, t, 0, :].unsqueeze(1).broadcast_to([P, EXPERTS, EXPERTS])
                le = route[:, t, 0, :].unsqueeze(2).broadcast_to([P, EXPERTS, EXPERTS])
                link(V.tensor_tensor(pairs[:, 0, :, :], lf, le, ALU.is_equal))
                link(V.tensor_tensor(pairs[:, 0, :, :], pairs[:, 0, :, :], pairs[:, 1, :, :], ALU.mult))
                link(V.reduce_sum(route[:, t, 1, :], pairs[:, 0, :, :], AX_X))
                link(V.tensor_tensor(pairs[:, 0, :, :], lf, le, ALU.is_gt))
                link(V.reduce_sum(route[:, t, 2, :], pairs[:, 0, :, :], AX_X))
                link(V.tensor_tensor(route[:, t, 1, :], route[:, t, 1, :], route[:, t, 2, :], ALU.add))
                link(V.tensor_scalar(route[:, t, 2, :], route[:, t, 1, :], 0.0, None, ALU.is_equal))
                link(V.tensor_scalar(route[:, t, 3, :], route[:, t, 1, :], 1.0, None, ALU.is_equal))
                link(V.tensor_tensor(pairs[:, 0, 0, :], route[:, t, 2, :], route[:, t, 0, :], ALU.mult))
                link(V.reduce_sum(stat[:, 52:53], pairs[:, 0, 0, :], AX_X))
                link(V.tensor_tensor(pairs[:, 0, 0, :], route[:, t, 3, :], route[:, t, 0, :], ALU.mult))
                link(V.reduce_sum(stat[:, 53:54], pairs[:, 0, 0, :], AX_X))
                ins = V.tensor_tensor(stat[:, 48 + t:49 + t], stat[:, 53:54], stat[:, 52:53], ALU.subtract)
                if t == 0:
                    link(ins)
            ins.then_inc(route_var, 1)
            dve.wait_ge(route_exp, 1)
            link(V.tensor_scalar(stat[:, 54:56], stat[:, 50:52], 1.0, None, ALU.add))
            link(V.reciprocal(stat[:, 56:58], stat[:, 54:56]))
            link(V.tensor_tensor(stat[:, 58:60], stat[:, 50:52], stat[:, 56:58], ALU.mult))
            for t in range(TT):
                link(V.tensor_scalar(gates[:, t, :], route[:, t, 2, :], stat[:, 56 + t:57 + t], None, ALU.mult))
                ins = V.scalar_tensor_tensor(gates[:, t, :], route[:, t, 3, :], stat[:, 58 + t:59 + t], gates[:, t, :],
                                             ALU.mult, ALU.add)
                if t == 0:
                    link(ins)
            link(ins)
            for t in range(TT):
                ins = V.tensor_tensor(route[:, t, 1, :], route[:, t, 2, :], route[:, t, 3, :], ALU.add)
            ins.then_inc(ranked, 1)
            dve.wait_ge(routed, 2)
            counts = over[:, 0, :]
            link(V.tensor_scalar(counts, ps[:, 4, 16:24], float(P), None, ALU.is_gt))
            for t in range(TT):
                link(V.tensor_scalar(over[:, 2, :], ps[:, 4, 8 * t:8 * t + 8], 1.0, None, ALU.add))
                link(V.tensor_tensor(over[:, 2, :], over[:, 2, :], route[:, t, 1, :], ALU.mult))
                link(V.tensor_scalar(item_pos[:, t, 0:EXPERTS], over[:, 2, :], -1.0, None, ALU.add))
                link(V.tensor_copy(item_gate[:, t, 0:EXPERTS], gates[:, t, :]))
                V.memset(item_pos[:, t, ITEMS - 1:ITEMS], -1.0)
                link(V.memset(item_gate[:, t, ITEMS - 1:ITEMS], 0.0))
            of = counts.unsqueeze(1).broadcast_to([P, EXPERTS, EXPERTS])
            link(V.tensor_tensor(pairs[:, 0, :, :], of, pairs[:, 1, :, :], ALU.mult))
            link(V.reduce_sum(over[:, 1, :], pairs[:, 0, :, :], AX_X))
            link(V.tensor_copy(table_f[:, 0:EXPERTS], iota[:, 0:EXPERTS]))
            for r in range(ITEMS - 1 - EXPERTS):
                q = EXPERTS + r
                link(V.tensor_scalar(over[:, 3, :], over[:, 1, :], float(r), None, ALU.is_equal))
                link(V.tensor_tensor(over[:, 3, :], over[:, 3, :], counts, ALU.mult))
                link(V.tensor_tensor(over[:, 2, :], over[:, 3, :], iota[:, 0:EXPERTS], ALU.mult))
                link(V.reduce_sum(table_f[:, q:q + 1], over[:, 2, :], AX_X))
                for t in range(TT):
                    link(V.tensor_scalar(over[:, 2, :], item_pos[:, t, 0:EXPERTS], -float(P), None, ALU.add))
                    link(V.tensor_tensor(over[:, 2, :], over[:, 2, :], over[:, 3, :], ALU.mult))
                    link(V.reduce_sum(item_pos[:, t, q:q + 1], over[:, 2, :], AX_X))
                    link(V.tensor_tensor(over[:, 2, :], gates[:, t, :], over[:, 3, :], ALU.mult))
                    link(V.reduce_sum(item_gate[:, t, q:q + 1], over[:, 2, :], AX_X))
            link(V.reduce_sum(table_f[:, ITEMS - 1:ITEMS], counts, AX_X))
            link(V.tensor_scalar(table_f[:, ITEMS - 1:ITEMS], table_f[:, ITEMS - 1:ITEMS], float(EXPERTS), None,
                                 ALU.add))
            V.tensor_copy(table[:, :], table_f[:, :]).then_inc(table_ready, 1)
            dve.wait_ge(table_ready, 1)
            link(V.memset(m_acc, 0.0))
            link(V.memset(m_yc, 0.0))
            V.memset(m_selt, 0.0).then_inc(yc_ready, 1)
            count = dve.value_load(table[0:1, ITEMS - 1:ITEMS], min_val=EXPERTS, max_val=ITEMS - 1)
            pos_flat = item_pos[:, :, :].rearrange("p t e -> p (t e)")
            gate_flat = item_gate[:, :, :].rearrange("p t e -> p (t e)")

            def select(at_item):
                for t in range(TT):
                    ins = V.tensor_scalar(m_sel[:, t, :], iota, pos_flat[:, bass.ds(at_item + t * ITEMS, 1)], None,
                                          ALU.is_equal)
                ins.then_inc(sel_ready, 1)

            def select_weighted(at_item):
                for t in range(TT):
                    ins = V.tensor_scalar(m_selg[:, t, :], iota, pos_flat[:, bass.ds(at_item + t * ITEMS, 1)],
                                          gate_flat[:, bass.ds(at_item + t * ITEMS, 1)], ALU.is_equal, ALU.mult)
                ins.then_inc(selg_ready, 1)

            def item_input(nth):
                dve.wait_ge(gathered, nth)
                a_bc = mod_a[:, :, 1:2].broadcast_to([P, KD, P])
                b_bc = mod[:, 3, 0:8, 0:1].broadcast_to([P, KD, P])
                V.tensor_tensor(m_x, psf[:, 2 * BANK:4 * BANK].rearrange("p (k s) -> p k s", k=KD), a_bc, ALU.mult
                                ).then_inc(m_x_scaled, 1)
                dve.wait_ge(m_x_scaled, nth)
                V.tensor_tensor(m_x, m_x, b_bc, ALU.add).then_inc(m_x_ready, 1)

            def item_low(nth):
                dve.wait_ge(m_x_high, nth)
                dve.wait_ge(m_x_ready, nth)
                V.tensor_tensor(x_lo[:, :, 0:P], m_x, x_hi[:, :, 0:P].bitcast(F32), ALU.subtract
                                ).then_inc(m_x_cut, 1)

            def add_shares(nth):
                for t in range(TT):
                    dve.wait_ge(scattered, nth * 2 + (t + 1))
                    dve.wait_ge(shares_added, nth * 2 + 1)
                    for half in range(2):
                        c = slice(half * BANK, half * BANK + BANK)
                        ins = V.tensor_tensor(m_acc[:, t, c], m_acc[:, t, c], ps[:, (2, 3, 5, 7)[2 * t + half], :],
                                              ALU.add)
                    ins.then_inc(shares_added, 1)

            select(0)
            item_input(1)
            item_low(1)
            with dve.Fori(0, count) as e:
                def selections():
                    dve.wait_ge(m_x_cut, e + 1)
                    select_weighted(e)
                    select(e + 1)

                def finish():
                    item_low(e + 2)
                    add_shares(e)

                glu("moe", 7, False, 1, At(None, e), per_item=7, after_first=selections,
                    after_second=lambda: item_input(e + 2), before_last=finish)
            add_shares(count)
            link(V.memset(stat[:, 0:1], 0.0))
            dve.wait_ge(ln_in, 32 * 8)
            link(V.tensor_tensor(ln_gb[:, 0, :], ln_gb[:, 0, :], ln_gb[:, 1, :], ALU.add))
            for t in range(TT):
                link(V.tensor_tensor(m_acc[:, t, :], m_acc[:, t, :], ln_gb[:, 0, :], ALU.mult))
                V.tensor_tensor(x_tok[:, t, :], x_tok[:, t, :], m_acc[:, t, :], ALU.add).then_inc(x_summed.sem, 1)
            dve.wait_ge(x_summed.sem, x_summed.after("moe", 1))
            dve.wait_ge(ln_in, 32 * 8 + 16)
            rms_scale("fin", x_tok, work)


PROJ_BASE = {"ret_in": 0, "att_in": 24, "w_in": 60, "four_a": 76, "four_y": 84}


def constants():
    f32 = np.float32
    k = {}
    k["squares"] = np.stack([np.eye(P), np.eye(P)[::-1], np.ones((P, P)),
                           np.triu(np.ones((P, P)), 1), np.tile(np.arange(P), (P, 1))], 1).astype(f32)
    inv = f32(1.0) / np.power(f32(10000.0), np.linspace(0.0, 1.0, RDK // 2, dtype=f32))
    ang = (np.arange(T, dtype=f32)[:, None] * inv[None, :]).astype(f32).astype(np.float64)
    k["rope"] = np.stack([np.cos(ang).T, np.sin(ang).T], 1).astype(f32)
    lg = np.log(1.0 - 2.0 ** (-5.0 - np.arange(RH)))
    j, i = np.arange(T)[:, None], np.arange(T)[None, :]
    dec = np.where(i >= j, np.exp(np.maximum(i - j, 0)[None] * lg[:, None, None]), 0.0) * RDK ** -0.5
    k["decay"] = np.concatenate([dec[:, 0:P, :], dec[:, P:T, P:T]], 2).transpose(1, 0, 2).astype(f32)
    dist = 255 - np.arange(ROWS_W)
    exact = BUCKETS // 2
    big = exact + (np.log(np.maximum(dist, 1).astype(f32) / f32(exact)) / f32(np.log(MAX_DIST / exact))
                   * f32(BUCKETS - exact)).astype(np.int32)
    bucket = np.where(dist < exact, dist, np.minimum(big, BUCKETS - 1))
    k["bucket_hot"] = ((bucket[None, :] == np.arange(BUCKETS)[:, None]) & (dist >= 0)[None, :]).astype(f32)
    rows = [np.where((dist >= 0) & (dist % dil == 0) & (dist <= win), 0.0, NEG) for win, dil in DILATIONS]
    k["rel_mask"] = np.repeat(np.stack(rows), AH, 0).astype(f32)
    t = np.linspace(0.0, 1.0, T, dtype=f32)[:, None]
    bands = np.linspace(1e-4, (EMB - 1) // 2 - 1, (EMB - 1) // 2, dtype=f32)
    ang = (f32(2.0 * np.pi / T) * np.arange(T, dtype=f32)[:, None] * bands[None, :]).astype(f32)
    k["features"] = np.concatenate([t, np.cos(ang), -np.sin(ang)], 1).T.astype(f32)
    deltas = np.abs(np.linspace(np.log(1e-2) / 1.5, np.log(1e-2) / 0.3, HC, dtype=f32))
    win = np.exp(-t * deltas[None, :]).astype(f32)
    later = win.copy()
    later[0] = 0.0
    k["window"] = np.stack([win, later]).reshape(2, TT, P, HC).transpose(2, 0, 1, 3)
    w = 2.0 * np.pi * (np.arange(T) + 0.5)[None, :] * np.arange(T)[:, None] / (2 * T)
    dft = [np.cos(w), np.sin(w), np.cos(w).T / T, np.sin(w).T / T]
    k["dft"] = np.stack(dft).reshape(4, TT, P, T).transpose(2, 0, 1, 3).astype(f32)
    c = 63 - np.arange(P) % 64
    start = np.clip(c - WIN_C // 2, 0, GRID_W - WIN_C)[:, None]
    cc = np.arange(GRID_W)[None, :]
    mask = np.where((cc >= start) & (cc < start + WIN_C), 0.0, NEG)
    k["window_mask"] = np.tile(mask, (1, 6)).astype(f32)
    w = 2.0 * np.pi * ((np.arange(T)[:, None] * np.arange(T)[None, :]) % T) / T
    cs = np.concatenate([np.cos(w), np.sin(w)], 1).reshape(2, P, 512)
    cl = np.concatenate([np.cos(w), -np.sin(w)], 1).reshape(2, P, 512)
    k["fourier"] = (np.concatenate([cs, cl], 0).transpose(1, 0, 2) / 16.0).astype(f32)
    return {n: np.ascontiguousarray(v, dtype=f32) for n, v in k.items()}


def by_partition(v, parts=P):
    v = v.reshape(-1, parts)
    return v.T


def kernel(**inputs):
    import numpy as _np
    import concourse.bacc as _bacc
    from concourse import mybir as _mybir
    from concourse.bass_utils import run_bass_kernel_spmd as _run

    x = {n: _np.asarray(v) for n, v in inputs.items()}

    def padded(v):
        o = _np.zeros((P, v.shape[1]), v.dtype)
        o[0:v.shape[0]] = v
        return o

    c2 = _np.stack([x["c_2"].reshape(-1), x["c_ctx_2"].reshape(-1)])
    parts = {
        "c": c2.reshape(2, KD, P).transpose(2, 1, 0).reshape(P, 16),
        "b_ada": by_partition(x["b_ada_2"]),
        "norm_g": by_partition(x["norm_g_2"]),
        "short_w": x["hy_short_w_2"][0].reshape(3, 12, P).transpose(2, 1, 0).reshape(P, 36),
        "short_b": by_partition(x["hy_short_b_2"]),
        "skip": by_partition(x["hy_skip_2"]),
        "f_b1": padded(x["hy_f_b1_2"].reshape(HID, 1)),
        "f_b2": padded(x["hy_f_b2_2"].reshape(HID, 1)),
        "f_freq": padded(x["hy_f_freq_2"][0].T),
    }
    arrays = dict(constants())
    arrays["cols"] = _np.concatenate([parts[n] for n, _ in COLS], 1)
    arrays["rel_bias"] = _np.ascontiguousarray(x["rel_bias"].T)
    arrays["x"] = x["x"][0]
    arrays["ctx_2"] = x["ctx_2"][0]
    for n in ("ret_w_in", "ret_w_out", "attn_w_in", "attn_w_out", "w_in_2", "w_mix_out_2", "ffn_w1_2", "ffn_w3_2",
              "ffn_w2_2", "w_fourier_2", "w_router_2", "b_router_2", "moe_w1_2", "moe_w3_2", "moe_w2_2",
              "hy_f_w1_2", "hy_f_w2_2", "hy_f_w3_2", "na_rpb_2"):
        arrays[n] = x[n][0]
    for n in ("ffn_w_up", "ffn_w_down", "ln_gain", "ln_bias", "w_ada_2", "b_ada_2", "final_g_2"):
        arrays[n] = x[n]
    arrays = {n: _np.ascontiguousarray(v) for n, v in arrays.items()}

    nc = _bacc.Bacc("TRN2", target_bir_lowering=False, num_devices=1)
    ins = {n: nc.dram_tensor(f"in_{n}", v.shape, _mybir.dt.float32, kind="ExternalInput").ap()
           for n, v in arrays.items()}
    out = nc.dram_tensor("out", (T, D), _mybir.dt.float32, kind="ExternalOutput").ap()
    build(nc, ins, out)
    r = _run(nc, [{f"in_{n}": v for n, v in arrays.items()}], core_ids=[0])
    return r.results[0]["out"].reshape(1, T, D)
```
